# Optimizing a Trainium2 kernel written in Bass

```python
import jax, jax.numpy as jnp
from jax import lax
import numpy as np
import math
import jax
import jax.numpy as jnp

D_MODEL = 1024
BATCH = 1
SEQ = 256
DEPTH = 1

HEAD_DIM = 64
N_MOBA_HEADS = 6
N_DIL_HEADS = 6
N_MEM_HEADS = 4
N_MEM = 256
MOBA_BLOCK = 256
MOBA_TOPK = 3
MOBA_QCHUNK = 128
DIL_PATTERNS = ((128, 1), (512, 4), (2048, 16))
DIL_BLOCK = 128
D_FF = 2816
CONV_WIDTH = 3
ROPE_THETA = 10000.0
EPS = 1e-6
N_BRANCHES = 3
MOBA_W = N_MOBA_HEADS * HEAD_DIM
DIL_W = N_DIL_HEADS * HEAD_DIM
MEM_W = N_MEM_HEADS * HEAD_DIM
IN_COLS = 3 * MOBA_W + 3 * DIL_W + MEM_W + N_BRANCHES * D_MODEL


def rmsnorm(x, g):
    x32 = x.astype(jnp.float32)
    y = x32 * lax.rsqrt(jnp.mean(x32 * x32, axis=-1, keepdims=True) + EPS)
    return (y * g.astype(jnp.float32)).astype(x.dtype)

def rope(x, positions):
    half = HEAD_DIM // 2
    inv_freq = ROPE_THETA ** (-jnp.arange(half, dtype=jnp.float32) / half)
    ang = positions.astype(jnp.float32)[..., None] * inv_freq
    cos = jnp.cos(ang)[:, :, None, :]
    sin = jnp.sin(ang)[:, :, None, :]
    x1 = x[..., :half].astype(jnp.float32)
    x2 = x[..., half:].astype(jnp.float32)
    out = jnp.concatenate([x1 * cos - x2 * sin, x1 * sin + x2 * cos], axis=-1)
    return out.astype(x.dtype)

def moba_attention(q, k, v):
    B, S, H, Dh = q.shape
    s_pad = -(-S // MOBA_BLOCK) * MOBA_BLOCK
    pad = s_pad - S
    q, k, v = [jnp.pad(t, ((0, 0), (0, pad), (0, 0), (0, 0))).transpose(0, 2, 1, 3) for t in (q, k, v)]
    nb = s_pad // MOBA_BLOCK
    topk = min(MOBA_TOPK, nb)
    kb = k.reshape(B, H, nb, MOBA_BLOCK, Dh)
    vb = v.reshape(B, H, nb, MOBA_BLOCK, Dh)
    k_mean = jnp.mean(kb.astype(jnp.float32), axis=3)
    scale = Dh ** -0.5
    bi = jnp.arange(B)[:, None, None, None]
    hi = jnp.arange(H)[None, :, None, None]
    blk_ids = jnp.arange(nb)

    def one_chunk(c):
        q0 = c * MOBA_QCHUNK
        qc = lax.dynamic_slice_in_dim(q, q0, MOBA_QCHUNK, axis=2)
        qpos = q0 + jnp.arange(MOBA_QCHUNK)
        own = q0 // MOBA_BLOCK
        gate = jnp.einsum('bhqd,bhnd->bhqn', qc.astype(jnp.float32), k_mean)
        gate = jnp.where(blk_ids < own, gate, -jnp.inf)
        gval, sel = lax.top_k(gate, topk)
        sel_ok = jnp.isfinite(gval)
        k_sel = kb[bi, hi, sel]
        v_sel = vb[bi, hi, sel]
        s_sel = jnp.einsum('bhqd,bhqnjd->bhqnj', qc, k_sel).astype(jnp.float32) * scale
        s_sel = jnp.where(sel_ok[..., None], s_sel, -jnp.inf)
        s_sel = s_sel.reshape(B, H, MOBA_QCHUNK, topk * MOBA_BLOCK)
        k_own = lax.dynamic_slice_in_dim(k, own * MOBA_BLOCK, MOBA_BLOCK, axis=2)
        v_own = lax.dynamic_slice_in_dim(v, own * MOBA_BLOCK, MOBA_BLOCK, axis=2)
        kpos = own * MOBA_BLOCK + jnp.arange(MOBA_BLOCK)
        s_own = jnp.einsum('bhqd,bhjd->bhqj', qc, k_own).astype(jnp.float32) * scale
        s_own = jnp.where(kpos[None, :] <= qpos[:, None], s_own, -jnp.inf)
        p = jax.nn.softmax(jnp.concatenate([s_sel, s_own], axis=-1), axis=-1)
        p_sel = p[..., :topk * MOBA_BLOCK].reshape(B, H, MOBA_QCHUNK, topk, MOBA_BLOCK)
        p_own = p[..., topk * MOBA_BLOCK:]
        o = (jnp.einsum('bhqnj,bhqnjd->bhqd', p_sel.astype(v.dtype), v_sel)
             + jnp.einsum('bhqj,bhjd->bhqd', p_own.astype(v.dtype), v_own))
        return o

    outs = lax.map(one_chunk, jnp.arange(s_pad // MOBA_QCHUNK))
    o = outs.transpose(1, 0, 3, 2, 4).reshape(B, s_pad, H, Dh)
    return o[:, :S]

def dilated_attention(q, k, v):
    B, S, H, Dh = q.shape
    max_dil = max(d for _, d in DIL_PATTERNS)
    unit = max_dil * DIL_BLOCK
    s_pad = -(-S // unit) * unit
    pad = s_pad - S
    q, k, v = [jnp.pad(t, ((0, 0), (0, pad), (0, 0), (0, 0))) for t in (q, k, v)]
    scale = Dh ** -0.5
    outs, lses = [], []
    for window, dil in DIL_PATTERNS:
        span = window // dil
        L = s_pad // dil
        nblk = L // DIL_BLOCK

        def to_sub(t):
            return t.reshape(B, L, dil, H, Dh).transpose(0, 2, 1, 3, 4).reshape(B, dil, nblk, DIL_BLOCK, H, Dh)

        def from_sub(t):
            rest = t.shape[4:]
            t = t.reshape((B, dil, L) + rest)
            t = jnp.moveaxis(t, 1, 2)
            return t.reshape((B, s_pad) + rest)

        def with_prev(t):
            prev = jnp.pad(t[:, :, :-1], ((0, 0), (0, 0), (1, 0), (0, 0), (0, 0), (0, 0)))
            return jnp.concatenate([prev, t], axis=3)

        qs = to_sub(q)
        ks = with_prev(to_sub(k))
        vs = with_prev(to_sub(v))
        s = jnp.einsum('brnqhd,brnkhd->brnhqk', qs, ks).astype(jnp.float32) * scale
        qi = jnp.arange(DIL_BLOCK)[:, None] + DIL_BLOCK
        kj = jnp.arange(2 * DIL_BLOCK)[None, :]
        dist = qi - kj
        band = (dist >= 0) & (dist <= span)
        not_before_start = (jnp.arange(nblk) > 0)[:, None, None] | (kj >= DIL_BLOCK)[None]
        mask = band[None] & not_before_start
        s = jnp.where(mask[None, None, :, None], s, -jnp.inf)
        m = jnp.max(s, axis=-1, keepdims=True)
        p = jnp.exp(s - m)
        den = jnp.sum(p, axis=-1)
        o = jnp.einsum('brnhqk,brnkhd->brnqhd', p.astype(v.dtype), vs)
        o = o / den.transpose(0, 1, 2, 4, 3)[..., None]
        lse = (m[..., 0] + jnp.log(den)).transpose(0, 1, 2, 4, 3)
        outs.append(from_sub(o))
        lses.append(from_sub(lse))
    w = jax.nn.softmax(jnp.stack(lses, axis=0), axis=0)
    o = jnp.einsum('pbsh,pbshd->bshd', w, jnp.stack(outs, axis=0).astype(jnp.float32))
    return o[:, :S].astype(q.dtype)

def memory_attention(q, mem_k, mem_v):
    s = jnp.einsum('bshd,bmhd->bhsm', q, mem_k).astype(jnp.float32) * (HEAD_DIM ** -0.5)
    p = jax.nn.softmax(s, axis=-1)
    return jnp.einsum('bhsm,bmhd->bshd', p.astype(mem_v.dtype), mem_v)

def causal_depthwise_conv(u, w, b):
    S = u.shape[1]
    u_pad = jnp.pad(u, ((0, 0), (CONV_WIDTH - 1, 0), (0, 0)))
    y = b
    for j in range(CONV_WIDTH):
        y = y + w[j] * u_pad[:, j:j + S]
    return y

def first_inputs(seed: int = 0) -> dict:
    key = jax.random.key(seed)
    ks = jax.random.split(key, 24)
    f32 = jnp.float32

    def nrm(k, shape, scale):
        return jax.random.normal(k, shape, f32) * scale

    def gain(k, shape):
        return 1.0 + 0.02 * jax.random.normal(k, shape, f32)

    return {
        "x": nrm(ks[0], (BATCH, SEQ, D_MODEL), 1.0),
        "mem": nrm(ks[1], (BATCH, N_MEM, D_MODEL), 1.0),
        "positions": jnp.broadcast_to(jnp.arange(SEQ, dtype=jnp.int32)[None], (BATCH, SEQ)),
        "mix_norm_g": gain(ks[2], (DEPTH, D_MODEL)),
        "mem_norm_g": gain(ks[3], (DEPTH, D_MODEL)),
        "w_in": nrm(ks[4], (DEPTH, D_MODEL, IN_COLS), D_MODEL ** -0.5),
        "moba_q_norm_g": gain(ks[5], (DEPTH, HEAD_DIM)),
        "moba_k_norm_g": gain(ks[6], (DEPTH, HEAD_DIM)),
        "dil_q_norm_g": gain(ks[7], (DEPTH, HEAD_DIM)),
        "dil_k_norm_g": gain(ks[8], (DEPTH, HEAD_DIM)),
        "mem_q_norm_g": gain(ks[9], (DEPTH, HEAD_DIM)),
        "mem_k_norm_g": gain(ks[10], (DEPTH, HEAD_DIM)),
        "w_mem_kv": nrm(ks[11], (DEPTH, D_MODEL, 2 * MEM_W), D_MODEL ** -0.5),
        "w_branch_moba": nrm(ks[12], (DEPTH, MOBA_W, D_MODEL), MOBA_W ** -0.5),
        "w_branch_dil": nrm(ks[13], (DEPTH, DIL_W, D_MODEL), DIL_W ** -0.5),
        "w_branch_mem": nrm(ks[14], (DEPTH, MEM_W, D_MODEL), MEM_W ** -0.5),
        "w_out": nrm(ks[15], (DEPTH, D_MODEL, D_MODEL), D_MODEL ** -0.5),
        "ffn_norm_g": gain(ks[16], (DEPTH, D_MODEL)),
        "w_ffn_up": nrm(ks[17], (DEPTH, D_MODEL, 2 * D_FF), D_MODEL ** -0.5),
        "ffn_conv_w": nrm(ks[18], (DEPTH, CONV_WIDTH, 2 * D_FF), CONV_WIDTH ** -0.5),
        "ffn_conv_b": nrm(ks[19], (DEPTH, 2 * D_FF), 0.01),
        "w_ffn_down": nrm(ks[20], (DEPTH, D_FF, D_MODEL), D_FF ** -0.5),
    }

def first_block(x, mem, positions, mix_norm_g, mem_norm_g, w_in, moba_q_norm_g, moba_k_norm_g,
              dil_q_norm_g, dil_k_norm_g, mem_q_norm_g, mem_k_norm_g, w_mem_kv,
              w_branch_moba, w_branch_dil, w_branch_mem, w_out, ffn_norm_g,
              w_ffn_up, ffn_conv_w, ffn_conv_b, w_ffn_down):
    B, S, _ = x.shape
    split_at = [int(c) for c in np.cumsum([MOBA_W, MOBA_W, MOBA_W, DIL_W, DIL_W, DIL_W, MEM_W])]
    for l in range(DEPTH):
        h = rmsnorm(x, mix_norm_g[l])
        proj = h @ w_in[l]
        qa, ka, va, qd, kd, vd, qm, graw = jnp.split(proj, split_at, axis=-1)
        heads = lambda t, n: t.reshape(B, S, n, HEAD_DIM)
        qa = rope(rmsnorm(heads(qa, N_MOBA_HEADS), moba_q_norm_g[l]), positions)
        ka = rope(rmsnorm(heads(ka, N_MOBA_HEADS), moba_k_norm_g[l]), positions)
        va = heads(va, N_MOBA_HEADS)
        qd = rope(rmsnorm(heads(qd, N_DIL_HEADS), dil_q_norm_g[l]), positions)
        kd = rope(rmsnorm(heads(kd, N_DIL_HEADS), dil_k_norm_g[l]), positions)
        vd = heads(vd, N_DIL_HEADS)
        qm = rmsnorm(heads(qm, N_MEM_HEADS), mem_q_norm_g[l])
        gates = jax.nn.sigmoid(graw.astype(jnp.float32)).astype(x.dtype).reshape(B, S, N_BRANCHES, D_MODEL)

        mem_n = rmsnorm(mem, mem_norm_g[l])
        mkv = (mem_n @ w_mem_kv[l]).reshape(B, N_MEM, 2, N_MEM_HEADS, HEAD_DIM)
        mk = rmsnorm(mkv[:, :, 0], mem_k_norm_g[l])
        mv = mkv[:, :, 1]

        o_a = moba_attention(qa, ka, va).reshape(B, S, MOBA_W) @ w_branch_moba[l]
        o_d = dilated_attention(qd, kd, vd).reshape(B, S, DIL_W) @ w_branch_dil[l]
        o_m = memory_attention(qm, mk, mv).reshape(B, S, MEM_W) @ w_branch_mem[l]
        merged = gates[:, :, 0] * o_a + gates[:, :, 1] * o_d + gates[:, :, 2] * o_m
        x = x + merged @ w_out[l]

        h2 = rmsnorm(x, ffn_norm_g[l])
        u = causal_depthwise_conv(h2 @ w_ffn_up[l], ffn_conv_w[l], ffn_conv_b[l])
        u_gate, u_val = jnp.split(u, 2, axis=-1)
        x = x + (jax.nn.silu(u_gate) * u_val) @ w_ffn_down[l]
    return x


DEPTH_2 = 2

CHUNK = 64
Q_BLOCK = 128
LN_EPS = 1e-5
DEEPNORM_ALPHA = (2 * DEPTH_2) ** 0.25
DEEPNORM_BETA = (8 * DEPTH_2) ** -0.25

FFN_RES = 0.5

H_A = 8
HD_A = 64
ROT_A = HD_A // 4
ROPE_THETA_2 = 500000.0
A_W = H_A * 2 * HD_A

H_B = 16
P_B = 64
D_INNER = H_B * P_B
G_B = 2
N_B = 128
CONV_B = 4
CONV_DIM = D_INNER + 2 * G_B * N_B

H_C = 16
HD_C = 64
C_W = H_C * HD_C

N_BRANCH = 3
BR_W = 1024

_SEGMENTS = (A_W, A_W, A_W, D_INNER, CONV_DIM, H_B, C_W, C_W, C_W, N_BRANCH * D_MODEL)
SPLIT_POINTS = tuple(int(v) for v in np.cumsum(_SEGMENTS)[:-1])
N_IN = int(sum(_SEGMENTS))


def _layernorm(x, g, b):
    xf = x.astype(jnp.float32)
    mu = jnp.mean(xf, -1, keepdims=True)
    xc = xf - mu
    var = jnp.mean(xc * xc, -1, keepdims=True)
    y = xc * lax.rsqrt(var + LN_EPS) * g.astype(jnp.float32) + b.astype(jnp.float32)
    return y.astype(x.dtype)

def _rmsnorm(x, g):
    xf = x.astype(jnp.float32)
    y = xf * lax.rsqrt(jnp.mean(xf * xf, -1, keepdims=True) + LN_EPS)
    return (y * g.astype(jnp.float32)).astype(x.dtype)

def _swiglu(x, w_in, w_out):
    gate, up = jnp.split(x @ w_in, 2, axis=-1)
    return (jax.nn.silu(gate) * up) @ w_out

def _rotary_tables(s):
    half = ROT_A // 2
    inv_freq = ROPE_THETA_2 ** (-jnp.arange(half, dtype=jnp.float32) * 2.0 / ROT_A)
    ang = jnp.arange(s, dtype=jnp.float32)[:, None] * inv_freq[None, :]
    return jnp.cos(ang), jnp.sin(ang)

def _apply_partial_rope(x, cos, sin):
    half = ROT_A // 2
    c = cos.reshape(cos.shape[0], 1, 1, half).astype(x.dtype)
    sn = sin.reshape(sin.shape[0], 1, 1, half).astype(x.dtype)
    x1 = x[..., :half]
    x2 = x[..., half:ROT_A]
    return jnp.concatenate([x1 * c - x2 * sn, x2 * c + x1 * sn, x[..., ROT_A:]], axis=-1)

def _diff_attention(qa, ka, va, lam, subln_g, layer):
    b, s, _ = qa.shape
    nb = s // Q_BLOCK
    cos, sin = _rotary_tables(s)
    q = _apply_partial_rope(qa.reshape(b, s, H_A, 2, HD_A), cos, sin)
    k = _apply_partial_rope(ka.reshape(b, s, H_A, 2, HD_A), cos, sin)
    v = va.reshape(b, s, H_A, 2 * HD_A)
    lam_init = 0.8 - 0.6 * math.exp(-0.3 * layer)
    lf = lam.astype(jnp.float32)
    lam_full = jnp.exp(jnp.sum(lf[0] * lf[1])) - jnp.exp(jnp.sum(lf[2] * lf[3])) + lam_init
    kpos = jnp.arange(s)
    kchunk = kpos // CHUNK
    qpos = kpos.reshape(nb, Q_BLOCK)
    qb = jnp.moveaxis(q.reshape(b, nb, Q_BLOCK, H_A, 2, HD_A), 1, 0)
    scale = HD_A ** -0.5

    def block(args):
        qblk, qp = args
        sc = jnp.einsum('bqhmd,bkhmd->bhmqk', qblk, k).astype(jnp.float32) * scale
        allowed = kchunk[None, :] <= (qp // CHUNK)[:, None]
        p = jax.nn.softmax(jnp.where(allowed, sc, -jnp.inf), axis=-1)
        w = p[:, :, 0] - lam_full * p[:, :, 1]
        return jnp.einsum('bhqk,bkhe->bqhe', w.astype(v.dtype), v)

    out = lax.map(block, (qb, qpos))
    out = jnp.moveaxis(out, 0, 1).reshape(b, s, H_A, 2 * HD_A)
    out = _rmsnorm(out, subln_g) * (1.0 - lam_init)
    return out.reshape(b, s, A_W)

def _stick_breaking(qc, kc, vc):
    b, s, _ = qc.shape
    nb = s // Q_BLOCK
    k = kc.reshape(b, s, H_C, HD_C)
    v = vc.reshape(b, s, H_C, HD_C)
    qb = jnp.moveaxis(qc.reshape(b, nb, Q_BLOCK, H_C, HD_C), 1, 0)
    kpos = jnp.arange(s)
    qpos = kpos.reshape(nb, Q_BLOCK)
    scale = HD_C ** -0.5

    def block(args):
        qblk, qp = args
        z = jnp.einsum('bqhd,bkhd->bhqk', qblk, k).astype(jnp.float32) * scale
        strict = kpos[None, :] < qp[:, None]
        log_stay = jnp.where(strict, jax.nn.log_sigmoid(-z), 0.0)
        after = lax.cumsum(log_stay, axis=3, reverse=True) - log_stay
        a = jnp.where(strict, jnp.exp(jax.nn.log_sigmoid(z) + after), 0.0)
        return jnp.einsum('bhqk,bkhd->bqhd', a.astype(v.dtype), v)

    out = lax.map(block, (qb, qpos))
    return jnp.moveaxis(out, 0, 1).reshape(b, s, C_W)

def _ssd(x, dt, a_neg, bm, cm):
    b, s = x.shape[:2]
    nc = s // CHUNK
    hg = H_B // G_B
    xr = x.reshape(b, nc, CHUNK, G_B, hg, P_B)
    dtr = dt.reshape(b, nc, CHUNK, G_B, hg)
    br = bm.reshape(b, nc, CHUNK, G_B, N_B)
    cr = cm.reshape(b, nc, CHUNK, G_B, N_B)
    acum = jnp.cumsum(dtr * a_neg.reshape(G_B, hg), axis=2)
    xdt = xr * dtr[..., None]
    causal = jnp.tril(jnp.ones((CHUNK, CHUNK), dtype=bool))[None, None, :, :, None, None]
    seg = acum[:, :, :, None] - acum[:, :, None, :]
    decay = jnp.exp(jnp.where(causal, seg, -jnp.inf))
    cb = jnp.einsum('bctgn,bcsgn->bctsg', cr, br)
    y_diag = jnp.einsum('bctsgh,bcsghp->bctghp', cb[..., None] * decay, xdt)
    decay_to_end = jnp.exp(acum[:, :, -1:] - acum)
    states = jnp.einsum('bclgn,bclghp->bcghpn', br, xdt * decay_to_end[..., None])
    chunk_decay = jnp.exp(acum[:, :, -1])

    def step(h_prev, inp):
        st, dc = inp
        return h_prev * dc[..., None, None] + st, h_prev

    h0 = jnp.zeros((b, G_B, hg, P_B, N_B), jnp.float32)
    _, h_in = lax.scan(step, h0, (jnp.moveaxis(states, 1, 0), jnp.moveaxis(chunk_decay, 1, 0)))
    h_in = jnp.moveaxis(h_in, 0, 1)
    y_off = jnp.einsum('bclgn,bcghpn->bclghp', cr, h_in) * jnp.exp(acum)[..., None]
    return (y_diag + y_off).reshape(b, s, H_B, P_B)

def _mamba2(zb, xbc, dtb, conv_w, conv_b, dt_bias, a_log, d_skip, norm_g):
    b, s, _ = zb.shape
    xbc = lax.conv_general_dilated(
        xbc, conv_w[:, None, :], window_strides=(1,), padding=[(CONV_B - 1, 0)],
        dimension_numbers=('NWC', 'WIO', 'NWC'), feature_group_count=CONV_DIM) + conv_b
    xbc = jax.nn.silu(xbc).astype(jnp.float32)
    xs, bm, cm = jnp.split(xbc, [D_INNER, D_INNER + G_B * N_B], axis=-1)
    dt = jax.nn.softplus(dtb.astype(jnp.float32) + dt_bias.astype(jnp.float32))
    a_neg = -jnp.exp(a_log.astype(jnp.float32))
    xh = xs.reshape(b, s, H_B, P_B)
    y = _ssd(xh, dt, a_neg, bm.reshape(b, s, G_B, N_B), cm.reshape(b, s, G_B, N_B))
    y = y + d_skip.astype(jnp.float32)[:, None] * xh
    y = y.reshape(b, s, D_INNER) * jax.nn.silu(zb.astype(jnp.float32))
    y = _rmsnorm(y.reshape(b, s, G_B, D_INNER // G_B), norm_g.reshape(G_B, D_INNER // G_B))
    return y.reshape(b, s, D_INNER).astype(zb.dtype)

def _hybrid_mixer(h, layer, w_in, gate_bias, diff_lambda, diff_subln_g, conv_w, conv_b,
                  dt_bias, a_log, d_skip, norm_g, w_branch, w_out):
    b, s, _ = h.shape
    qa, ka, va, zb, xbc, dtb, qc, kc, vc, gpre = jnp.split(h @ w_in, SPLIT_POINTS, axis=-1)
    o_a = _diff_attention(qa, ka, va, diff_lambda, diff_subln_g, layer)
    o_b = _mamba2(zb, xbc, dtb, conv_w, conv_b, dt_bias, a_log, d_skip, norm_g)
    o_c = _stick_breaking(qc, kc, vc)
    branches = jnp.stack([o_a, o_b.astype(h.dtype), o_c], axis=2)
    proj = jnp.einsum('bsrc,rcd->bsrd', branches, w_branch)
    gates = jax.nn.sigmoid(gpre.reshape(b, s, N_BRANCH, D_MODEL) + gate_bias)
    merged = jnp.einsum('bsrd,bsrd->bsd', gates, proj)
    return merged @ w_out

def second_inputs(seed: int = 0) -> dict:
    key = jax.random.key(seed)
    ks = jax.random.split(key, 24)
    f32 = jnp.float32
    L = DEPTH_2

    def nrm(k, shape, scale):
        return jax.random.normal(k, shape, f32) * scale

    dt0 = jnp.exp(jax.random.uniform(ks[11], (L, H_B), f32, math.log(1e-3), math.log(1e-1)))
    return {
        'x': nrm(ks[0], (BATCH, SEQ, D_MODEL), 1.0),
        'ffn1_w_in': nrm(ks[1], (L, D_MODEL, 2 * D_FF), DEEPNORM_BETA * D_MODEL ** -0.5),
        'ffn1_w_out': nrm(ks[2], (L, D_FF, D_MODEL), DEEPNORM_BETA * D_FF ** -0.5),
        'ln1_g': 1.0 + nrm(ks[3], (L, D_MODEL), 0.02),
        'ln1_b': nrm(ks[4], (L, D_MODEL), 0.02),
        'w_mix_in': nrm(ks[5], (L, D_MODEL, N_IN), D_MODEL ** -0.5),
        'gate_bias': nrm(ks[6], (L, N_BRANCH, D_MODEL), 0.02),
        'diff_lambda': nrm(ks[7], (L, 4, HD_A), 0.1),
        'diff_subln_g': 1.0 + nrm(ks[8], (L, 2 * HD_A), 0.02),
        'ssm_conv_w': nrm(ks[9], (L, CONV_B, CONV_DIM), CONV_B ** -0.5),
        'ssm_conv_b': nrm(ks[10], (L, CONV_DIM), 0.02),
        'ssm_dt_bias': dt0 + jnp.log(-jnp.expm1(-dt0)),
        'ssm_A_log': jnp.log(jax.random.uniform(ks[12], (L, H_B), f32, 1.0, 16.0)),
        'ssm_D': 1.0 + nrm(ks[13], (L, H_B), 0.02),
        'ssm_norm_g': 1.0 + nrm(ks[14], (L, D_INNER), 0.02),
        'w_branch': nrm(ks[15], (L, N_BRANCH, BR_W, D_MODEL), DEEPNORM_BETA * BR_W ** -0.5),
        'w_mix_out': nrm(ks[16], (L, D_MODEL, D_MODEL), DEEPNORM_BETA * D_MODEL ** -0.5),
        'ln2_g': 1.0 + nrm(ks[17], (L, D_MODEL), 0.02),
        'ln2_b': nrm(ks[18], (L, D_MODEL), 0.02),
        'ffn2_w_in': nrm(ks[19], (L, D_MODEL, 2 * D_FF), DEEPNORM_BETA * D_MODEL ** -0.5),
        'ffn2_w_out': nrm(ks[20], (L, D_FF, D_MODEL), DEEPNORM_BETA * D_FF ** -0.5),
        'ln3_g': 1.0 + nrm(ks[21], (L, D_MODEL), 0.02),
        'ln3_b': nrm(ks[22], (L, D_MODEL), 0.02),
    }

def second_block(x, ffn1_w_in, ffn1_w_out, ln1_g, ln1_b, w_mix_in, gate_bias, diff_lambda,
              diff_subln_g, ssm_conv_w, ssm_conv_b, ssm_dt_bias, ssm_A_log, ssm_D, ssm_norm_g,
              w_branch, w_mix_out, ln2_g, ln2_b, ffn2_w_in, ffn2_w_out, ln3_g, ln3_b):
    for l in range(DEPTH_2):
        x = _layernorm(DEEPNORM_ALPHA * x + FFN_RES * _swiglu(x, ffn1_w_in[l], ffn1_w_out[l]),
                       ln1_g[l], ln1_b[l])
        mix = _hybrid_mixer(x, l, w_mix_in[l], gate_bias[l], diff_lambda[l], diff_subln_g[l],
                            ssm_conv_w[l], ssm_conv_b[l], ssm_dt_bias[l], ssm_A_log[l], ssm_D[l],
                            ssm_norm_g[l], w_branch[l], w_mix_out[l])
        x = _layernorm(DEEPNORM_ALPHA * x + mix, ln2_g[l], ln2_b[l])
        x = _layernorm(DEEPNORM_ALPHA * x + FFN_RES * _swiglu(x, ffn2_w_in[l], ffn2_w_out[l]),
                       ln3_g[l], ln3_b[l])
    return x


def setup_inputs(seed=0):
    out = dict(first_inputs(seed))
    for name, value in second_inputs(seed + 1).items():
        if name != "x":
            out[name + "_2"] = value
    return out


def reference(
    x, mem, positions, mix_norm_g, mem_norm_g, w_in, moba_q_norm_g, moba_k_norm_g, dil_q_norm_g,
    dil_k_norm_g, mem_q_norm_g, mem_k_norm_g, w_mem_kv, w_branch_moba, w_branch_dil,
    w_branch_mem, w_out, ffn_norm_g, w_ffn_up, ffn_conv_w, ffn_conv_b, w_ffn_down, ffn1_w_in_2,
    ffn1_w_out_2, ln1_g_2, ln1_b_2, w_mix_in_2, gate_bias_2, diff_lambda_2, diff_subln_g_2,
    ssm_conv_w_2, ssm_conv_b_2, ssm_dt_bias_2, ssm_A_log_2, ssm_D_2, ssm_norm_g_2, w_branch_2,
    w_mix_out_2, ln2_g_2, ln2_b_2, ffn2_w_in_2, ffn2_w_out_2, ln3_g_2, ln3_b_2,
):
    x = first_block(
        x, mem, positions, mix_norm_g, mem_norm_g, w_in, moba_q_norm_g, moba_k_norm_g,
        dil_q_norm_g, dil_k_norm_g, mem_q_norm_g, mem_k_norm_g, w_mem_kv, w_branch_moba,
        w_branch_dil, w_branch_mem, w_out, ffn_norm_g, w_ffn_up, ffn_conv_w, ffn_conv_b,
        w_ffn_down,
    )
    return second_block(
        x, ffn1_w_in_2, ffn1_w_out_2, ln1_g_2, ln1_b_2, w_mix_in_2, gate_bias_2, diff_lambda_2,
        diff_subln_g_2, ssm_conv_w_2, ssm_conv_b_2, ssm_dt_bias_2, ssm_A_log_2, ssm_D_2,
        ssm_norm_g_2, w_branch_2, w_mix_out_2, ln2_g_2, ln2_b_2, ffn2_w_in_2, ffn2_w_out_2,
        ln3_g_2, ln3_b_2,
    )


_drawn_inputs = setup_inputs


def setup_inputs(seed=0):
    import zlib

    import numpy as np

    out = dict(_drawn_inputs(seed))
    spreads = {}
    factors = {'mix_norm_g': 8.0,
     'mem_norm_g': 8.0,
     'moba_q_norm_g': 8.0,
     'moba_k_norm_g': 8.0,
     'dil_q_norm_g': 8.0,
     'dil_k_norm_g': 8.0,
     'mem_q_norm_g': 8.0,
     'mem_k_norm_g': 8.0,
     'ffn_norm_g': 3.871,
     'ffn_conv_b': 7.688,
     'gate_bias_2': 8.0,
     'diff_lambda_2': 6.242,
     'diff_subln_g_2': 33.284,
     'ssm_conv_b_2': 8.0,
     'ssm_A_log_2': 27.856,
     'ssm_D_2': 29.426,
     'ssm_norm_g_2': 26.473}
    for name, (base, spread) in spreads.items():
        noise = np.random.default_rng([zlib.crc32(name.encode()), seed]).standard_normal(out[name].shape)
        drawn = base * np.exp(spread * noise) if base else spread * noise
        out[name] = jnp.asarray(drawn.astype(out[name].dtype))
    for name, factor in factors.items():
        out[name] = (out[name] * factor).astype(out[name].dtype)
    return out
```

```python
from contextlib import ExitStack

import numpy as np

import concourse.bass as bass
from concourse import mybir

ALU = mybir.AluOpType
ACT = mybir.ActivationFunctionType
F32 = mybir.dt.float32
I32 = mybir.dt.int32
AX_X = mybir.AxisListType.X

P = 128
D = 1024
TOK = 256
T = TOK // P
KD = D // P
FF = 2816
KF = FF // P
FFC = KF // 2
HD = 64
BANK = 512
LAYERS = 2
SLOTS = 4
SLOT = 2048
ALPHA = (2 * LAYERS) ** 0.25
FFN_RES = 0.5
RMS_EPS = 1e-6
LN_EPS = 1e-5
SCALE = HD ** -0.5
NEG = -1e30

QKV1 = 2560
GATE1 = QKV1
TOKW = 3072
NORMED = [(0, 6, 0, True), (384, 6, 1, True), (1152, 6, 2, True), (1536, 6, 3, True),
          (2304, 4, 4, False), (2560, 4, 5, False)]
Q_COL = [0, 128, 256, 1152, 1280, 1408, 2304, 2432]
K_COL = [384, 512, 640, 1536, 1664, 1792, 2560, 2688]
V_COL = [768, 896, 1024, 1920, 2048, 2176, 2816, 2944]
PAIRS = 8
BRANCH_TILES = (3, 3, 2)

MIX = dict(qa=0, ka=1024, va=2048, zb=3072, xbc=4096, dt=5632, qc=5648, kc=6672, vc=7696, gate=8720)
NH = 16
DH = 8
N_XBC = 12
CAUS = 384

CONST = {}
_at = 0
for _name, _n in (("ident", 128), ("ones", 128), ("after", 128), ("upto", 256), ("from_on", 128),
                  ("strict_neg", CAUS), ("causal", CAUS), ("chunk_neg", CAUS), ("cos", T * 16), ("sin", T * 16),
                  ("freq", 32), ("lam", 4), ("minus_half", 1), ("moba_neg", CAUS), ("dil_add", CAUS)):
    CONST[_name] = (_at, _at + _n)
    _at += _n
CONST_ALL = _at
CONST_W = CONST["moba_neg"][0]

ROWS1 = dict(mix=0, mem=8, ffn=16, conv_b=24)
N_ROWS1 = 68
N_CONV1 = 3 * 2 * KF
ROWS2 = dict(ln_g=(0, 16, 32), ln_b=(8, 24, 40), gate_b=48, norm=72, subln=80)
N_ROWS2 = 81
N_CONV2 = 5 * N_XBC


def constants():
    i = np.arange(P)[:, None]
    j = np.arange(P)[None, :]
    t = np.arange(TOK)[None, :]
    c = np.zeros((P, CONST_ALL), np.float32)

    def put(name, a):
        c[:, CONST[name][0]:CONST[name][1]] = a

    def queries(rule):
        return np.concatenate([rule(i, j), rule(i + P, t)], axis=1)

    def keys(rule):
        return np.concatenate([rule(i, t), rule(i, j)], axis=1)

    put("ident", i == j)
    put("ones", 1.0)
    put("after", i > j)
    put("upto", i <= t)
    put("from_on", i >= j)
    put("strict_neg", keys(lambda k, q: np.where(k < q, 0.0, NEG)))
    put("causal", keys(lambda k, q: k <= q))
    put("chunk_neg", queries(lambda q, k: np.where(k // HD <= q // HD, 0.0, NEG)))
    put("moba_neg", queries(lambda q, k: np.where(k <= q, 0.0, NEG)))

    def dilated(q, k):
        n = (k <= q) * ((q - k <= 128) * 1 + ((q - k) % 4 == 0) * 1 + ((q - k) % 16 == 0) * 1)
        return np.where(n > 0, np.log(np.maximum(n, 1)), NEG)

    put("dil_add", queries(dilated))
    half = 8
    inv = (np.float32(500000.0) ** (-np.arange(half, dtype=np.float32) * np.float32(2.0) / np.float32(16))).astype(np.float32)
    ang = (np.arange(TOK, dtype=np.float32)[:, None] * inv[None, :]).astype(np.float32)
    for name, f in (("cos", np.cos), ("sin", np.sin)):
        v = f(ang).astype(np.float32).reshape(T, P, half).transpose(1, 0, 2)
        first = -v if name == "sin" else v
        put(name, np.concatenate([first, v], axis=2).reshape(P, T * 16))
    put("freq", np.float32(10000.0) ** (-np.arange(32, dtype=np.float32) / np.float32(32)))
    lam = [0.8 - 0.6 * np.exp(-0.3 * layer) for layer in range(LAYERS)]
    put("minus_half", -0.5)
    put("lam", np.array([[lam[0], 1 - lam[0], lam[1], 1 - lam[1]]]))
    return c



class Chunk:

    def __init__(self, name, index, mode, srcs, act, pair, evacs=1):
        self.name, self.index, self.mode, self.srcs, self.act = name, index, mode, srcs, act
        self.pair, self.evacs = pair, evacs


class Plan:

    def __init__(self):
        self.slot = 0
        self.free = [0, 0, 0, 0]

    def chunk(self, c):
        c.slot0 = self.slot
        self.slot += 2
        c.need = {b: self.free[b] for b in (2 * c.pair, 2 * c.pair + 1)}
        for b in c.need:
            self.free[b] += c.evacs
        return c

    def ffn(self, f):
        f["slot0"], f["free0"] = self.slot, list(self.free)
        self.slot += 3 * FFC
        self.free = [n + FFC // 2 + (1 if b < 2 else 0) + 1 for b, n in enumerate(self.free)]
        return f


def beats_of(n, stages, lags):
    return [[(s, i - lag) for s, lag in zip(stages, lags) if 0 <= i - lag < n]
            for i in range(n + max(lags))]


def woven(chunks, beats, first, rate):
    steps, done, halves, prev = [], 0, 0, None
    for n, c in enumerate(chunks):
        for half in range(2):
            steps.append(("half", c, half))
            if half == 0 and prev is not None:
                steps.append(("drain", prev))
            if n >= first:
                halves += 1
                while done < len(beats) and done < rate * halves:
                    steps += beats[done]
                    done += 1
        prev = c
    return steps + [("drain", prev)], beats[done:]


def plan_block1(plan):
    chunks = [Chunk("tok", n, "A", [("w_in", h, n * BANK) for h in range(2)], "xT", n % 2) for n in range(5)]
    chunks += [Chunk("tok", 5, "A", [("w_mem_kv", h, 0) for h in range(2)], "memT", 1)]
    chunks += [Chunk("gate1", n, "B", [("w_in", None, GATE1 + n * BANK + h * TOK) for h in range(2)], "xT", n % 2)
               for n in range(6)]
    head = [plan.chunk(c) for c in chunks]
    beats = [[("pair1", p), ("pair1", p + 1)] for p in range(0, PAIRS, 2)]
    beats += beats_of(2 * PAIRS, ("out1", "turn1", "score1"), (3, 2, 0))
    return head, beats


def plan_layer(plan):
    def a(name, n, pair, evacs=1, w="w_mix_in_2", act="xT"):
        return Chunk(name, n, "A", [(w, h, MIX.get(name, 0) + n * BANK) for h in range(2)], act, pair, evacs)

    def b(name, n, pair, w="w_mix_in_2", act="xT"):
        return Chunk(name, n, "B", [(w, None, MIX.get(name, 0) + n * BANK + h * TOK) for h in range(2)], act, pair)

    jobs = [(a, "qa", n, 2) for n in range(2)] + [(a, "ka", n, 2) for n in range(2)] + [(a, "va", n, 1) for n in range(2)]
    jobs += [(b, "zb", n) for n in range(2)] + [(b, "xbc", n) for n in range(3)]
    jobs += [(b, "qc", n) for n in range(2)] + [(b, "kc", n) for n in range(2)] + [(a, "vc", n, 1) for n in range(2)]
    jobs += [(b, "gate", n) for n in range(6)]
    ffn1 = plan.ffn({"index": 0})
    ffn1["after"] = list(plan.free)
    mix = [plan.chunk(j[0](j[1], j[2], i % 2, *j[3:])) for i, j in enumerate(jobs)]
    for r, act in enumerate(("oAT", "oBT", "oCT")):
        for n in range(2):
            c = b("branch", n, (len(mix)) % 2, w=("w_branch_2", r), act=act)
            c.r = r
            mix.append(plan.chunk(c))
    out = [plan.chunk(a("out", n, n, w="w_mix_out_2", act="mT")) for n in range(2)]
    out[1].after = list(plan.free)
    ffn2 = plan.ffn({"index": 1})
    return ffn1, mix, out, ffn2


def mixer_steps(mix):
    beats = [[("turn_qk", 2 * j), ("turn_qk", 2 * j + 1)] for j in range(4)]
    beats += beats_of(2 * DH, ("dout", "dturn", "dscore"), (3, 2, 0))
    beats += [[("turn_oa", 0), ("turn_oa", 1)], [("turn_oa", 2), ("turn_oa", 3)]]
    beats += [[("turn_xs", 0), ("turn_xs", 1)], [("turn_xs", 2), ("turn_xs", 3)], [("cb", 0), ("cb", 1)]]
    beats += beats_of(NH, ("sout", "sdecay"), (2, 0))
    beats += [[("snorm", 0), ("snorm", 1)]]
    beats += beats_of(NH, ("kout", "ksum", "ksoft", "kscore"), (3, 2, 1, 0))
    steps, rest = woven(mix, beats, 6, 1.75)
    assert not rest
    steps.insert(steps.index(("half", mix[6], 0)), ("dt",))
    return steps


def program(nc, ins, out):
    plan = Plan()
    head1, beats1 = plan_block1(plan)
    branch1_slot0 = plan.slot
    plan.slot += 4
    out1 = [plan.chunk(Chunk("out1", n, "A", [("w_out", h, n * BANK) for h in range(2)], "mT", n)) for n in range(2)]
    ffn0 = plan.ffn({"index": None})
    start = (plan.slot, list(plan.free))
    ffn1, mix, out2, ffn2 = plan_layer(plan)
    SLOT_LAP = plan.slot - start[0]
    FREE_LAP = [n - m for n, m in zip(plan.free, start[1])]
    assert SLOT_LAP % SLOTS == 0
    steps1, rest1 = woven(head1, beats1, 6, 2.0)
    steps1 += [step for beat in rest1 for step in beat]
    mixed = mixer_steps(mix)

    ctx = ExitStack()
    with ctx:
        def sb(name, shape, dt=F32):
            return ctx.enter_context(nc.sbuf_tensor(name, shape, dt))

        def sem(name):
            return ctx.enter_context(nc.semaphore(name))

        ring = sb("ring", [P, SLOTS, SLOT])
        const = sb("const", [P, CONST_W])
        x = sb("x", [P, T, D])
        xT = sb("xT", [P, KD, TOK])
        wide = sb("wide", [P, 24, TOK])
        tok = sb("tok", [P, 3 * T * D])
        qT = sb("qT", [P, KD, TOK])
        kT = sb("kT", [P, KD, TOK])
        zT = sb("zT", [P, KD, TOK])
        xbc = sb("xbc", [P, N_XBC, TOK])
        qcT = sb("qcT", [P, KD, TOK])
        kcT = sb("kcT", [P, KD, TOK])
        vc = sb("vc", [P, T, D])
        gb = sb("gb", [P, 2, D])
        h2 = wide[:, 0:KF, :]
        xhat = vc
        tok1 = tok[:, :].rearrange("p (t n) -> p t n", t=T)
        qa = tok[:, 0:T * D].rearrange("p (t n) -> p t n", t=T)
        ka = tok[:, T * D:2 * T * D].rearrange("p (t n) -> p t n", t=T)
        va = tok[:, 2 * T * D:3 * T * D].rearrange("p (t n) -> p t n", t=T)
        oA, xs = qa, ka
        mT = tok[:, 2 * T * D:3 * T * D].rearrange("p (k n) -> p k n", k=KD)
        acts = {"xT": xT, "memT": xbc[:, 0:KD, :], "oAT": qT, "oBT": zT, "oCT": kT, "mT": mT}
        o1T = zT
        const1 = xbc[:, KD:KD + 3, :].rearrange("p a n -> p (a n)")
        act_s = sb("act_s", [P, 2, BANK])
        conv_s = sb("conv_s", [P, 2, BANK])
        sm = sb("sm", [P, 2, BANK])
        ex = sb("ex", [P, 2, BANK])
        wt = sb("wt", [P, 2, BANK])
        lmat = sb("lmat", [P, 2, CAUS])
        cbm = sb("cbm", [P, 2, CAUS])
        seg_w = act_s[:, :, 0:3 * P]
        small = sb("small", [P, 256])
        cols = sb("cols", [P, 256])
        rows = sb("rows", [P, 2, P])
        bcast = sb("bcast", [P, 4 * HD + 6 * HD + 3 * NH])
        dtw = sb("dtw", [P, KD, NH])
        dts = sb("dts", [P, 6, T * NH])
        conv1 = sb("conv1", [P, N_CONV1 + N_ROWS1])
        stats = sb("stats", [P, T, 12])
        act_j = sb("act_j", [P, P])
        pos = sb("pos", [P, T], I32)
        ps = ctx.enter_context(nc.psum_tensor("ps", [P, 8, BANK], F32))
        S0, S1, TB, OB = 4, 5, 6, 7

        def cst(name):
            a, b = CONST[name]
            return const[:, a:b] if b <= CONST_W else const1[:, a - CONST_W:b - CONST_W]

        ident, ones, after, upto, from_on = (cst(n) for n in ("ident", "ones", "after", "upto", "from_on"))

        w_loaded = [sem(f"w_loaded{i}") for i in range(SLOTS)]
        drained = [sem(f"drained{b}") for b in range(4)]
        multiplied, in_loaded, par1_loaded, par_loaded, rows1_loaded = (sem(n) for n in ("multiplied", "in_loaded", "par1_loaded", "par_loaded", "rows1_loaded"))
        rows_loaded, gb_loaded, rows1_turned, rows_turned, cols_ready = (sem(n) for n in ("rows_loaded", "gb_loaded", "rows1_turned", "rows_turned", "cols_ready"))
        sq_ready, stat_ready, hat_ready, hat_turned, xT_act = (sem(n) for n in ("sq_ready", "stat_ready", "hat_ready", "hat_turned", "xT_act"))
        xT_dve, x_ready, x_added, conv_begun, conv_tap = (sem(n) for n in ("xT_dve", "x_ready", "x_added", "conv_begun", "conv_tap"))
        act_ready, h_ready, dve_chain, act_chain, pool_chain = (sem(n) for n in ("act_ready", "h_ready", "dve_chain", "act_chain", "pool_chain"))
        angle_ready, sin_ready, norm1_done, pair1_turned, pair1_copied = (sem(n) for n in ("angle_ready", "sin_ready", "norm1_done", "pair1_turned", "pair1_copied"))
        score1_ready, masked1, peak1, exp1, prob1 = (sem(n) for n in ("score1_ready", "masked1", "peak1", "exp1", "prob1"))
        prob1_turned, prob1_copied, out1_ready, out1_copied, branch1_free = (sem(n) for n in ("prob1_turned", "prob1_copied", "out1_ready", "out1_copied", "branch1_free"))
        mixed1, q_turned, q_copied, k_turned, k_copied = (sem(n) for n in ("mixed1", "q_turned", "q_copied", "k_turned", "k_copied"))
        d_score, d_masked, d_peak, d_exp, d_w = (sem(n) for n in ("d_score", "d_masked", "d_peak", "d_exp", "d_w"))
        d_turned, d_copied, d_out, d_sq, d_norm = (sem(n) for n in ("d_turned", "d_copied", "d_out", "d_sq", "d_norm"))
        oa_turned, oa_copied, lam_arg, lam_exp, lam_ready = (sem(n) for n in ("oa_turned", "oa_copied", "lam_arg", "lam_exp", "lam_ready"))
        dt_ready, dt_arg, dt_log, dt_done, z_exp = (sem(n) for n in ("dt_ready", "dt_arg", "dt_log", "dt_done", "z_exp"))
        xbc_begun, xbc_exp, xbc_done, xs_turned, xs_copied = (sem(n) for n in ("xbc_begun", "xbc_exp", "xbc_done", "xs_turned", "xs_copied"))
        cb_ready, cb_masked, seg_built, seg_ready, seg_exp = (sem(n) for n in ("cb_ready", "cb_masked", "seg_built", "seg_ready", "seg_exp"))
        l_ready, y_ready, y_gated, y_sq, y_sum = (sem(n) for n in ("l_ready", "y_ready", "y_gated", "y_sq", "y_sum"))
        o_b, s_score, s_masked, s_abs, s_log = (sem(n) for n in ("o_b", "s_score", "s_masked", "s_abs", "s_log"))
        s_soft, s_sum, s_arg, s_exp, s_out = (sem(n) for n in ("s_soft", "s_sum", "s_arg", "s_exp", "s_out"))
        s_copied, mixed_sem, out_stored = (sem(n) for n in ("s_copied", "mixed_sem", "out_stored"))
        root_asked, root_done = sem("root_asked"), sem("root_done")
        ROOTS_LAP = 3 * T + 2 * DH + 2

        def lap(L, k, per):
            return k if L is None else L * per + k

        CHAIN_LAP = 2000

        class Chain:

            def __init__(self, eng, s):
                self.eng, self.sem, self.n, self.L = eng, s, 0, None

            def link(self, ins):
                self.n += 1
                ins.then_inc(self.sem, 1)

            def sync(self):
                self.eng.wait_ge(self.sem, lap(self.L, self.n, CHAIN_LAP))

            def enter(self, L):
                self.L, self.n0 = L, self.n

            def leave(self):
                self.eng.sem_inc(self.sem, CHAIN_LAP - (self.n - self.n0))

        block = ctx.enter_context(nc.Block())

        @block.sync
        def _(sp):
            sp.dma_start(const[:, :], ins["const"][:, 0:CONST_W]).then_inc(in_loaded, 16)
            sp.dma_start(const1, ins["const"][:, CONST_W:CONST_ALL]).then_inc(in_loaded, 16)
            sp.dma_start(x[:, :, :], ins["x"][0].rearrange("(t p) n -> p t n", p=P)).then_inc(in_loaded, 16)
            sp.dma_start(gb[:, :, :], ins["mem"][0].rearrange("(t p) n -> p t n", p=P)).then_inc(in_loaded, 16)

            def slot_wait(L, s, more=0):
                if L is not None or s >= SLOTS:
                    sp.wait_ge(multiplied, lap(L, s - SLOTS + 1, SLOT_LAP) + more)

            def matrix(L, w):
                if isinstance(w, tuple):
                    return ins[w[0]][bass.ds(L, 1), w[1]].rearrange("a k n -> (a k) n")
                if L is None:
                    return ins[w][0]
                return ins[w][bass.ds(L, 1)].rearrange("a k n -> (a k) n")

            def load(L, s, src):
                w, half, c0 = src
                m = matrix(L, w)
                if s != mix[0].slot0:
                    slot_wait(L, s)
                if half is None:
                    a = m[:, c0:c0 + TOK].rearrange("(k p) n -> p k n", p=P)
                    d = ring[:, s % SLOTS, :].rearrange("p (k n) -> p k n", n=TOK)
                else:
                    a = m[half * 4 * P:(half + 1) * 4 * P, c0:c0 + BANK].rearrange("(k p) n -> p k n", p=P)
                    d = ring[:, s % SLOTS, :].rearrange("p (k n) -> p k n", n=BANK)
                sp.dma_start(d, a).then_inc(w_loaded[s % SLOTS], 16)

            def chunk_loads(L, chunks):
                for c in chunks:
                    for h in range(2):
                        load(L, c.slot0 + h, c.srcs[h])

            def ffn_loads(L, f, up, down, between=None):
                s0 = f["slot0"]
                wu, wd = matrix(L, up), matrix(L, down)

                def up_loads(it, js):
                    for j in js:
                        if len(js) == 1:
                            slot_wait(L, s0 + 2 * j + 1, it * 4)
                        for side in range(2):
                            s = s0 + 2 * j + side
                            if len(js) > 1:
                                slot_wait(L, s, it * 4)
                            a = wu[:, bass.ds(it * BANK + (j * TOK + side * FF), TOK)].rearrange("(k p) n -> p k n", p=P)
                            sp.dma_start(ring[:, s % SLOTS, :].rearrange("p (k n) -> p k n", n=TOK), a)\
                                .then_inc(w_loaded[s % SLOTS], 16)

                with sp.Fori(0, FFC // 2) as it:
                    up_loads(it, range(2))
                up_loads(FFC // 2, range(1))
                if between:
                    between()
                for i in range(FFC):
                    s = s0 + 2 * FFC + i
                    slot_wait(L, s + (i == FFC - 1))
                    a = wd[i * 2 * P:(i + 1) * 2 * P, :].rearrange("(k p) n -> p k n", p=P)
                    sp.dma_start(ring[:, s % SLOTS, :].rearrange("p (k n) -> p k n", n=D), a)\
                        .then_inc(w_loaded[s % SLOTS], 16)

            chunk_loads(None, head1)
            for j in range(4):
                s = branch1_slot0 + j
                slot_wait(None, s)
                d = ring[:, s % SLOTS, :].rearrange("p (k n) -> p k n", n=TOK)
                k0 = 0
                for w, n in zip(("w_branch_moba", "w_branch_dil", "w_branch_mem"), BRANCH_TILES):
                    sp.dma_start(d[:, k0:k0 + n, :], ins[w][0][:, j * TOK:(j + 1) * TOK].rearrange("(k p) n -> p k n", p=P))\
                        .then_inc(w_loaded[s % SLOTS], 16)
                    k0 += n
            chunk_loads(None, out1)
            ffn_loads(None, ffn0, "w_ffn_up", "w_ffn_down")
            with sp.Fori(0, LAYERS) as L:
                def row(name):
                    return ins[name][bass.ds(L, 1)].rearrange("l (a b) -> (l a) b", b=P)

                sp.wait_ge(rows_turned, lap(L, 0, 1))
                for k in range(3):
                    for s, at in (("g", ROWS2["ln_g"][k]), ("b", ROWS2["ln_b"][k])):
                        sp.dma_start(rows[at:at + 8, 0, :], row(f"ln{k + 1}_{s}_2")).then_inc(rows_loaded, 16)
                at = ROWS2["gate_b"]
                sp.dma_start(rows[at:at + 24, 0, :], ins["gate_bias_2"][bass.ds(L, 1)].rearrange("l r (a b) -> (l r a) b", b=P)).then_inc(rows_loaded, 16)
                at = ROWS2["norm"]
                sp.dma_start(rows[at:at + 8, 0, :], row("ssm_norm_g_2")).then_inc(rows_loaded, 16)
                at = ROWS2["subln"]
                sp.dma_start(rows[at:at + 1, 0, :], ins["diff_subln_g_2"][bass.ds(L, 1)]).then_inc(rows_loaded, 16)
                sp.dma_start(rows[0:4 * N_XBC, 1, :], ins["ssm_conv_w_2"][bass.ds(L, 1)].rearrange("l j (a b) -> (l j a) b", b=P)).then_inc(rows_loaded, 16)
                sp.dma_start(rows[4 * N_XBC:5 * N_XBC, 1, :], row("ssm_conv_b_2")).then_inc(rows_loaded, 16)
                sp.wait_ge(dt_done, lap(L, 0, 1))
                sp.wait_ge(lam_ready, lap(L, 0, 1))
                sp.dma_start(bcast[:, 0:256], ins["diff_lambda_2"][bass.ds(L, 1)].rearrange("l a d -> l (a d)").to_broadcast([P, 256])).then_inc(par_loaded, 16)
                sp.dma_start(bcast[:, 640:656], ins["ssm_dt_bias_2"][bass.ds(L, 1)].to_broadcast([P, NH])).then_inc(par_loaded, 16)
                sp.dma_start(bcast[:, 656:672], ins["ssm_A_log_2"][bass.ds(L, 1)].to_broadcast([P, NH])).then_inc(par_loaded, 16)
                sp.dma_start(bcast[:, 672:688], ins["ssm_D_2"][bass.ds(L, 1)].to_broadcast([P, NH])).then_inc(par_loaded, 16)
                sp.dma_start(dtw[:, :, :], ins["w_mix_in_2"][bass.ds(L, 1), :, MIX["dt"]:MIX["dt"] + NH].rearrange("l (k p) n -> p (l k) n", p=P))\
                    .then_inc(par_loaded, 16)

                def load_gb(k):
                    if k == 0:
                        sp.wait_ge(hat_ready, 4)
                    sp.wait_ge(x_ready, lap(L, 2 * k, 6))
                    for i, side in enumerate("gb"):
                        sp.dma_start(gb[:, i, :], ins[f"ln{k + 1}_{side}_2"][bass.ds(L, 1)].to_broadcast([P, D])).then_inc(gb_loaded, 16)

                ffn_loads(L, ffn1, "ffn1_w_in_2", "ffn1_w_out_2", lambda: load_gb(0))
                chunk_loads(L, mix[:6])
                load_gb(1)
                chunk_loads(L, mix[6:] + out2)
                ffn_loads(L, ffn2, "ffn2_w_in_2", "ffn2_w_out_2", lambda: load_gb(2))

        def bank(b):
            return ps[:, b, :]

        def tiles(b):
            return ps[:, b, :].rearrange("p (f n) -> p f n", n=TOK)

        def wait_drained(eng, L, c):
            for b, n in c.need.items():
                eng.wait_ge(drained[b], lap(L, n + c.evacs, FREE_LAP[b]))

        def wait_products(eng, L, c, more=0):
            eng.wait_ge(multiplied, lap(L, c.slot0 + 2, SLOT_LAP) + more)

        @block.tensor
        def _(pe):
            def wait_block(L, s, more=0):
                extra = 16 * (len(BRANCH_TILES) - 1) if s >= branch1_slot0 else 0
                pe.wait_ge(w_loaded[s % SLOTS], lap(L, 16 * (s // SLOTS + 1) + extra, 16 * SLOT_LAP // SLOTS) + more)

            def wait_xT(L, event):
                pe.wait_ge(xT_act, lap(L, 2 * event, 6))
                pe.wait_ge(xT_dve, lap(L, 2 * event, 6))

            def half(L, c, h):
                act = acts[c.act]
                if h == 0:
                    for b, n in c.need.items():
                        if n:
                            pe.wait_ge(drained[b], lap(L, n, FREE_LAP[b]))
                s = c.slot0 + h
                wait_block(L, s)
                if c.mode == "A":
                    w = ring[:, s % SLOTS, :].rearrange("p (k n) -> p k n", n=BANK)
                    for t in range(T):
                        for k in range(4):
                            mm = pe.matmul(bank(2 * c.pair + t), act[:, 4 * h + k, t * P:(t + 1) * P], w[:, k, :],
                                           start=(h == 0 and k == 0), stop=(h == 1 and k == 3))
                else:
                    w = ring[:, s % SLOTS, :].rearrange("p (k n) -> p k n", n=TOK)
                    for f in range(2):
                        for k in range(KD):
                            mm = pe.matmul(tiles(2 * c.pair + h)[:, f, :], w[:, k, f * P:(f + 1) * P], act[:, k, :],
                                           start=(k == 0), stop=(k == KD - 1))
                mm.then_inc(multiplied, 1)

            def ffn(L, f, event, before_down=None):
                s0 = f["slot0"]

                def up(it, js):
                    for j in js:
                        for side in range(2):
                            b = 2 * j + side
                            s = s0 + b
                            if side == 0:
                                wait_xT(L, event)
                            pe.wait_ge(drained[b], lap(L, f["free0"][b], FREE_LAP[b]) + it)
                            wait_block(L, s, it * 16)
                            w = ring[:, s % SLOTS, :].rearrange("p (k n) -> p k n", n=TOK)
                            for ft in range(2):
                                for k in range(KD):
                                    mm = pe.matmul(tiles(b)[:, ft, :], w[:, k, ft * P:(ft + 1) * P], xT[:, k, :],
                                                   start=(k == 0), stop=(k == KD - 1))
                            mm.then_inc(multiplied, 1)

                with pe.Fori(0, FFC // 2) as it:
                    up(it, range(2))
                up(FFC // 2, range(1))
                if before_down:
                    before_down()
                for b in range(4):
                    pe.wait_ge(drained[b], lap(L, f["free0"][b] + FFC // 2 + (b < 2), FREE_LAP[b]))
                if f["index"] is None:
                    pe.wait_ge(h_ready, FFC)
                for i in range(FFC):
                    s = s0 + 2 * FFC + i
                    wait_block(L, s)
                    w = ring[:, s % SLOTS, :].rearrange("p (k n) -> p k n", n=D)
                    for t in range(T):
                        for n in range(2):
                            for k in range(2):
                                mm = pe.matmul(bank(2 * n + t), h2[:, 2 * i + k, t * P:(t + 1) * P],
                                               w[:, k, n * BANK:(n + 1) * BANK],
                                               start=(i == 0 and k == 0), stop=(i == FFC - 1 and k == 1))
                    mm.then_inc(multiplied, 1)

            def norm(L, event, src):
                for t in range(T):
                    pe.wait_ge(hat_ready, lap(L, 2 * event + t + 1, 6))
                    for g in range(2):
                        for k in range(4):
                            tr = pe.transpose(ps[:, 4 + 2 * t + g, k * P:(k + 1) * P],
                                              src[:, t, (4 * g + k) * P:(4 * g + k + 1) * P], ident)
                        tr.then_inc(hat_turned, 1)

            pe.wait_ge(in_loaded, 4 * 16)
            pe.wait_ge(rows1_loaded, 6 * 16)
            rows1 = wide[:, 0:2, :].rearrange("p a (b n) -> p (a b) n", n=P)
            pe.transpose(bank(4)[:, 0:88], rows1[0:88, 0, :], ident[0:88, 0:88])
            pe.transpose(bank(4)[:, 88:132], rows1[0:44, 1, :], ident[0:44, 0:44])
            pe.transpose(bank(4)[:, 132:132 + N_ROWS1], rows1[0:N_ROWS1, 2, :], ident[0:N_ROWS1, 0:N_ROWS1])\
                .then_inc(rows1_turned, 1)
            pe.wait_ge(cols_ready, 1)
            norm(None, 0, xhat)
            wait_xT(None, 1)
            norm(None, 1, xhat)

            def pair1(p):
                segs = (2, 4, 6)[(p >= 3) + (p >= 6)]
                pe.wait_ge(norm1_done, 2 * segs)
                if p >= 2:
                    pe.wait_ge(pair1_copied, p - 1)
                for a, col in enumerate((Q_COL[p], K_COL[p])):
                    for t in range(T):
                        tr = pe.transpose(ps[:, TB + p % 2, (2 * a + t) * P:(2 * a + t + 1) * P], tok1[:, t, col:col + P], ident)
                tr.then_inc(pair1_turned, 1)

            def keys1(u):
                return P if u % 2 == 0 and u // 2 < 6 else TOK

            def score1(u):
                p, qt, nk = u // 2, u % 2, keys1(u)
                pe.wait_ge(pair1_copied, p + 1)
                if u:
                    pe.wait_ge(masked1, u)
                for m in range(2):
                    r = slice(HD * m, HD * (m + 1))
                    mm = pe.matmul(ps[:, S0 + m, (u % 2) * TOK:(u % 2) * TOK + nk], qT[r, p, qt * P:(qt + 1) * P],
                                   kT[r, p, 0:nk], start=True, stop=True)
                mm.then_inc(score1_ready, 1)

            def turn1(u):
                nt = keys1(u) // P
                pe.wait_ge(prob1, u + 1)
                if u == 0:
                    pe.wait_ge(pair1_copied, PAIRS)
                else:
                    pe.wait_ge(prob1_copied, u)
                for m in range(2):
                    for k in range(nt):
                        tr = pe.transpose(ps[:, TB, (m * nt + k) * P:(m * nt + k + 1) * P],
                                          ex[:, u % 2, (m * nt + k) * P:(m * nt + k + 1) * P], ident)
                tr.then_inc(prob1_turned, 1)

            def out1_of(u):
                p, nt = u // 2, keys1(u) // P
                pe.wait_ge(prob1_copied, u + 1)
                if u == 0:
                    for c in head1[:6]:
                        wait_drained(pe, None, c)
                else:
                    pe.wait_ge(out1_copied, u)
                for m in range(2):
                    for k in range(nt):
                        v = V_COL[p] + HD * m
                        mm = pe.matmul(ps[HD * m:HD * (m + 1), OB, (u % 4) * P:(u % 4 + 1) * P], tok1[:, k, v:v + HD],
                                       wt[:, u % 2, (m * nt + k) * P:(m * nt + k + 1) * P],
                                       start=(k == 0), stop=(k == nt - 1))
                mm.then_inc(out1_ready, 1)

            for step in steps1:
                if step[0] == "half":
                    if step[1].act == "memT" and step[2] == 0:
                        wait_xT(None, 2)
                    half(None, step[1], step[2])
                elif step[0] == "pair1":
                    pair1(step[1])
                elif step[0] == "score1":
                    score1(step[1])
                elif step[0] == "turn1":
                    turn1(step[1])
                elif step[0] == "out1":
                    out1_of(step[1])
            pe.wait_ge(out1_copied, 2 * PAIRS)
            for c in head1[-2:]:
                wait_drained(pe, None, c)
            for j in range(4):
                s = branch1_slot0 + j
                if j >= 2:
                    pe.wait_ge(branch1_free, j - 1)
                wait_block(None, s)
                w = ring[:, s % SLOTS, :].rearrange("p (k n) -> p k n", n=TOK)
                k0 = 0
                for r, n in enumerate(BRANCH_TILES):
                    for f in range(2):
                        for k in range(k0, k0 + n):
                            mm = pe.matmul(tiles(4 * (j % 2) + r)[:, f, :], w[:, k, f * P:(f + 1) * P], o1T[:, k, :],
                                           start=(k == k0), stop=(k == k0 + n - 1))
                    k0 += n
                mm.then_inc(multiplied, 1)
            pe.wait_ge(mixed1, 4)
            for c in out1:
                for h in range(2):
                    half(None, c, h)
            norm(None, 2, xhat)
            ffn(None, ffn0, 3)
            norm(None, 3, x)

            with pe.Fori(0, LAYERS) as L:
                def turn_rows():
                    pe.wait_ge(rows_loaded, lap(L, 11 * 16, 11 * 16))
                    pe.transpose(bank(OB)[:, 0:N_ROWS2], rows[0:N_ROWS2, 0, :], ident[0:N_ROWS2, 0:N_ROWS2])
                    pe.transpose(bank(OB)[:, P:P + N_CONV2], rows[0:N_CONV2, 1, :], ident[0:N_CONV2, 0:N_CONV2])\
                        .then_inc(rows_turned, 1)

                def dt():
                    pe.wait_ge(par_loaded, lap(L, 5 * 16, 5 * 16))
                    for t in range(T):
                        for k in range(KD):
                            mm = pe.matmul(ps[:, OB, t * NH:(t + 1) * NH], xT[:, k, t * P:(t + 1) * P], dtw[:, k, :],
                                           start=(k == 0), stop=(k == KD - 1))
                    mm.then_inc(dt_ready, 1)

                def turn_qk(j):
                    which, hp = j % 2, j // 2
                    src = (qa, ka)[which]
                    wait_drained(pe, L, mix[2 * which + hp // 2])
                    if hp == 0 and which == 1:
                        pe.wait_ge(dt_arg, lap(L, 1, 1))
                    if hp:
                        pe.wait_ge((q_copied, k_copied)[which], lap(L, hp, 4))
                    for h in range(2):
                        for t in range(T):
                            tr = pe.transpose(ps[:, TB + which, (2 * h + t) * P:(2 * h + t + 1) * P],
                                              src[:, t, (2 * hp + h) * P:(2 * hp + h + 1) * P], ident)
                    tr.then_inc((q_turned, k_turned)[which], 1)

                def dscore(u):
                    h, qt = u // 2, u % 2
                    nk = P * (1 + qt)
                    pe.wait_ge(q_copied, lap(L, h // 2 + 1, 4))
                    pe.wait_ge(k_copied, lap(L, h // 2 + 1, 4))
                    if u:
                        pe.wait_ge(d_masked, lap(L, u, 2 * DH))
                    for m in range(2):
                        r = slice(HD * m, HD * (m + 1))
                        mm = pe.matmul(ps[:, S0 + m, (u % 2) * TOK:(u % 2) * TOK + nk], qT[r, h, qt * P:(qt + 1) * P],
                                       kT[r, h, 0:nk], start=True, stop=True)
                    mm.then_inc(d_score, 1)

                def dturn(u):
                    pe.wait_ge(d_w, lap(L, u + 1, 2 * DH))
                    if u:
                        pe.wait_ge(d_copied, lap(L, u, 2 * DH))
                    else:
                        pe.wait_ge(q_copied, lap(L, 4, 4))
                    for k in range(1 + u % 2):
                        tr = pe.transpose(ps[:, TB, (u % 2) * TOK + k * P:(u % 2) * TOK + (k + 1) * P],
                                          ex[:, u % 2, k * P:(k + 1) * P], ident)
                    tr.then_inc(d_turned, 1)

                def dout(u):
                    h, nt = u // 2, 1 + u % 2
                    pe.wait_ge(d_copied, lap(L, u + 1, 2 * DH))
                    if u == 0:
                        for n in (4, 5):
                            wait_drained(pe, L, mix[n])
                        pe.wait_ge(k_copied, lap(L, 4, 4))
                    else:
                        pe.wait_ge(d_norm, lap(L, u, 2 * DH))
                    for k in range(nt):
                        mm = pe.matmul(ps[:, OB, (u % 4) * P:(u % 4 + 1) * P], wt[:, u % 2, k * P:(k + 1) * P],
                                       va[:, k, h * P:(h + 1) * P], start=(k == 0), stop=(k == nt - 1))
                    mm.then_inc(d_out, 1)

                def turn_oa(j):
                    if j < 2:
                        pe.wait_ge(d_norm, lap(L, 2 * DH, 2 * DH))
                    else:
                        pe.wait_ge(oa_copied, lap(L, j - 1, 4))
                    for h in range(2):
                        for t in range(T):
                            tr = pe.transpose(ps[:, TB + j % 2, (2 * h + t) * P:(2 * h + t + 1) * P],
                                              oA[:, t, (2 * j + h) * P:(2 * j + h + 1) * P], ident)
                    tr.then_inc(oa_turned, 1)

                def turn_xs(j):
                    if j < 2:
                        pe.wait_ge(oa_copied, lap(L, j + 3, 4))
                        pe.wait_ge(xbc_done, lap(L, 6, 6))
                    else:
                        pe.wait_ge(xs_copied, lap(L, j - 1, 4))
                    for t in range(T):
                        for f in range(2):
                            tr = pe.transpose(ps[:, TB + j % 2, (2 * t + f) * P:(2 * t + f + 1) * P],
                                              xbc[:, 2 * j + f, t * P:(t + 1) * P], ident)
                    tr.then_inc(xs_turned, 1)

                def causal_pair(out_bank, lhs0, lhs1, rhs):
                    pe.matmul(ps[:, out_bank, 0:TOK], lhs0, rhs[:, 0:TOK], start=True, stop=True)
                    return pe.matmul(ps[:, out_bank, TOK:CAUS], lhs1, rhs[:, P:TOK], start=True, stop=True)

                def causal_values(m, b, v0, v1, w):
                    r = slice(HD * m, HD * (m + 1))
                    pe.matmul(ps[r, b, 0:TOK], v0, w[:, 0:TOK], start=True, stop=False)
                    return pe.matmul(ps[r, b, P:TOK], v1, w[:, TOK:CAUS], start=False, stop=True)

                def cb(g):
                    if g == 0:
                        pe.wait_ge(d_masked, lap(L, 2 * DH, 2 * DH))
                        pe.wait_ge(xbc_done, lap(L, 6, 6))
                    causal_pair(S0 + g, xbc[:, 8 + g, 0:P], xbc[:, 8 + g, P:TOK], xbc[:, 10 + g, :]).then_inc(cb_ready, 1)

                def sdecay(u):
                    b = S0 + u % 2
                    pe.wait_ge(seg_built, lap(L, u + 1, NH))
                    if u < 2:
                        pe.wait_ge(cb_masked, lap(L, 2, 2))
                    else:
                        pe.wait_ge(seg_exp, lap(L, u - 1, NH))
                    w = seg_w[:, u % 2, :]
                    pe.matmul(ps[:, b, 0:TOK], w[:, 0:P], upto, start=True, stop=False)
                    pe.matmul(ps[:, b, P:TOK], w[:, 2 * P:3 * P], upto[:, 0:P], start=False, stop=True)
                    pe.matmul(ps[:, b, TOK:CAUS], w[:, P:2 * P], upto[:, 0:P], start=True, stop=True).then_inc(seg_ready, 1)

                def sout(u):
                    p = u // 2
                    pe.wait_ge(l_ready, lap(L, u + 1, NH))
                    if u == 0:
                        pe.wait_ge(xs_copied, lap(L, 4, 4))
                    if p >= 2 and u % 2 == 0:
                        pe.wait_ge(y_gated, lap(L, p - 1, NH // 2))
                    causal_values(u % 2, TB + p % 2, xs[:, 0, u * HD:(u + 1) * HD], xs[:, 1, u * HD:(u + 1) * HD],
                                  lmat[:, u % 2, :]).then_inc(y_ready, 1)

                def snorm(g):
                    pe.wait_ge(y_sq, lap(L, g + 1, 2))
                    pe.wait_ge(y_gated, lap(L, NH // 2, NH // 2))
                    w = wt[:, :, :].rearrange("p a (b n) -> p (a b) n", n=TOK)
                    for k in range(4):
                        mm = pe.matmul(ps[:, TB + g, 0:TOK], ones, w[:, k, :], start=(k == 0), stop=(k == 3))
                    mm.then_inc(y_sum, 1)

                def kscore(u):
                    r, pair = slice(HD * (u % 2), HD * (u % 2 + 1)), u // 2
                    if u == 0:
                        for c in mix[11:15]:
                            wait_drained(pe, L, c)
                    if u < 2:
                        pe.wait_ge(seg_exp, lap(L, NH, NH))
                    else:
                        pe.wait_ge(s_masked, lap(L, u - 1, NH))
                    causal_pair(S0 + u % 2, kcT[r, pair, 0:P], kcT[r, pair, P:TOK], qcT[r, pair, :]).then_inc(s_score, 1)

                def ksum(u):
                    pe.wait_ge(s_soft, lap(L, u + 1, NH))
                    if u == 0:
                        pe.wait_ge(o_b, lap(L, 2, 2))
                    else:
                        pe.wait_ge(s_arg, lap(L, u, NH))
                    sp_ = lmat[:, u % 2, :]
                    pe.matmul(ps[:, TB, TOK:CAUS], from_on, sp_[:, TOK:CAUS], start=True, stop=True)
                    pe.matmul(ps[:, TB, 0:TOK], from_on, sp_[:, 0:TOK], start=True, stop=False)
                    pe.matmul(ps[:, TB, P:TOK], ones, sp_[:, TOK:CAUS], start=False, stop=True).then_inc(s_sum, 1)

                def kout(u):
                    p = u // 2
                    pe.wait_ge(s_exp, lap(L, u + 1, NH))
                    if u == 0:
                        for c in mix[15:17]:
                            wait_drained(pe, L, c)
                    if u % 2 == 0:
                        if p:
                            pe.wait_ge(s_copied, lap(L, p, NH // 2))
                        else:
                            pe.wait_ge(o_b, lap(L, 2, 2))
                    causal_values(u % 2, OB, vc[:, 0, u * HD:(u + 1) * HD], vc[:, 1, u * HD:(u + 1) * HD],
                                  ex[:, u % 2, :]).then_inc(s_out, 1)

                attention = dict(turn_qk=turn_qk, dscore=dscore, dturn=dturn, dout=dout, turn_oa=turn_oa, turn_xs=turn_xs,
                                 cb=cb, sdecay=sdecay, sout=sout, snorm=snorm, kscore=kscore, ksum=ksum, kout=kout)
                ffn(L, ffn1, 4, turn_rows)
                pe.wait_ge(cols_ready, lap(L, 2, 1))
                norm(L, 4, xhat)
                wait_xT(L, 5)
                for step in mixed:
                    if step[0] == "half":
                        c = step[1]
                        if c.name == "branch" and c.index == 0 and step[2] == 0:
                            if c.r == 0:
                                pe.wait_ge(oa_copied, lap(L, 4, 4))
                            elif c.r == 1:
                                pe.wait_ge(o_b, lap(L, 2, 2))
                            else:
                                pe.wait_ge(s_copied, lap(L, NH // 2, NH // 2))
                        half(L, c, step[2])
                    elif step[0] == "dt":
                        dt()
                    elif step[0] in attention:
                        attention[step[0]](step[1])
                pe.wait_ge(mixed_sem, lap(L, 4, 4))
                for c in out2:
                    for h in range(2):
                        half(L, c, h)
                norm(L, 5, xhat)
                ffn(L, ffn2, 6)
                norm(L, 6, xhat)

        @block.scalar
        def _(act):
            chain = Chain(act, act_chain)

            def norm_cols(L, event, g, b, dst):
                for t in range(T):
                    act.wait_ge(hat_turned, lap(L, 4 * event + 2 * t + 1, 12))
                    for k in range(4):
                        o, i = dst[:, k, t * P:(t + 1) * P], ps[:, 4 + 2 * t, k * P:(k + 1) * P]
                        if g is None:
                            ins_ = act.activation(o, i, ACT.Copy)
                        elif b is None:
                            ins_ = act.activation(o, i, ACT.Copy, scale=g[:, k:k + 1])
                        else:
                            ins_ = act.activation(o, i, ACT.Identity, scale=g[:, k:k + 1], bias=b[:, k:k + 1])
                    ins_.then_inc(xT_act, 1)

            def squares(src, event):
                for t in range(T):
                    if event >= 2:
                        act.wait_ge(x_added, t + 1)
                    if 2 * event + t:
                        act.wait_ge(sq_ready, 2 * event + t)
                    act.activation(wide[:, 4:8, :].rearrange("p a n -> p (a n)"), src[:, t, :], ACT.Square,
                                   accum_out=small[:, 64 + 2 * event + t:65 + 2 * event + t]).then_inc(sq_ready, 1)

            def ffn_silu(L, f):
                def up(it, js):
                    for j in js:
                        act.wait_ge(multiplied, lap(L, f["slot0"] + 2 * j + 1, SLOT_LAP) + it * 4)
                        act.wait_ge(drained[2 * j + 1], lap(L, f["free0"][2 * j + 1], FREE_LAP[2 * j + 1]) + it)
                        act.activation(act_s[:, j, :], bank(2 * j), ACT.Silu).then_inc(drained[2 * j], 1)

                with act.Fori(0, FFC // 2) as it:
                    up(it, range(2))
                up(FFC // 2, range(1))

            def ffn_conv(f):
                def up(it, js):
                    for j in js:
                        act.wait_ge(multiplied, f["slot0"] + 2 * j + 2 + it * 4)
                        act.wait_ge(h_ready, it * 2)
                        for side, dst in enumerate((act_s, conv_s)):
                            for ft in range(2):
                                tile = it * 4 + (2 * j + ft + side * KF)
                                ins_ = act.activation(
                                    dst[:, j, ft * TOK:(ft + 1) * TOK], tiles(2 * j + side)[:, ft, :], ACT.Identity,
                                    scale=conv1[:, bass.ds(tile + 2 * 2 * KF, 1)],
                                    bias=conv1[:, bass.ds(tile + N_CONV1 + ROWS1["conv_b"], 1)])
                        ins_.then_inc(conv_begun, 1)
                        act.wait_ge(drained[2 * j], f["free0"][2 * j] + it + 1)
                        act.activation(act_s[:, j, :], act_s[:, j, :], ACT.Silu).then_inc(act_ready, 1)

                with act.Fori(0, FFC // 2) as it:
                    up(it, range(2))
                up(FFC // 2, range(1))

            act.wait_ge(in_loaded, 4 * 16)
            squares(x, 0)
            squares(gb, 1)
            act.wait_ge(angle_ready, 1)
            act.activation(kcT[:, 7, 128:256], kcT[:, 7, 0:128], ACT.Sin).then_inc(sin_ready, 1)
            act.wait_ge(cols_ready, 1)
            g1 = conv1[:, N_CONV1:N_CONV1 + N_ROWS1]
            norm_cols(None, 0, g1[:, 0:8], None, xT)
            norm_cols(None, 1, g1[:, 8:16], None, acts["memT"])

            def drain_tok(c):
                wait_products(act, None, c)
                col = c.index * BANK
                for t in range(T):
                    act.activation(tok1[:, t, col:col + BANK], bank(2 * c.pair + t), ACT.Copy).then_inc(drained[2 * c.pair + t], 1)

            def drain_gate1(c):
                wait_products(act, None, c)
                for j in range(2):
                    k = 4 * c.index + 2 * j
                    act.activation(wide[:, k:k + 2, :], tiles(2 * c.pair + j), ACT.Exp, scale=-1.0)\
                        .then_inc(drained[2 * c.pair + j], 1)

            def pair1(p):
                act.wait_ge(pair1_turned, p + 1)
                act.activation(qT[:, p, :], ps[:, TB + p % 2, 0:TOK], ACT.Copy)
                act.activation(kT[:, p, :], ps[:, TB + p % 2, TOK:BANK], ACT.Copy).then_inc(pair1_copied, 1)

            def keys1(u):
                return P if u % 2 == 0 and u // 2 < 6 else TOK

            def score1(u):
                nk, at = keys1(u), (u % 4) * 16
                act.wait_ge(peak1, u + 1)
                if u >= 2:
                    act.wait_ge(prob1_turned, u - 1)
                for m in range(2):
                    ins_ = act.activation(ex[:, u % 2, m * nk:(m + 1) * nk], sm[:, u % 2, m * nk:(m + 1) * nk], ACT.Exp,
                                          bias=small[:, at + m:at + m + 1], accum_out=small[:, at + 2 + m:at + 3 + m])
                ins_.then_inc(exp1, 1)

            def turn1(u):
                act.wait_ge(prob1_turned, u + 1)
                if u >= 2:
                    act.wait_ge(out1_ready, u - 1)
                act.activation(wt[:, u % 2, 0:2 * keys1(u)], ps[:, TB, 0:2 * keys1(u)], ACT.Copy).then_inc(prob1_copied, 1)

            def out1_of(u):
                act.wait_ge(out1_ready, u + 1)
                act.activation(o1T[:, u // 2, (u % 2) * P:(u % 2 + 1) * P], ps[:, OB, (u % 4) * P:(u % 4 + 1) * P], ACT.Copy)\
                    .then_inc(out1_copied, 1)

            for step in steps1:
                if step[0] == "drain":
                    (drain_tok if step[1].name == "tok" else drain_gate1)(step[1])
                elif step[0] == "pair1":
                    pair1(step[1])
                elif step[0] == "score1":
                    score1(step[1])
                elif step[0] == "turn1":
                    turn1(step[1])
                elif step[0] == "out1":
                    out1_of(step[1])
            squares(x, 2)
            norm_cols(None, 2, g1[:, 16:24], None, xT)
            ffn_conv(ffn0)
            norm_cols(None, 3, None, None, xT)

            with act.Fori(0, LAYERS) as L:
                chain.enter(L)

                def xhat_of(k):
                    for t in range(T):
                        act.wait_ge(stat_ready, lap(L, 2 * k + t + 1, 6))
                        s = small[:, 96 + 4 * t:96 + 4 * t + 4]
                        act.activation(xhat[:, t, :], x[:, t, :], ACT.Identity, scale=s[:, 2:3], bias=s[:, 3:4]).then_inc(hat_ready, 1)

                def layer_norm(k):
                    xhat_of(k)
                    g, b = ROWS2["ln_g"][k], ROWS2["ln_b"][k]
                    norm_cols(L, 4 + k, cols[:, g:g + 8], cols[:, b:b + 8], xT)

                def drain(c):
                    p = c.pair
                    if c.name in ("qa", "ka"):
                        dst = qa if c.name == "qa" else ka
                        wait_products(act, L, c)
                        for t in range(T):
                            o = dst[:, t, c.index * BANK:(c.index + 1) * BANK].rearrange("p (m d) -> p m d", d=HD)
                            i = bank(2 * p + t).rearrange("p (m d) -> p m d", d=HD)
                            act.activation(o[:, :, 16:HD], i[:, :, 16:HD], ACT.Copy).then_inc(drained[2 * p + t], 1)
                    elif c.name == "va":
                        wait_products(act, L, c)
                        for t in range(T):
                            act.activation(va[:, t, c.index * BANK:(c.index + 1) * BANK], bank(2 * p + t), ACT.Copy)\
                                .then_inc(drained[2 * p + t], 1)
                    elif c.name == "zb":
                        wait_products(act, L, c)
                        if c.index:
                            wait_drained(act, L, mix[6])
                        for j in range(2):
                            act.activation(act_s[:, j, :], bank(2 * p + j), ACT.Exp, scale=-1.0).then_inc(z_exp, 1)
                    elif c.name == "xbc":
                        wait_products(act, L, c)
                        if c.index == 0:
                            wait_drained(act, L, mix[7])
                        else:
                            act.wait_ge(xbc_done, lap(L, 2 * c.index, 6))
                        for j in range(2):
                            for f in range(2):
                                k = 4 * c.index + 2 * j + f
                                ins_ = act.activation(conv_s[:, j, f * TOK:(f + 1) * TOK], tiles(2 * p + j)[:, f, :], ACT.Identity,
                                                      scale=cols[:, P + 3 * N_XBC + k:P + 3 * N_XBC + k + 1],
                                                      bias=cols[:, P + 4 * N_XBC + k:P + 4 * N_XBC + k + 1])
                            ins_.then_inc(xbc_begun, 1)
                        for j in range(2):
                            act.wait_ge(drained[2 * p + j], lap(L, c.need[2 * p + j] + 1, FREE_LAP[2 * p + j]))
                            act.activation(act_s[:, j, :], conv_s[:, j, :], ACT.Exp, scale=-1.0).then_inc(xbc_exp, 1)
                    elif c.name in ("qc", "kc"):
                        wait_products(act, L, c)
                        dst = qcT if c.name == "qc" else kcT
                        act.activation(dst[:, 4 * c.index:4 * c.index + 2, :], tiles(2 * p), ACT.Copy).then_inc(drained[2 * p], 1)
                    elif c.name == "vc":
                        wait_products(act, L, c)
                        act.wait_ge(x_ready, lap(L, 2, 6))
                        act.activation(vc[:, 0, c.index * BANK:(c.index + 1) * BANK], bank(2 * p), ACT.Copy).then_inc(drained[2 * p], 1)
                    elif c.name == "gate":
                        wait_products(act, L, c)
                        for j in range(2):
                            for f in range(2):
                                k = 4 * c.index + 2 * j + f
                                ins_ = act.activation(wide[:, k, :], tiles(2 * p + j)[:, f, :], ACT.Exp, scale=-1.0,
                                                      bias=small[:, 128 + k:129 + k])
                            ins_.then_inc(drained[2 * p + j], 1)

                def dt():
                    act.wait_ge(par_loaded, lap(L, 5 * 16, 5 * 16))
                    chain.link(act.activation(dts[:, 5, 0:NH], bcast[:, 656:672], ACT.Exp))
                    act.wait_ge(lam_arg, lap(L, 1, 1))
                    act.activation(small[:, 162:164], small[:, 160:162], ACT.Exp).then_inc(lam_exp, 1)
                    act.wait_ge(dt_arg, lap(L, 1, 1))
                    chain.link(act.activation(dts[:, 2, :], dts[:, 1, :], ACT.Exp, scale=-1.0))
                    chain.sync()
                    act.activation(dts[:, 3, :], dts[:, 2, :], ACT.Ln, bias=1.0).then_inc(dt_log, 1)

                def turn_qk(j):
                    if j % 2 == 0:
                        act.wait_ge(q_turned, lap(L, j // 2 + 1, 4))
                        act.activation(qT[:, j:j + 2, :], tiles(TB), ACT.Copy).then_inc(q_copied, 1)

                def dscore(u):
                    nk, at = P * (1 + u % 2), (u % 4) * 16
                    act.wait_ge(d_peak, lap(L, u + 1, 2 * DH))
                    if u >= 2:
                        act.wait_ge(d_turned, lap(L, u - 1, 2 * DH))
                    for m in range(2):
                        ins_ = act.activation(ex[:, u % 2, m * nk:(m + 1) * nk], sm[:, u % 2, m * nk:(m + 1) * nk], ACT.Exp,
                                              bias=small[:, at + m:at + m + 1], accum_out=small[:, at + 2 + m:at + 3 + m])
                    ins_.then_inc(d_exp, 1)

                def dturn(u):
                    nk = P * (1 + u % 2)
                    act.wait_ge(d_turned, lap(L, u + 1, 2 * DH))
                    if u >= 2:
                        act.wait_ge(d_out, lap(L, u - 1, 2 * DH))
                    act.activation(wt[:, u % 2, 0:nk], ps[:, TB, (u % 2) * TOK:(u % 2) * TOK + nk], ACT.Copy).then_inc(d_copied, 1)

                def dout(u):
                    at = (u % 4) * 16
                    act.wait_ge(d_out, lap(L, u + 1, 2 * DH))
                    act.wait_ge(d_sq, lap(L, u, 2 * DH))
                    act.activation(act_j[:, :], ps[:, OB, (u % 4) * P:(u % 4 + 1) * P], ACT.Square,
                                   accum_out=small[:, at + 7:at + 8]).then_inc(d_sq, 1)

                def turn_oa(j):
                    act.wait_ge(oa_turned, lap(L, j + 1, 4))
                    if j == 0:
                        act.wait_ge(lam_ready, lap(L, 1, 1))
                    act.activation(qT[:, 2 * j:2 * j + 2, :], tiles(TB + j % 2), ACT.Copy, scale=small[:, 166:167]).then_inc(oa_copied, 1)

                def turn_xs(j):
                    act.wait_ge(xs_turned, lap(L, j + 1, 4))
                    act.activation(xs[:, :, 2 * j * P:(2 * j + 2) * P], tiles(TB + j % 2), ACT.Copy).then_inc(xs_copied, 1)

                def sdecay(u):
                    act.wait_ge(seg_ready, lap(L, u + 1, NH))
                    if u < 2:
                        act.wait_ge(d_turned, lap(L, 2 * DH, 2 * DH))
                    else:
                        act.wait_ge(l_ready, lap(L, u - 1, NH))
                    act.activation(ex[:, u % 2, 0:CAUS], ps[:, S0 + u % 2, 0:CAUS], ACT.Exp).then_inc(seg_exp, 1)

                def snorm(g):
                    act.wait_ge(y_gated, lap(L, 4 * (g + 1), NH // 2))
                    if g:
                        act.wait_ge(y_sum, lap(L, g, 2))
                    act.activation(wt[:, :, :].rearrange("p a n -> p (a n)"),
                                   zT[:, 4 * g:4 * g + 4, :].rearrange("p a n -> p (a n)"), ACT.Square).then_inc(y_sq, 1)

                def kscore(u):
                    b = lmat[:, u % 2, :]
                    act.wait_ge(s_abs, lap(L, u + 1, NH))
                    chain.link(act.activation(b, b, ACT.Exp, scale=-1.0))
                    chain.sync()
                    act.activation(b, b, ACT.Ln, bias=1.0).then_inc(s_log, 1)

                def ksum(u):
                    act.wait_ge(s_arg, lap(L, u + 1, NH))
                    if u < 2:
                        act.wait_ge(l_ready, lap(L, NH, NH))
                    else:
                        act.wait_ge(s_out, lap(L, u - 1, NH))
                    act.activation(ex[:, u % 2, 0:CAUS], sm[:, u % 2, 0:CAUS], ACT.Exp).then_inc(s_exp, 1)

                def kout(u):
                    if u % 2:
                        p = u // 2
                        act.wait_ge(s_out, lap(L, u + 1, NH))
                        act.activation(kT[:, p, :], ps[:, OB, 0:TOK], ACT.Copy).then_inc(s_copied, 1)

                attention = dict(turn_qk=turn_qk, dscore=dscore, dturn=dturn, dout=dout, turn_oa=turn_oa, turn_xs=turn_xs,
                                 sdecay=sdecay, snorm=snorm, kscore=kscore, ksum=ksum, kout=kout, drain=drain)
                ffn_silu(L, ffn1)
                act.wait_ge(cols_ready, lap(L, 2, 1))
                layer_norm(0)
                for step in mixed:
                    if step[0] == "dt":
                        dt()
                    elif step[0] in attention:
                        attention[step[0]](step[1])
                layer_norm(1)
                ffn_silu(L, ffn2)
                layer_norm(2)
                chain.leave()

        @block.vector
        def _(dve):
            chain = Chain(dve, dve_chain)
            link, sync = chain.link, chain.sync

            roots = [0]

            def ask_root(L, ins_):
                ins_.then_inc(root_asked, 1)
                roots[0] += 1
                dve.wait_ge(root_done, lap(L, roots[0], ROOTS_LAP))

            def silu(out_, e, v):
                share(e)
                return dve.tensor_tensor(out_, v, e, ALU.mult)

            def share(e):
                link(dve.tensor_scalar(e, e, 1.0, None, ALU.add))
                sync()
                link(dve.reciprocal(e, e))
                sync()

            def gates(L, c):
                wait_drained(dve, L, c)
                for j in range(2):
                    k = 4 * c.index + 2 * j
                    share(wide[:, k:k + 2, :].rearrange("p a n -> p (a n)"))

            def norm_cols(L, event, g, b, dst):
                for t in range(T):
                    dve.wait_ge(hat_turned, lap(L, 4 * event + 2 * t + 2, 12))
                    for k in range(4):
                        o, i = dst[:, 4 + k, t * P:(t + 1) * P], ps[:, 5 + 2 * t, k * P:(k + 1) * P]
                        if g is None:
                            ins_ = dve.tensor_copy(o, i)
                        elif b is None:
                            ins_ = dve.tensor_scalar(o, i, g[:, 4 + k:5 + k], None, ALU.mult)
                        else:
                            ins_ = dve.tensor_scalar(o, i, g[:, 4 + k:5 + k], b[:, 4 + k:5 + k], ALU.mult, ALU.add)
                    ins_.then_inc(xT_dve, 1)

            def rms_rows(src, event):
                for t in range(T):
                    r = small[:, 64 + 2 * event + t:65 + 2 * event + t]
                    dve.wait_ge(sq_ready, 2 * event + t + 1)
                    ask_root(None, dve.tensor_scalar(r, r, D * RMS_EPS, None, ALU.add))
                    if event == 1:
                        dve.wait_ge(hat_turned, 2 * t + 2)
                    dve.tensor_scalar(xhat[:, t, :], src[:, t, :], r, float(D) ** 0.5, ALU.mult, ALU.mult).then_inc(hat_ready, 1)

            def ffn_mul(L, f):
                def up(it, js):
                    for j in js:
                        b = 2 * j
                        dve.wait_ge(drained[b], lap(L, f["free0"][b] + 1, FREE_LAP[b]) + it)
                        dve.wait_ge(multiplied, lap(L, f["slot0"] + b + 2, SLOT_LAP) + it * 4)
                        dve.tensor_tensor(h2[:, bass.ds(it * 4 + 2 * j, 2), :].rearrange("p a n -> p (a n)"),
                                          act_s[:, j, :], bank(b + 1), ALU.mult).then_inc(drained[b + 1], 1)

                with dve.Fori(0, FFC // 2) as it:
                    up(it, range(2))
                up(FFC // 2, range(1))

            def ffn_conv(f):
                def up(it, js):
                    for j in js:
                        dve.wait_ge(conv_begun, it * 2 + j + 1)
                        for tap in (1, 0):
                            s = 2 - tap
                            if tap == 0:
                                dve.wait_ge(conv_tap, it * 2 + j + 1)
                            for side, dst in enumerate((act_s, conv_s)):
                                for ft in range(2):
                                    tile = it * 4 + (2 * j + ft + side * KF)
                                    o = dst[:, j, ft * TOK + s:(ft + 1) * TOK]
                                    ins_ = dve.scalar_tensor_tensor(
                                        o, tiles(2 * j + side)[:, ft, 0:TOK - s],
                                        conv1[:, bass.ds(tile + tap * 2 * KF, 1)], o, ALU.mult, ALU.add)
                                if tap == 0:
                                    ins_.then_inc(drained[2 * j + side], 1)
                            if tap == 1:
                                ins_.then_inc(conv_tap, 1)
                        dve.wait_ge(act_ready, it * 2 + j + 1)
                        dve.wait_ge(drained[2 * j + 1], f["free0"][2 * j + 1] + it + 1)
                        dve.tensor_tensor(h2[:, bass.ds(it * 4 + 2 * j, 2), :].rearrange("p a n -> p (a n)"),
                                          act_s[:, j, :], conv_s[:, j, :], ALU.mult).then_inc(h_ready, 1)

                with dve.Fori(0, FFC // 2) as it:
                    up(it, range(2))
                up(FFC // 2, range(1))

            dve.wait_ge(in_loaded, 4 * 16)
            dve.wait_ge(rows1_turned, 1)
            dve.tensor_copy(conv1[:, :], ps[:, 4, 0:N_CONV1 + N_ROWS1]).then_inc(cols_ready, 1)
            dve.wait_ge(cols_ready, 1)
            rms_rows(x, 0)
            dve.wait_ge(par1_loaded, 8 * 16)
            posf, ang, turns, red = small[:, 80:82], kcT[:, 6, 0:64], kcT[:, 6, 64:128], kcT[:, 7, 0:128]
            link(dve.tensor_copy(posf, pos[:, :]))
            sync()
            for t in range(T):
                link(dve.tensor_scalar(ang[:, 32 * t:32 * t + 32], cst("freq"), posf[:, t:t + 1], None, ALU.mult))
            sync()
            link(dve.tensor_scalar(turns, ang, float(1 / (2 * np.pi)), 12582912.0, ALU.mult, ALU.add))
            sync()
            link(dve.tensor_scalar(turns, turns, 12582912.0, None, ALU.subtract))
            sync()
            c1 = 6.28125
            c2 = int((2 * np.pi - c1) * 2 ** 20) / 2 ** 20
            c3 = float(2 * np.pi - c1 - c2)
            for c in (c1, c2, c3):
                link(dve.scalar_tensor_tensor(ang, turns, -c, ang, ALU.mult, ALU.add))
                sync()
            halfpi = float(np.float32(np.pi / 2))
            pi_in = 3.1415925
            link(dve.tensor_scalar(red[:, 0:64], ang, pi_in, -pi_in, ALU.min, ALU.max))
            link(dve.tensor_scalar(red[:, 64:128], ang, halfpi, None, ALU.add))
            sync()
            link(dve.tensor_scalar(turns, red[:, 64:128], float(np.pi), -2 * float(np.pi), ALU.is_gt, ALU.mult))
            sync()
            link(dve.tensor_tensor(red[:, 64:128], red[:, 64:128], turns, ALU.add))
            sync()
            dve.tensor_scalar(red[:, 64:128], red[:, 64:128], pi_in, -pi_in, ALU.min, ALU.max).then_inc(angle_ready, 1)
            norm_cols(None, 0, conv1[:, N_CONV1:N_CONV1 + 8], None, xT)
            rms_rows(gb, 1)
            norm_cols(None, 1, conv1[:, N_CONV1 + 8:N_CONV1 + 16], None, acts["memT"])
            dve.wait_ge(sin_ready, 1)
            sin, cos = kcT[:, 7, 128:192], kcT[:, 7, 192:256]
            gain = bcast[:, 256:640].rearrange("p (a d) -> p a d", d=HD)
            link(dve.tensor_scalar(bcast[:, 256:640], bcast[:, 256:640], float(HD) ** 0.5, None, ALU.mult))
            sync()

            def rot(i, t):
                return qcT[:, i, t * HD:(t + 1) * HD], qcT[:, i, P + t * HD:P + (t + 1) * HD]

            for i in range(4):
                for t in range(T):
                    c_, s_ = rot(i, t)
                    ct, st = cos[:, 32 * t:32 * t + 32], sin[:, 32 * t:32 * t + 32]
                    lo, hi = slice(0, 32), slice(32, HD)
                    link(dve.tensor_tensor(c_[:, lo], gain[:, i, lo], ct, ALU.mult))
                    link(dve.tensor_tensor(c_[:, hi], gain[:, i, hi], ct, ALU.mult))
                    link(dve.scalar_tensor_tensor(s_[:, lo], gain[:, i, hi], -1.0, st, ALU.mult, ALU.mult))
                    link(dve.tensor_tensor(s_[:, hi], gain[:, i, lo], st, ALU.mult))
            sync()

            def norm1(n):
                col, heads, i, turned = NORMED[n]
                for t in range(T):
                    v = tok1[:, t, col:col + heads * HD].rearrange("p (h d) -> p h d", d=HD)
                    sq, xn, rx = (kcT[:, 2 * a:2 * a + 2, :].rearrange("p a n -> p (a n)")[:, 0:heads * HD]
                                  .rearrange("p (h d) -> p h d", d=HD) for a in range(3))
                    r = small[:, 84:84 + heads]
                    if n or t:
                        dve.wait_ge(norm1_done, 2 * n + t)
                    link(dve.tensor_tensor(sq, v, v, ALU.mult))
                    sync()
                    link(dve.tensor_reduce(r, sq, AX_X, ALU.add))
                    sync()
                    ask_root(None, dve.tensor_scalar(r, r, HD * RMS_EPS, None, ALU.add))
                    link(dve.tensor_tensor(xn, v, r.unsqueeze(2).to_broadcast([P, heads, HD]), ALU.mult))
                    sync()
                    if not turned:
                        dve.tensor_tensor(v, xn, gain[:, i, :].unsqueeze(1).to_broadcast([P, heads, HD]), ALU.mult).then_inc(norm1_done, 1)
                        continue
                    c_, s_ = (a.unsqueeze(1).to_broadcast([P, heads, HD]) for a in rot(i, t))
                    link(dve.tensor_tensor(sq, xn, c_, ALU.mult))
                    link(dve.tensor_tensor(rx[:, :, 0:32], xn[:, :, 32:HD], s_[:, :, 0:32], ALU.mult))
                    link(dve.tensor_tensor(rx[:, :, 32:HD], xn[:, :, 0:32], s_[:, :, 32:HD], ALU.mult))
                    sync()
                    dve.tensor_tensor(v, sq, rx, ALU.add).then_inc(norm1_done, 1)

            def drain1(c):
                if c.name == "tok":
                    wait_drained(dve, None, c)
                    norm1(c.index)
                else:
                    gates(None, c)

            def keys1(u):
                return P if u % 2 == 0 and u // 2 < 6 else TOK

            def peak(L, u, nk, per, masked, peak_):
                at = (u % 4) * 16
                dve.wait_ge(masked, lap(L, u + 1, per))
                link(dve.tensor_reduce(small[:, at + 4:at + 6], sm[:, u % 2, 0:2 * nk].rearrange("p (m k) -> p m k", k=nk), AX_X, ALU.max))
                sync()
                dve.tensor_scalar(small[:, at:at + 2], small[:, at + 4:at + 6], -1.0, None, ALU.mult).then_inc(peak_, 1)

            def score1(u):
                p, qt, nk = u // 2, u % 2, keys1(u)
                dve.wait_ge(score1_ready, u + 1)
                if u >= 2:
                    dve.wait_ge(exp1, u - 1)
                o = sm[:, u % 2, 0:2 * nk].rearrange("p (m k) -> p m k", k=nk)
                i = ps[:, S0:S0 + 2, (u % 2) * TOK:(u % 2) * TOK + nk]
                if p < 6:
                    m = cst("moba_neg" if p < 3 else "dil_add")[:, P * qt:P * qt + nk]
                    dve.scalar_tensor_tensor(o, i, SCALE, m.unsqueeze(1).to_broadcast([P, 2, nk]), ALU.mult, ALU.add).then_inc(masked1, 1)
                else:
                    dve.tensor_scalar(o, i, SCALE, None, ALU.mult).then_inc(masked1, 1)
                peak(None, u, nk, 0, masked1, peak1)

            def turn1(u):
                nk, at = keys1(u), (u % 4) * 16
                dve.wait_ge(exp1, u + 1)
                link(dve.reciprocal(small[:, at + 4:at + 6], small[:, at + 2:at + 4]))
                sync()
                for m in range(2):
                    e = ex[:, u % 2, m * nk:(m + 1) * nk]
                    ins_ = dve.tensor_scalar(e, e, small[:, at + 4 + m:at + 5 + m], None, ALU.mult)
                ins_.then_inc(prob1, 1)

            for step in steps1:
                if step[0] == "drain":
                    drain1(step[1])
                elif step[0] == "score1":
                    score1(step[1])
                elif step[0] == "turn1":
                    turn1(step[1])
            for j in range(4):
                b = 4 * (j % 2)
                dve.wait_ge(multiplied, branch1_slot0 + j + 1)
                if j:
                    dve.wait_ge(mixed1, j)
                parts = [mT[:, 2 * j:2 * j + 2, :].rearrange("p a n -> p (a n)"), act_s[:, 0, :], act_s[:, 1, :]]
                for r in range(3):
                    e = wide[:, 8 * r + 2 * j:8 * r + 2 * j + 2, :].rearrange("p a n -> p (a n)")
                    ins_ = dve.tensor_tensor(parts[r], bank(b + r), e, ALU.mult)
                    if r < 2:
                        link(ins_)
                ins_.then_inc(branch1_free, 1)
                sync()
                link(dve.tensor_tensor(parts[0], parts[0], parts[1], ALU.add))
                sync()
                dve.wait_ge(branch1_free, j + 1)
                dve.tensor_tensor(parts[0], parts[0], parts[2], ALU.add).then_inc(mixed1, 1)

            def add_x(L, slots, s, last=None):
                dve.wait_ge(multiplied, lap(L, slots, SLOT_LAP))
                for t in range(T):
                    for n in range(2):
                        xv = x[:, t, n * BANK:(n + 1) * BANK]
                        dve.scalar_tensor_tensor(xv, bank(2 * n + t), s, xv, ALU.mult, ALU.add).then_inc(drained[2 * n + t], 1)
                    yield t

            for t in add_x(None, out1[1].slot0 + 2, 1.0):
                for b in (t, 2 + t):
                    dve.wait_ge(drained[b], out1[b // 2].need[b] + 1)
                dve.sem_inc(x_added, 1)
            rms_rows(x, 2)
            norm_cols(None, 2, conv1[:, N_CONV1 + 16:N_CONV1 + 24], None, xT)
            ffn_conv(ffn0)
            for t in add_x(None, ffn0["slot0"] + 3 * FFC, 1.0):
                for b in (t, 2 + t):
                    dve.wait_ge(drained[b], start[1][b])
                dve.sem_inc(hat_ready, 1)
            norm_cols(None, 3, None, None, xT)

            with dve.Fori(0, LAYERS) as L:
                chain.enter(L)

                def layer_norm(k, slots, s, free):
                    dve.wait_ge(x_ready, lap(L, 2 * k, 6))
                    for t in add_x(L, slots, s):
                        for b in (t, 2 + t):
                            dve.wait_ge(drained[b], lap(L, free[b], FREE_LAP[b]))
                        st = stats[:, t, :]
                        v = small[:, 96 + 4 * t:100 + 4 * t]
                        for n in range(2):
                            link(dve.bn_stats(st[:, 6 * n:6 * n + 6], x[:, t, n * BANK:(n + 1) * BANK]))
                        sync()
                        dve.memset(small[:, 250:251], 0.0)
                        link(dve.bn_aggr(v[:, 0:2], st))
                        sync()
                        ask_root(L, dve.tensor_scalar(v[:, 2:3], v[:, 1:2], LN_EPS / ALPHA ** 2, None, ALU.add))
                        dve.scalar_tensor_tensor(v[:, 3:4], v[:, 0:1], -1.0, v[:, 2:3], ALU.mult, ALU.mult).then_inc(stat_ready, 1)
                    g, b = ROWS2["ln_g"][k], ROWS2["ln_b"][k]
                    norm_cols(L, 4 + k, cols[:, g:g + 8], cols[:, b:b + 8], xT)

                def turn_rows():
                    dve.wait_ge(rows_turned, lap(L, 1, 1))
                    dve.wait_ge(xT_act, lap(L, 8, 6))
                    dve.wait_ge(xT_dve, lap(L, 8, 6))
                    link(dve.tensor_copy(cols[:, 0:N_ROWS2], ps[:, OB, 0:N_ROWS2]))
                    link(dve.tensor_copy(cols[:, P:P + N_CONV2], ps[:, OB, P:P + N_CONV2]))
                    sync()
                    g = ROWS2["gate_b"]
                    dve.tensor_scalar(small[:, 128:152], cols[:, g:g + 24], -1.0, None, ALU.mult).then_inc(cols_ready, 1)

                def drain(c):
                    p = c.pair
                    if c.name in ("qa", "ka"):
                        dst = qa if c.name == "qa" else ka
                        wait_products(dve, L, c)
                        for t in range(T):
                            dve.wait_ge(drained[2 * p + t], lap(L, c.need[2 * p + t] + 1, FREE_LAP[2 * p + t]))
                            i = bank(2 * p + t).rearrange("p (m d) -> p m d", d=HD)
                            o = dst[:, t, c.index * BANK:(c.index + 1) * BANK].rearrange("p (m d) -> p m d", d=HD)
                            a, r = (sm[:, n, t * TOK:t * TOK + P].rearrange("p (m d) -> p m d", d=16) for n in range(2))
                            cs = cst("cos")[:, 16 * t:16 * t + 16].unsqueeze(1).to_broadcast([P, 8, 16])
                            sn = cst("sin")[:, 16 * t:16 * t + 16].unsqueeze(1).to_broadcast([P, 8, 16])
                            link(dve.tensor_tensor(a, i[:, :, 0:16], cs, ALU.mult))
                            link(dve.tensor_tensor(r[:, :, 0:8], i[:, :, 8:16], sn[:, :, 0:8], ALU.mult))
                            link(dve.tensor_tensor(r[:, :, 8:16], i[:, :, 0:8], sn[:, :, 8:16], ALU.mult))
                            sync()
                            dve.tensor_tensor(o[:, :, 0:16], a, r, ALU.add).then_inc(drained[2 * p + t], 1)
                    elif c.name == "zb":
                        for j in range(2):
                            dve.wait_ge(z_exp, lap(L, 2 * c.index + j + 1, 4))
                            k = 4 * c.index + 2 * j
                            silu(zT[:, k:k + 2, :].rearrange("p a n -> p (a n)"), act_s[:, j, :], bank(2 * p + j)).then_inc(drained[2 * p + j], 1)
                    elif c.name == "xbc":
                        for j in range(2):
                            dve.wait_ge(xbc_begun, lap(L, 2 * c.index + j + 1, 6))
                            for s in (1, 2, 3):
                                for f in range(2):
                                    k = P + (3 - s) * N_XBC + 4 * c.index + 2 * j + f
                                    o = conv_s[:, j, f * TOK + s:(f + 1) * TOK]
                                    ins_ = dve.scalar_tensor_tensor(o, tiles(2 * p + j)[:, f, 0:TOK - s], cols[:, k:k + 1], o, ALU.mult, ALU.add)
                                    if s < 3:
                                        link(ins_)
                                if s < 3:
                                    sync()
                            ins_.then_inc(drained[2 * p + j], 1)
                        for j in range(2):
                            dve.wait_ge(xbc_exp, lap(L, 2 * c.index + j + 1, 6))
                            k = 4 * c.index + 2 * j
                            silu(xbc[:, k:k + 2, :].rearrange("p a n -> p (a n)"), act_s[:, j, :], conv_s[:, j, :]).then_inc(xbc_done, 1)
                    elif c.name in ("qc", "kc"):
                        wait_products(dve, L, c)
                        dst = qcT if c.name == "qc" else kcT
                        dve.tensor_copy(dst[:, 4 * c.index + 2:4 * c.index + 4, :], tiles(2 * p + 1)).then_inc(drained[2 * p + 1], 1)
                    elif c.name == "vc":
                        wait_products(dve, L, c)
                        dve.wait_ge(x_ready, lap(L, 2, 6))
                        dve.tensor_copy(vc[:, 1, c.index * BANK:(c.index + 1) * BANK], bank(2 * p + 1)).then_inc(drained[2 * p + 1], 1)
                    elif c.name == "gate":
                        gates(L, c)
                    elif c.name == "branch":
                        wait_products(dve, L, c)
                        for j in range(2):
                            k = 4 * c.index + 2 * j
                            e = wide[:, 8 * c.r + k:8 * c.r + k + 2, :].rearrange("p a n -> p (a n)")
                            m = mT[:, k:k + 2, :].rearrange("p a n -> p (a n)")
                            b = 2 * p + j
                            dve.tensor_tensor(m if c.r == 0 else conv_s[:, j, :], bank(b), e, ALU.mult).then_inc(drained[b], 1)
                            if c.r:
                                dve.wait_ge(drained[b], lap(L, c.need[b] + 1, FREE_LAP[b]))
                                ins_ = dve.tensor_tensor(m, m, conv_s[:, j, :], ALU.add)
                                if c.r == 2:
                                    ins_.then_inc(mixed_sem, 1)
                                else:
                                    link(ins_)
                                    sync()

                def dt():
                    dve.wait_ge(par_loaded, lap(L, 5 * 16, 5 * 16))
                    lf = bcast[:, 0:4 * HD].rearrange("p (a b d) -> p a b d", a=2, b=2)
                    pr = dts[:, 0:4, :].rearrange("p a n -> p (a n)").rearrange("p (a d) -> p a d", d=HD)
                    link(dve.tensor_tensor(pr, lf[:, :, 0, :], lf[:, :, 1, :], ALU.mult))
                    sync()
                    dve.tensor_reduce(small[:, 160:162], pr, AX_X, ALU.add).then_inc(lam_arg, 1)
                    link(dve.tensor_copy(small[:, 168:170], const[:, bass.ds(L * 2 + CONST["lam"][0], 2)]))
                    sync()
                    dve.wait_ge(lam_exp, lap(L, 1, 1))
                    link(dve.tensor_tensor(small[:, 164:165], small[:, 163:164], small[:, 162:163], ALU.subtract))
                    link(dve.tensor_scalar(small[:, 166:167], cols[:, ROWS2["subln"]:ROWS2["subln"] + 1], small[:, 169:170], None, ALU.mult))
                    sync()
                    dve.tensor_tensor(small[:, 165:166], small[:, 164:165], small[:, 168:169], ALU.subtract).then_inc(lam_ready, 1)
                    for m in range(2):
                        link(dve.tensor_copy(small[HD * m:HD * (m + 1), 176:184], bcast[HD * m:HD * (m + 1), 672 + m:688:2]))
                    dve.wait_ge(dt_ready, lap(L, 1, 1))
                    two = lambda n: dts[:, n, :].rearrange("p (t h) -> p t h", t=T)
                    over_t = lambda a: a.unsqueeze(1).to_broadcast([P, T, NH])
                    link(dve.tensor_tensor(two(0), ps[:, OB, 0:T * NH].rearrange("p (t h) -> p t h", t=T), over_t(bcast[:, 640:656]), ALU.add))
                    sync()
                    dve.scalar_tensor_tensor(dts[:, 1, :], dts[:, 0, :], -1.0, dts[:, 0, :], ALU.mult, ALU.max).then_inc(dt_arg, 1)
                    dve.wait_ge(dt_log, lap(L, 1, 1))
                    link(dve.scalar_tensor_tensor(dts[:, 2, :], dts[:, 0, :], 0.0, dts[:, 3, :], ALU.max, ALU.add))
                    sync()
                    dve.scalar_tensor_tensor(two(4), two(2), -1.0, over_t(dts[:, 5, 0:NH]), ALU.mult, ALU.mult).then_inc(dt_done, 1)

                def turn_qk(j):
                    if j % 2:
                        dve.wait_ge(k_turned, lap(L, j // 2 + 1, 4))
                        dve.tensor_copy(kT[:, j - 1:j + 1, :], tiles(OB)).then_inc(k_copied, 1)

                def dscore(u):
                    qt = u % 2
                    nk = P * (1 + qt)
                    dve.wait_ge(d_score, lap(L, u + 1, 2 * DH))
                    if u >= 2:
                        dve.wait_ge(d_exp, lap(L, u - 1, 2 * DH))
                    o = sm[:, u % 2, 0:2 * nk].rearrange("p (m k) -> p m k", k=nk)
                    i = ps[:, S0:S0 + 2, (u % 2) * TOK:(u % 2) * TOK + nk]
                    m = cst("chunk_neg")[:, P * qt:P * qt + nk].unsqueeze(1).to_broadcast([P, 2, nk])
                    dve.scalar_tensor_tensor(o, i, SCALE, m, ALU.mult, ALU.add).then_inc(d_masked, 1)
                    peak(L, u, nk, 2 * DH, d_masked, d_peak)

                def dturn(u):
                    nk, at = P * (1 + u % 2), (u % 4) * 16
                    dve.wait_ge(d_exp, lap(L, u + 1, 2 * DH))
                    if u == 0:
                        dve.wait_ge(lam_ready, lap(L, 1, 1))
                    e0, e1 = (ex[:, u % 2, m * nk:(m + 1) * nk] for m in range(2))
                    link(dve.reciprocal(small[:, at + 4:at + 6], small[:, at + 2:at + 4]))
                    sync()
                    link(dve.tensor_scalar(e0, e0, small[:, at + 4:at + 5], None, ALU.mult))
                    link(dve.tensor_tensor(small[:, at + 6:at + 7], small[:, at + 5:at + 6], small[:, 165:166], ALU.mult))
                    sync()
                    dve.scalar_tensor_tensor(e0, e1, small[:, at + 6:at + 7], e0, ALU.mult, ALU.add).then_inc(d_w, 1)

                def dout(u):
                    h, qt, at = u // 2, u % 2, (u % 4) * 16
                    dve.wait_ge(d_sq, lap(L, u + 1, 2 * DH))
                    ask_root(L, dve.tensor_scalar(small[:, at + 8:at + 9], small[:, at + 7:at + 8], 1.0 / P, LN_EPS, ALU.mult, ALU.add))
                    dve.tensor_scalar(oA[:, qt, h * P:(h + 1) * P], ps[:, OB, (u % 4) * P:(u % 4 + 1) * P],
                                      small[:, at + 8:at + 9], None, ALU.mult).then_inc(d_norm, 1)

                def cb(g):
                    dve.wait_ge(cb_ready, lap(L, g + 1, 2))
                    dve.tensor_tensor(cbm[:, g, :], ps[:, S0 + g, 0:CAUS], cst("causal"), ALU.mult).then_inc(cb_masked, 1)

                def sdecay(u):
                    dve.wait_ge(seg_exp, lap(L, u + 1, NH))
                    if u == 0:
                        dve.wait_ge(cb_masked, lap(L, 2, 2))
                    if u >= 2:
                        dve.wait_ge(y_ready, lap(L, u - 1, NH))
                    g = u // (NH // 2)
                    for t, r in enumerate((slice(0, TOK), slice(TOK, CAUS))):
                        ins_ = dve.scalar_tensor_tensor(lmat[:, u % 2, r], ex[:, u % 2, r], dts[:, 2, t * NH + u:t * NH + u + 1],
                                                        cbm[:, g, r], ALU.mult, ALU.mult)
                    ins_.then_inc(l_ready, 1)

                def sout(u):
                    if u % 2:
                        p = u // 2
                        dve.wait_ge(y_ready, lap(L, u + 1, NH))
                        d = small[:, 176 + p:177 + p]
                        s = sm[:, p % 2, 0:TOK]
                        link(dve.scalar_tensor_tensor(s, xbc[:, p, :], d, ps[:, TB + p % 2, 0:TOK], ALU.mult, ALU.add))
                        sync()
                        dve.tensor_tensor(zT[:, p, :], s, zT[:, p, :], ALU.mult).then_inc(y_gated, 1)

                def snorm(g):
                    dve.wait_ge(y_sum, lap(L, g + 1, 2))
                    r = sm[:, g, 0:TOK]
                    ask_root(L, dve.tensor_scalar(r, ps[:, TB + g, 0:TOK], 1.0 / (4 * P), LN_EPS, ALU.mult, ALU.add))
                    for k in range(4 * g, 4 * g + 4):
                        w = cols[:, ROWS2["norm"] + k:ROWS2["norm"] + k + 1]
                        ins_ = dve.scalar_tensor_tensor(zT[:, k, :], zT[:, k, :], w, r, ALU.mult, ALU.mult)
                    ins_.then_inc(o_b, 1)

                def kscore(u):
                    z = sm[:, u % 2, 0:CAUS]
                    dve.wait_ge(s_score, lap(L, u + 1, NH))
                    if u >= 2:
                        dve.wait_ge(s_exp, lap(L, u - 1, NH))
                        dve.wait_ge(s_sum, lap(L, u - 1, NH))
                    dve.scalar_tensor_tensor(z, ps[:, S0 + u % 2, 0:CAUS], SCALE, cst("strict_neg"), ALU.mult, ALU.add).then_inc(s_masked, 1)
                    dve.wait_ge(s_masked, lap(L, u + 1, NH))
                    dve.scalar_tensor_tensor(lmat[:, u % 2, :], z, -1.0, z, ALU.mult, ALU.max).then_inc(s_abs, 1)

                def ksoft(u):
                    dve.wait_ge(s_log, lap(L, u + 1, NH))
                    b = lmat[:, u % 2, :]
                    dve.scalar_tensor_tensor(b, sm[:, u % 2, 0:CAUS], 0.0, b, ALU.max, ALU.add).then_inc(s_soft, 1)

                def ksum(u):
                    z = sm[:, u % 2, 0:CAUS]
                    dve.wait_ge(s_sum, lap(L, u + 1, NH))
                    dve.tensor_tensor(z, z, ps[:, TB, 0:CAUS], ALU.subtract).then_inc(s_arg, 1)

                attention = dict(turn_qk=turn_qk, dscore=dscore, dturn=dturn, dout=dout, cb=cb, sdecay=sdecay, sout=sout,
                                 snorm=snorm, kscore=kscore, ksoft=ksoft, ksum=ksum, drain=drain)
                ffn_mul(L, ffn1)
                turn_rows()
                layer_norm(0, ffn1["slot0"] + 3 * FFC, FFN_RES / ALPHA, ffn1["after"])
                for step in mixed:
                    if step[0] == "dt":
                        dt()
                    elif step[0] in attention:
                        attention[step[0]](step[1])
                layer_norm(1, out2[1].slot0 + 2, 1 / ALPHA, out2[1].after)
                ffn_mul(L, ffn2)
                layer_norm(2, ffn2["slot0"] + 3 * FFC, FFN_RES / ALPHA, list(plan.free))
                chain.leave()

        @block.gpsimd
        def _(pool):
            chain = Chain(pool, pool_chain)
            link, sync = chain.link, chain.sync
            rows1 = wide[:, 0:2, :].rearrange("p a (b n) -> p (a b) n", n=P)
            cw = ins["ffn_conv_w"][0].rearrange("j (a b) -> (j a) b", b=P)
            pool.dma_start(rows1[0:88, 0, :], cw[0:88, :]).then_inc(rows1_loaded, 16)
            pool.dma_start(rows1[0:44, 1, :], cw[88:132, :]).then_inc(rows1_loaded, 16)
            for name, key, n in (("mix_norm_g", "mix", 8), ("mem_norm_g", "mem", 8), ("ffn_norm_g", "ffn", 8), ("ffn_conv_b", "conv_b", 44)):
                pool.dma_start(rows1[ROWS1[key]:ROWS1[key] + n, 2, :], ins[name][0].rearrange("(a b) -> a b", b=P)).then_inc(rows1_loaded, 16)
            with nc.allow_non_contiguous_dma(reason="256 positions, one per partition"):
                for t in range(T):
                    pool.dma_start(pos[:, t:t + 1], ins["positions"][0, t * P:(t + 1) * P].unsqueeze(1)).then_inc(par1_loaded, 16)
            for i, name in enumerate(("moba_q_norm_g", "moba_k_norm_g", "dil_q_norm_g", "dil_k_norm_g", "mem_q_norm_g", "mem_k_norm_g")):
                pool.dma_start(bcast[:, 256 + i * HD:256 + (i + 1) * HD], ins[name][0:1, :].to_broadcast([P, HD])).then_inc(par1_loaded, 16)

            roots = [0]

            def root(L, a):
                roots[0] += 1
                pool.wait_ge(root_asked, lap(L, roots[0], ROOTS_LAP))
                n = a.shape[-1]
                pool.tensor_tensor(a, a, cst("minus_half").to_broadcast([P, n]), ALU.pow).then_inc(root_done, 1)

            pool.wait_ge(in_loaded, 4 * 16)
            for event in range(2):
                for t in range(T):
                    root(None, small[:, 64 + 2 * event + t:65 + 2 * event + t])
            for step in steps1:
                if step[0] == "drain" and step[1].name == "tok":
                    for t in range(T):
                        root(None, small[:, 84:84 + NORMED[step[1].index][1]])
            for t in range(T):
                root(None, small[:, 64 + 4 + t:65 + 4 + t])
            with pool.Fori(0, LAYERS) as L:
                chain.enter(L)

                def residual(k):
                    for t in range(T):
                        root(L, small[:, 98 + 4 * t:99 + 4 * t])
                    pool.wait_ge(gb_loaded, lap(L, 32 * (k + 1), 96))
                    for t in range(T):
                        pool.wait_ge(hat_ready, lap(L, 2 * (4 + k) + t + 1, 6))
                        link(pool.tensor_tensor(x[:, t, :], xhat[:, t, :], gb[:, 0, :], ALU.mult))
                        sync()
                        pool.tensor_tensor(x[:, t, :], x[:, t, :], gb[:, 1, :], ALU.add).then_inc(x_ready, 1)

                def sdecay(u):
                    if u == 0:
                        pool.wait_ge(dt_done, lap(L, 1, 1))
                        pool.wait_ge(xbc_done, lap(L, 6, 6))
                    if u >= 2:
                        pool.wait_ge(seg_ready, lap(L, u - 1, NH))
                    for n, (m, t) in enumerate(((after, 0), (after, 1), (ones, 1))):
                        ins_ = pool.tensor_tensor(seg_w[:, u % 2, n * P:(n + 1) * P], m,
                                                  dts[:, 4, t * NH + u:t * NH + u + 1].to_broadcast([P, P]), ALU.mult)
                    ins_.then_inc(seg_built, 1)

                residual(0)
                for step in mixed:
                    if step[0] == "sdecay":
                        sdecay(step[1])
                    elif step[0] == "dout":
                        at = (step[1] % 4) * 16
                        root(L, small[:, at + 8:at + 9])
                    elif step[0] == "snorm":
                        root(L, sm[:, step[1], 0:TOK])
                residual(1)
                residual(2)
                chain.leave()
            pool.wait_ge(x_ready, 6 * LAYERS)
            pool.dma_start(out[0].rearrange("(t p) n -> p t n", p=P), x[:, :, :]).then_inc(out_stored, 16)
            pool.wait_ge(out_stored, 16)

    return nc


INPUTS = ["x", "mem", "positions", "mix_norm_g", "mem_norm_g", "w_in", "moba_q_norm_g", "moba_k_norm_g", "dil_q_norm_g",
          "dil_k_norm_g", "mem_q_norm_g", "mem_k_norm_g", "w_mem_kv", "w_branch_moba", "w_branch_dil", "w_branch_mem", "w_out",
          "ffn_norm_g", "w_ffn_up", "ffn_conv_w", "ffn_conv_b", "w_ffn_down", "ffn1_w_in_2", "ffn1_w_out_2", "ln1_g_2",
          "ln1_b_2", "w_mix_in_2", "gate_bias_2", "diff_lambda_2", "diff_subln_g_2", "ssm_conv_w_2", "ssm_conv_b_2",
          "ssm_dt_bias_2", "ssm_A_log_2", "ssm_D_2", "ssm_norm_g_2", "w_branch_2", "w_mix_out_2", "ln2_g_2", "ln2_b_2",
          "ffn2_w_in_2", "ffn2_w_out_2", "ln3_g_2", "ln3_b_2"]


def kernel(**inputs):
    import concourse.bacc as bacc
    from concourse.bass_utils import run_bass_kernel_spmd

    nc = bacc.Bacc("TRN2", target_bir_lowering=False, num_devices=1)
    arrays, aps = {}, {}
    for name in INPUTS:
        a = np.ascontiguousarray(inputs[name])
        arrays["in_" + name] = a
        aps[name] = nc.dram_tensor("in_" + name, a.shape, mybir.dt.from_np(a.dtype), kind="ExternalInput").ap()
    arrays["const_table"] = constants()
    aps["const"] = nc.dram_tensor("const_table", (P, CONST_ALL), F32, kind="ExternalInput").ap()
    out = nc.dram_tensor("out", (1, TOK, D), F32, kind="ExternalOutput").ap()
    program(nc, aps, out)
    return run_bass_kernel_spmd(nc, [arrays], core_ids=[0]).results[0]["out"]
```

```python
from contextlib import ExitStack

import numpy as np

import concourse.bass as bass
from concourse import mybir

ALU = mybir.AluOpType
ACT = mybir.ActivationFunctionType
F32 = mybir.dt.float32
F32R = mybir.dt.float32r
I32 = mybir.dt.int32
AX_X = mybir.AxisListType.X

P = 128
D = 1024
TOK = 256
T = TOK // P
KD = D // P
FF = 2816
KF = FF // P
FFC = KF // 2
HD = 64
BANK = 512
LAYERS = 2
SLOTS = 4
HIGHS = 2
HALVES = 2
SLOT = 2048
RATE1, RATE2 = 1.0, 0.875
ALPHA = (2 * LAYERS) ** 0.25
FFN_RES = 0.5
RMS_EPS = 1e-6
LN_EPS = 1e-5
SCALE = HD ** -0.5
NEG = -1e30

QKV1 = 2560
GATE1 = QKV1
TOKW = 3072
NORMED = [(0, 6, 0, True), (384, 6, 1, True), (1152, 6, 2, True), (1536, 6, 3, True),
          (2304, 4, 4, False), (2560, 4, 5, False)]
Q_COL = [0, 128, 256, 1152, 1280, 1408, 2304, 2432]
K_COL = [384, 512, 640, 1536, 1664, 1792, 2560, 2688]
V_COL = [768, 896, 1024, 1920, 2048, 2176, 2816, 2944]
PAIRS = 8
BRANCH_TILES = (3, 3, 2)

MIX = dict(qa=0, ka=1024, va=2048, zb=3072, xbc=4096, dt=5632, qc=5648, kc=6672, vc=7696, gate=8720)
NH = 16
DH = 8
N_XBC = 12
CAUS = 384

CONST = {}
_at = 0
for _name, _n in (("ident", 128), ("ones", 128), ("after", 128), ("from_on", 128),
                  ("strict_neg", CAUS), ("causal", CAUS), ("chunk_neg", CAUS), ("cos", T * 16), ("sin", T * 16),
                  ("freq", 32), ("lam", 4), ("minus_half", 1), ("ln_eps", 1), ("moba_neg", CAUS), ("dil_add", CAUS)):
    CONST[_name] = (_at, _at + _n)
    _at += _n
CONST_ALL = _at
CONST_W = CONST["moba_neg"][0]

ROWS1 = dict(mix=0, mem=8, ffn=16, conv_b=24)
N_ROWS1 = 68
N_CONV1 = 3 * 2 * KF
ROWS2 = dict(ln_g=(0, 16, 32), ln_b=(8, 24, 40), gate_b=48, norm=72, subln=80)
N_ROWS2 = 81
N_CONV2 = 5 * N_XBC


def constants():
    i = np.arange(P)[:, None]
    j = np.arange(P)[None, :]
    t = np.arange(TOK)[None, :]
    c = np.zeros((P, CONST_ALL), np.float32)

    def put(name, a):
        c[:, CONST[name][0]:CONST[name][1]] = a

    def queries(rule):
        return np.concatenate([rule(i, j), rule(i + P, t)], axis=1)

    def keys(rule):
        return np.concatenate([rule(i, t), rule(i, j)], axis=1)

    put("ident", i == j)
    put("ones", 1.0)
    put("after", i > j)
    put("from_on", i >= j)
    put("strict_neg", keys(lambda k, q: np.where(k < q, 0.0, NEG)))
    put("causal", keys(lambda k, q: k <= q))
    put("chunk_neg", queries(lambda q, k: np.where(k // HD <= q // HD, 0.0, NEG)))
    put("moba_neg", queries(lambda q, k: np.where(k <= q, 0.0, NEG)))

    def dilated(q, k):
        n = (k <= q) * ((q - k <= 128) * 1 + ((q - k) % 4 == 0) * 1 + ((q - k) % 16 == 0) * 1)
        return np.where(n > 0, np.log(np.maximum(n, 1)), NEG)

    put("dil_add", queries(dilated))
    half = 8
    inv = (np.float32(500000.0) ** (-np.arange(half, dtype=np.float32) * np.float32(2.0) / np.float32(16))).astype(np.float32)
    ang = (np.arange(TOK, dtype=np.float32)[:, None] * inv[None, :]).astype(np.float32)
    for name, f in (("cos", np.cos), ("sin", np.sin)):
        v = f(ang).astype(np.float32).reshape(T, P, half).transpose(1, 0, 2)
        first = -v if name == "sin" else v
        put(name, np.concatenate([first, v], axis=2).reshape(P, T * 16))
    put("freq", np.float32(10000.0) ** (-np.arange(32, dtype=np.float32) / np.float32(32)))
    lam = [0.8 - 0.6 * np.exp(-0.3 * layer) for layer in range(LAYERS)]
    put("minus_half", -0.5)
    put("ln_eps", LN_EPS)
    put("lam", np.array([[lam[0], 1 - lam[0], lam[1], 1 - lam[1]]]))
    return c



class Chunk:

    def __init__(self, name, index, mode, srcs, act, pair, evacs=1):
        self.name, self.index, self.mode, self.srcs, self.act = name, index, mode, srcs, act
        self.pair, self.evacs = pair, evacs


class Plan:

    def __init__(self):
        self.slot = 0
        self.hidden = 0
        self.free = [0, 0, 0, 0]

    def chunk(self, c):
        c.slot0 = self.slot
        self.slot += 2
        c.need = {b: self.free[b] for b in (2 * c.pair, 2 * c.pair + 1)}
        for b in c.need:
            self.free[b] += c.evacs
        return c

    def ffn(self, f):
        f["slot0"], f["free0"], f["h0"] = self.slot, list(self.free), self.hidden
        self.hidden += FFC
        self.slot += 3 * FFC
        f["ahead"] = 1 if f["index"] == 0 else 0
        self.free = [n + FFC // 2 + (1 if b < 2 else 0) + 1 for b, n in enumerate(self.free)]
        return f


def beats_of(n, stages, lags):
    return [[(s, i - lag) for s, lag in zip(stages, lags) if 0 <= i - lag < n]
            for i in range(n + max(lags))]


def woven(chunks, beats, first, rate):
    steps, done, halves, prev = [], 0, 0, None
    for n, c in enumerate(chunks):
        for part in range(2 * HALVES):
            steps.append(("half", c, part // HALVES, part % HALVES))
            if part == 0 and prev is not None:
                steps.append(("drain", prev))
            if n >= first:
                halves += 1
                while done < len(beats) and done < rate * halves:
                    steps += beats[done]
                    done += 1
        prev = c
    return steps + [("drain", prev)], beats[done:]


def plan_block1(plan):
    chunks = [Chunk("tok", n, "A", [("w_in", h, n * BANK) for h in range(2)], "xT", n % 2) for n in range(5)]
    chunks += [Chunk("tok", 5, "A", [("w_mem_kv", h, 0) for h in range(2)], "memT", 1)]
    chunks += [Chunk("gate1", n, "B", [("w_in", None, GATE1 + n * BANK + h * TOK) for h in range(2)], "xT", n % 2)
               for n in range(6)]
    head = [plan.chunk(c) for c in chunks]
    beats = [[("pair1", p), ("pair1", p + 1)] for p in range(0, PAIRS, 2)]
    beats += beats_of(2 * PAIRS, ("out1", "turn1", "score1"), (3, 2, 0))
    return head, beats


def plan_layer(plan):
    def a(name, n, pair, evacs=1, w="w_mix_in_2", act="xT"):
        return Chunk(name, n, "A", [(w, h, MIX.get(name, 0) + n * BANK) for h in range(2)], act, pair, evacs)

    def b(name, n, pair, w="w_mix_in_2", act="xT"):
        return Chunk(name, n, "B", [(w, None, MIX.get(name, 0) + n * BANK + h * TOK) for h in range(2)], act, pair)

    jobs = [(a, "qa", n, 2) for n in range(2)] + [(a, "ka", n, 2) for n in range(2)] + [(a, "va", n, 1) for n in range(2)]
    jobs += [(b, name, n) for name, count in (("xbc", 3), ("qc", 2), ("kc", 2), ("zb", 2)) for n in range(count)]
    jobs += [(a, "vc", n, 1) for n in range(2)] + [(b, "gate", n) for n in range(6)]
    ffn1 = plan.ffn({"index": 0})
    ffn1["after"] = list(plan.free)
    mix = [plan.chunk(j[0](j[1], j[2], i % 2, *j[3:])) for i, j in enumerate(jobs)]
    for r, act in enumerate(("oAT", "oBT", "oCT")):
        for n in range(2):
            c = b("branch", n, (len(mix)) % 2, w=("w_branch_2", r), act=act)
            c.r = r
            mix.append(plan.chunk(c))
    out = [plan.chunk(a("out", n, n, w="w_mix_out_2", act="mT")) for n in range(2)]
    out[1].after = list(plan.free)
    ffn2 = plan.ffn({"index": 1})
    return ffn1, mix, out, ffn2


def with_splits(steps, end):
    all_ = []
    for step in steps:
        all_.append(step)
        if step[0] == "half":
            s = step[1].slot0 + step[2] + HIGHS
            if s < end:
                all_.append(("split", s, step[3]))
    return all_


def mixer_steps(mix):
    beats = [[("turn_qk", 2 * j), ("turn_qk", 2 * j + 1)] for j in range(4)]
    beats += beats_of(2 * DH, ("dout", "dturn", "dscore"), (3, 2, 0))
    beats += [[("dnorm", 0)]]
    beats += [[("turn_oa", 0), ("turn_oa", 1)], [("turn_oa", 2), ("turn_oa", 3)]]
    beats += [[("turn_xs", 0), ("turn_xs", 1)], [("turn_xs", 2), ("turn_xs", 3)], [("cb", 0), ("cb", 1)]]
    beats += beats_of(NH, ("sout", "sdecay"), (2, 0))
    beats += [[("snorm", 0), ("snorm", 1)]]
    tail = beats_of(NH, ("osplit", "kout", "ksum", "ksoft", "kscore"), (4, 3, 2, 1, 0))
    tail[1].append(("bsplit", 0))
    tail[1].append(("bsplit", 1))
    beats += tail
    steps, rest = woven(mix, beats, 6, RATE2)
    assert not rest
    steps.insert(steps.index(("half", mix[6], 0, 0)), ("dt",))

    def before(a, b):
        assert steps.index(a) < steps.index(b), (a, b)

    z = [c for c in mix if c.name == "zb"]
    branch = [c for c in mix if c.name == "branch"]
    before(("dout", 2 * DH - 1), ("drain", z[0]))
    before(("drain", z[0]), ("sout", 1))
    before(("drain", z[1]), ("sout", NH // 2 + 1))
    before(("sout", NH - 1), ("drain", branch[0]))
    for b, last in ((0, ("turn_oa", 3)), (2, ("bsplit", 1)), (4, ("osplit", NH - 1))):
        before(last, ("half", branch[b], 0, 0))
    return steps


def program(nc, ins, out):
    plan = Plan()
    head1, beats1 = plan_block1(plan)
    branch1_slot0 = plan.slot
    plan.slot += 4
    out1 = [plan.chunk(Chunk("out1", n, "A", [("w_out", h, n * BANK) for h in range(2)], "mT", n)) for n in range(2)]
    ffn0 = plan.ffn({"index": None})
    start = (plan.slot, list(plan.free))
    ffn1, mix, out2, ffn2 = plan_layer(plan)
    SLOT_LAP = plan.slot - start[0]
    FREE_LAP = [n - m for n, m in zip(plan.free, start[1])]
    assert SLOT_LAP % SLOTS == 0
    steps1, rest1 = woven(head1, beats1, 6, RATE1)
    steps1 += [step for beat in rest1 for step in beat]
    steps1 = with_splits(steps1, out1[0].slot0)
    mixed = with_splits(mixer_steps(mix), out2[0].slot0 + 2)

    ctx = ExitStack()
    with ctx:
        def sb(name, shape, dt=F32):
            return ctx.enter_context(nc.sbuf_tensor(name, shape, dt))

        def sem(name):
            return ctx.enter_context(nc.semaphore(name))

        def both(name, shape):
            with nc.sbuf_tensor(name, shape, F32) as plain:
                pass
            return plain, sb(name + "_r", shape, F32R)

        ring, ring_lo = both("ring", [P, SLOTS, SLOT])
        ring_hi = sb("ring_hi", [P, HIGHS, SLOT], F32R)
        const = sb("const", [P, CONST_W])
        x = sb("x", [P, T, D])
        xT_hi = sb("xT_hi", [P, KD, TOK], F32R)
        xT, xT_lo = both("xT", [P, KD, TOK])
        wide, wide_r = both("wide", [P, 24, TOK])
        tok, tok_r = both("tok", [P, 3 * T * D])
        qT, qT_r = both("qT", [P, KD, TOK])
        kT, kT_r = both("kT", [P, KD, TOK])
        xbc, xbc_r = both("xbc", [P, N_XBC, TOK])
        qcT, qcT_r = both("qcT", [P, KD, TOK])
        kcT, kcT_r = both("kcT", [P, KD, TOK])
        vc_, vc_r = both("vc", [P, T * D])

        def rows_of(a):
            return a.rearrange("p (t n) -> p t n", t=T)

        def feats_of(a):
            return a.rearrange("p (k n) -> p k n", n=TOK)

        vc = rows_of(vc_[:, :])
        xhat = vc
        gb = qT[:, :, :].rearrange("p a n -> p (a n)").rearrange("p (t n) -> p t n", t=2)
        tok1 = tok[:, :].rearrange("p (t n) -> p t n", t=T)
        qa, ka, va = (rows_of(tok[:, i * T * D:(i + 1) * T * D]) for i in range(3))
        oA, xs = qa, ka
        mT, zT = (feats_of(tok[:, i * T * D:(i + 1) * T * D]) for i in (1, 2))
        mT_lo, zT_lo = (feats_of(tok_r[:, i * T * D:(i + 1) * T * D]) for i in (1, 2))
        h2, h2_lo, h2_hi = feats_of(tok[:, 0:KF * TOK]), feats_of(tok_r[:, 0:KF * TOK]), wide_r[:, 0:KF, :]
        o1T = feats_of(vc_[:, :])
        memT = wide[:, 16:24, :]
        acts = {"xT": (xT_hi, xT_lo), "memT": (xbc_r[:, 0:KD, :], wide_r[:, 16:24, :]), "o1T": (xbc_r[:, 0:KD, :], feats_of(vc_r[:, :])),
                "oAT": (kT_r, qT_r), "oBT": (xbc_r[:, 0:KD, :], zT_lo), "oCT": (kcT_r, qcT_r), "mT": (xT_hi, mT_lo)}
        const1 = xbc[:, KD:KD + 3, :].rearrange("p a n -> p (a n)")
        gains1 = qcT[:, 4:6, :].rearrange("p a n -> p (a n)")[:, 0:6 * HD]
        act_s = sb("act_s", [P, 2, BANK])
        conv_s = sb("conv_s", [P, 2, BANK])
        sm = sb("sm", [P, 2, BANK])
        ex = sb("ex", [P, 2, BANK])
        wt = sb("wt", [P, 2, BANK])
        lmat, cbm = (tok[:, i * 2 * CAUS:(i + 1) * 2 * CAUS].rearrange("p (a n) -> p a n", a=2) for i in range(2))
        seg_w = act_s[:, :, 0:3 * P]
        small = sb("small", [P, 256])
        cols = sb("cols", [P, 256])
        rows = sb("rows", [P, 2, P])
        bcast = sb("bcast", [P, 4 * HD + 3 * NH])
        dtw = sb("dtw", [P, KD, NH])
        dts = sb("dts", [P, 6, T * NH])
        conv1 = sb("conv1", [P, N_CONV1 + N_ROWS1])
        stats = sb("stats", [P, T, 12])
        act_j = sb("act_j", [P, P])
        pos = sb("pos", [P, T], I32)
        ps = ctx.enter_context(nc.psum_tensor("ps", [P, 8, BANK], F32))
        S0, S1, TB, OB = 4, 5, 6, 7

        def cst(name):
            a, b = CONST[name]
            return const[:, a:b] if b <= CONST_W else const1[:, a - CONST_W:b - CONST_W]

        ident, ones, after, from_on = (cst(n) for n in ("ident", "ones", "after", "from_on"))
        upto = cst("causal")[:, 0:TOK]

        w_loaded = [sem(f"w_loaded{i}") for i in range(SLOTS)]
        drained = [sem(f"drained{b}") for b in range(4)]
        multiplied, in_loaded, par1_loaded, par_loaded, rows1_loaded = (sem(n) for n in ("multiplied", "in_loaded", "par1_loaded", "par_loaded", "rows1_loaded"))
        rows_loaded, gb_loaded, rows1_turned, rows_turned, cols_ready = (sem(n) for n in ("rows_loaded", "gb_loaded", "rows1_turned", "rows_turned", "cols_ready"))
        sq_ready, stat_ready, hat_ready, hat_turned, xT_act = (sem(n) for n in ("sq_ready", "stat_ready", "hat_ready", "hat_turned", "xT_act"))
        xT_dve, x_ready, x_added, conv_begun, conv_tap = (sem(n) for n in ("xT_dve", "x_ready", "x_added", "conv_begun", "conv_tap"))
        act_ready, h_ready, dve_chain, act_chain, pool_chain = (sem(n) for n in ("act_ready", "h_ready", "dve_chain", "act_chain", "pool_chain"))
        angle_ready, sin_ready, norm1_done, pair1_turned, pair1_copied = (sem(n) for n in ("angle_ready", "sin_ready", "norm1_done", "pair1_turned", "pair1_copied"))
        score1_ready, masked1, peak1, exp1, prob1 = (sem(n) for n in ("score1_ready", "masked1", "peak1", "exp1", "prob1"))
        prob1_turned, prob1_copied, out1_ready, out1_copied, branch1_free = (sem(n) for n in ("prob1_turned", "prob1_copied", "out1_ready", "out1_copied", "branch1_free"))
        mixed1, q_turned, q_copied, k_turned, k_copied = (sem(n) for n in ("mixed1", "q_turned", "q_copied", "k_turned", "k_copied"))
        d_score, d_masked, d_peak, d_exp, d_w = (sem(n) for n in ("d_score", "d_masked", "d_peak", "d_exp", "d_w"))
        d_turned, d_copied, d_out, d_sq, d_norm = (sem(n) for n in ("d_turned", "d_copied", "d_out", "d_sq", "d_norm"))
        oa_turned, oa_copied, lam_arg, lam_exp, lam_ready = (sem(n) for n in ("oa_turned", "oa_copied", "lam_arg", "lam_exp", "lam_ready"))
        dt_ready, dt_arg, dt_log, dt_done, z_exp = (sem(n) for n in ("dt_ready", "dt_arg", "dt_log", "dt_done", "z_exp"))
        xbc_begun, xbc_exp, xbc_done, xs_turned, xs_copied = (sem(n) for n in ("xbc_begun", "xbc_exp", "xbc_done", "xs_turned", "xs_copied"))
        cb_ready, cb_masked, seg_built, seg_ready, seg_exp = (sem(n) for n in ("cb_ready", "cb_masked", "seg_built", "seg_ready", "seg_exp"))
        l_ready, y_ready, y_gated, y_sq, y_sum = (sem(n) for n in ("l_ready", "y_ready", "y_gated", "y_sq", "y_sum"))
        o_b, s_score, s_masked, s_abs, s_log = (sem(n) for n in ("o_b", "s_score", "s_masked", "s_abs", "s_log"))
        s_soft, s_sum, s_arg, s_exp, s_out = (sem(n) for n in ("s_soft", "s_sum", "s_arg", "s_exp", "s_out"))
        s_copied, mixed_sem, out_stored = (sem(n) for n in ("s_copied", "mixed_sem", "out_stored"))
        w_hi, w_lo, h_hi, h_lo, gate_ready, first_used = (sem(n) for n in ("w_hi", "w_lo", "h_hi", "h_lo", "gate_ready", "first_used"))
        o1_split, m_hi, m_split, y_root = (sem(n) for n in ("o1_split", "m_hi", "m_split", "y_root"))
        oa_split, ob_hi, ob_split, oc_split = (sem(n) for n in ("oa_split", "ob_hi", "ob_split", "oc_split"))
        root_asked, root_done = sem("root_asked"), sem("root_done")
        ROOTS_LAP = 3 * T + 1

        def lap(L, k, per):
            return k if L is None else L * per + k

        def x_count(L, k):
            return lap(L, k + 1, 6)

        CHAIN_LAP = 2000

        class Chain:

            def __init__(self, eng, s):
                self.eng, self.sem, self.n, self.L = eng, s, 0, None

            def link(self, ins):
                self.n += 1
                ins.then_inc(self.sem, 1)

            def sync(self):
                self.eng.wait_ge(self.sem, lap(self.L, self.n, CHAIN_LAP))

            def enter(self, L):
                self.L, self.n0 = L, self.n

            def leave(self):
                self.eng.sem_inc(self.sem, CHAIN_LAP - (self.n - self.n0))

        block = ctx.enter_context(nc.Block())

        @block.sync
        def _(sp):
            sp.dma_start(const[:, :], ins["const"][:, 0:CONST_W]).then_inc(in_loaded, 16)
            sp.dma_start(const1, ins["const"][:, CONST_W:CONST_ALL]).then_inc(in_loaded, 16)
            sp.dma_start(x[:, :, :], ins["x"][0].rearrange("(t p) n -> p t n", p=P)).then_inc(in_loaded, 16)
            sp.dma_start(gb[:, :, :], ins["mem"][0].rearrange("(t p) n -> p t n", p=P)).then_inc(in_loaded, 16)

            def slot_wait(L, s, more=0):
                if L is not None or s >= SLOTS:
                    sp.wait_ge(multiplied, lap(L, s - SLOTS + 1, SLOT_LAP) + more)

            def matrix(L, w):
                if isinstance(w, tuple):
                    return ins[w[0]][bass.ds(L, 1), w[1]].rearrange("a k n -> (a k) n")
                if L is None:
                    return ins[w][0]
                return ins[w][bass.ds(L, 1)].rearrange("a k n -> (a k) n")

            def load(L, s, src):
                w, half, c0 = src
                m = matrix(L, w)
                if s != mix[0].slot0:
                    slot_wait(L, s)
                if half is None:
                    a = m[:, c0:c0 + TOK].rearrange("(k p) n -> p k n", p=P)
                    d = ring[:, s % SLOTS, :].rearrange("p (k n) -> p k n", n=TOK)
                else:
                    a = m[half * 4 * P:(half + 1) * 4 * P, c0:c0 + BANK].rearrange("(k p) n -> p k n", p=P)
                    d = ring[:, s % SLOTS, :].rearrange("p (k n) -> p k n", n=BANK)
                sp.dma_start(d, a).then_inc(w_loaded[s % SLOTS], 16)

            def chunk_loads(L, chunks):
                for c in chunks:
                    for h in range(2):
                        load(L, c.slot0 + h, c.srcs[h])

            def ffn_loads(L, f, up, down, between=None):
                s0 = f["slot0"]
                wu, wd = matrix(L, up), matrix(L, down)

                def up_loads(it, js):
                    for j in js:
                        if len(js) == 1:
                            slot_wait(L, s0 + 2 * j + 1, it * 4)
                        for side in range(2):
                            s = s0 + 2 * j + side
                            if len(js) > 1:
                                slot_wait(L, s, it * 4)
                            a = wu[:, bass.ds(it * BANK + (j * TOK + side * FF), TOK)].rearrange("(k p) n -> p k n", p=P)
                            sp.dma_start(ring[:, s % SLOTS, :].rearrange("p (k n) -> p k n", n=TOK), a)\
                                .then_inc(w_loaded[s % SLOTS], 16)

                with sp.Fori(0, FFC // 2) as it:
                    up_loads(it, range(2))
                up_loads(FFC // 2, range(1))
                if between:
                    between()
                for i in range(FFC):
                    s = s0 + 2 * FFC + i
                    slot_wait(L, s + (i == FFC - 1))
                    a = wd[i * 2 * P:(i + 1) * 2 * P, :].rearrange("(k p) n -> p k n", p=P)
                    sp.dma_start(ring[:, s % SLOTS, :].rearrange("p (k n) -> p k n", n=D), a)\
                        .then_inc(w_loaded[s % SLOTS], 16)

            chunk_loads(None, head1)
            for j in range(4):
                s = branch1_slot0 + j
                slot_wait(None, s)
                d = ring[:, s % SLOTS, :].rearrange("p (k n) -> p k n", n=TOK)
                k0 = 0
                for w, n in zip(("w_branch_moba", "w_branch_dil", "w_branch_mem"), BRANCH_TILES):
                    sp.dma_start(d[:, k0:k0 + n, :], ins[w][0][:, j * TOK:(j + 1) * TOK].rearrange("(k p) n -> p k n", p=P))\
                        .then_inc(w_loaded[s % SLOTS], 16)
                    k0 += n
            chunk_loads(None, out1)
            ffn_loads(None, ffn0, "w_ffn_up", "w_ffn_down")
            with sp.Fori(0, LAYERS) as L:
                def row(name):
                    return ins[name][bass.ds(L, 1)].rearrange("l (a b) -> (l a) b", b=P)

                sp.wait_ge(cols_ready, lap(L, 1, 1))
                for k in range(3):
                    for s, at in (("g", ROWS2["ln_g"][k]), ("b", ROWS2["ln_b"][k])):
                        sp.dma_start(rows[at:at + 8, 0, :], row(f"ln{k + 1}_{s}_2")).then_inc(rows_loaded, 16)
                at = ROWS2["gate_b"]
                sp.dma_start(rows[at:at + 24, 0, :], ins["gate_bias_2"][bass.ds(L, 1)].rearrange("l r (a b) -> (l r a) b", b=P)).then_inc(rows_loaded, 16)
                at = ROWS2["norm"]
                sp.dma_start(rows[at:at + 8, 0, :], row("ssm_norm_g_2")).then_inc(rows_loaded, 16)
                at = ROWS2["subln"]
                sp.dma_start(rows[at:at + 1, 0, :], ins["diff_subln_g_2"][bass.ds(L, 1)]).then_inc(rows_loaded, 16)
                sp.dma_start(rows[0:4 * N_XBC, 1, :], ins["ssm_conv_w_2"][bass.ds(L, 1)].rearrange("l j (a b) -> (l j a) b", b=P)).then_inc(rows_loaded, 16)
                sp.dma_start(rows[4 * N_XBC:5 * N_XBC, 1, :], row("ssm_conv_b_2")).then_inc(rows_loaded, 16)
                sp.wait_ge(x_ready, x_count(L, 0))
                sp.dma_start(bcast[:, 0:256], ins["diff_lambda_2"][bass.ds(L, 1)].rearrange("l a d -> l (a d)").to_broadcast([P, 256])).then_inc(par_loaded, 16)
                sp.dma_start(bcast[:, 256:272], ins["ssm_dt_bias_2"][bass.ds(L, 1)].to_broadcast([P, NH])).then_inc(par_loaded, 16)
                sp.dma_start(bcast[:, 272:288], ins["ssm_A_log_2"][bass.ds(L, 1)].to_broadcast([P, NH])).then_inc(par_loaded, 16)
                sp.dma_start(bcast[:, 288:304], ins["ssm_D_2"][bass.ds(L, 1)].to_broadcast([P, NH])).then_inc(par_loaded, 16)
                sp.dma_start(dtw[:, :, :], ins["w_mix_in_2"][bass.ds(L, 1), :, MIX["dt"]:MIX["dt"] + NH].rearrange("l (k p) n -> p (l k) n", p=P))\
                    .then_inc(par_loaded, 16)

                def load_gb(k):
                    sp.wait_ge(x_ready, x_count(L, 2 * k))
                    for i, side in enumerate("gb"):
                        sp.dma_start(gb[:, i, :], ins[f"ln{k + 1}_{side}_2"][bass.ds(L, 1)].to_broadcast([P, D])).then_inc(gb_loaded, 16)

                ffn_loads(L, ffn1, "ffn1_w_in_2", "ffn1_w_out_2", lambda: load_gb(0))
                second = 1 + max(n for n, c in enumerate(mix) if c.name == "branch" and c.r == 1)
                chunk_loads(L, mix[:second])
                load_gb(1)
                chunk_loads(L, mix[second:] + out2)
                ffn_loads(L, ffn2, "ffn2_w_in_2", "ffn2_w_out_2", lambda: load_gb(2))

        def bank(b):
            return ps[:, b, :]

        def tiles(b):
            return ps[:, b, :].rearrange("p (f n) -> p f n", n=TOK)

        def wait_drained(eng, L, c):
            for b, n in c.need.items():
                eng.wait_ge(drained[b], lap(L, n + c.evacs, FREE_LAP[b]))

        def wait_products(eng, L, c, more=0):
            eng.wait_ge(multiplied, lap(L, c.slot0 + 2, SLOT_LAP) + more)

        by_rows = {c.slot0 + h for c in head1 + out1 + mix + out2 if c.mode == "A" for h in range(2)}
        by_rows |= {f["slot0"] + 2 * FFC + i for f in (ffn0, ffn1, ffn2) for i in range(FFC)}

        def half_of(place, s, q):
            if s in by_rows:
                return place[:, q * SLOT // HALVES:(q + 1) * SLOT // HALVES]
            return place.rearrange("p (k n) -> p k n", n=TOK)[:, :, q * P:(q + 1) * P]

        def wait_loaded(eng, L, s, more=0):
            extra = 16 * (len(BRANCH_TILES) - 1) if s >= branch1_slot0 else 0
            eng.wait_ge(w_loaded[s % SLOTS], lap(L, 16 * (s // SLOTS + 1) + extra, 16 * SLOT_LAP // SLOTS) + more)

        @block.tensor
        def _(pe):
            def wait_block(L, s, q, it=0):
                pe.wait_ge(w_lo, lap(L, HALVES * s + q + 1, HALVES * SLOT_LAP) + it * (HALVES * SLOTS))

            def used(mm, q):
                mm.then_inc(multiplied if q else first_used, 1)

            def block(s, n):
                return [a.rearrange("p (k n) -> p k n", n=n) for a in (ring_hi[:, s % HIGHS, :], ring_lo[:, s % SLOTS, :])]

            def product(out_, stat, mov, first, last):
                pe.matmul(out_, stat[0], mov[0], start=first, stop=False)
                pe.matmul(out_, stat[0], mov[1], start=False, stop=False)
                return pe.matmul(out_, stat[1], mov[0], start=False, stop=last)

            def wait_xT(L, event):
                pe.wait_ge(xT_act, lap(L, 2 * event, 6))
                pe.wait_ge(xT_dve, lap(L, 2 * event, 6))

            def half(L, c, h, q):
                act = acts[c.act]
                if h == 0 and q == 0:
                    for b, n in c.need.items():
                        if n:
                            pe.wait_ge(drained[b], lap(L, n, FREE_LAP[b]))
                s = c.slot0 + h
                wait_block(L, s, q)
                if c.mode == "A":
                    w = block(s, BANK)
                    for t in range(T):
                        for k in (2 * q, 2 * q + 1):
                            mm = product(bank(2 * c.pair + t), [a[:, 4 * h + k, t * P:(t + 1) * P] for a in act], [v[:, k, :] for v in w],
                                         h == 0 and k == 0, h == 1 and k == 3)
                else:
                    w = block(s, TOK)
                    for k in range(KD):
                        mm = product(tiles(2 * c.pair + h)[:, q, :], [v[:, k, q * P:(q + 1) * P] for v in w], [a[:, k, :] for a in act],
                                     k == 0, k == KD - 1)
                used(mm, q)

            def ffn(L, f, event, before_down=None):
                s0 = f["slot0"]

                def up(it, js):
                    for j in js:
                        for side in range(2):
                            b = 2 * j + side
                            s = s0 + b
                            if side == 0:
                                wait_xT(L, event)
                            pe.wait_ge(drained[b], lap(L, f["free0"][b], FREE_LAP[b]) + it)
                            w = block(s, TOK)
                            for q in range(HALVES):
                                wait_block(L, s, q, it)
                                for k in range(KD):
                                    mm = product(tiles(b)[:, q, :], [v[:, k, q * P:(q + 1) * P] for v in w],
                                                 [a[:, k, :] for a in acts["xT"]], k == 0, k == KD - 1)
                                used(mm, q)

                with pe.Fori(0, FFC // 2) as it:
                    up(it, range(2))
                up(FFC // 2, range(1))
                if before_down:
                    before_down()
                for b in range(4):
                    pe.wait_ge(drained[b], lap(L, f["free0"][b] + FFC // 2 + (b < 2), FREE_LAP[b]))
                pe.wait_ge(h_lo, lap(L, f["h0"] + FFC, 2 * FFC))
                for i in range(FFC):
                    s = s0 + 2 * FFC + i
                    w = block(s, D)
                    for k in range(HALVES):
                        wait_block(L, s, k)
                        for t in range(T):
                            for n in range(2):
                                mm = product(bank(2 * n + t), [a[:, 2 * i + k, t * P:(t + 1) * P] for a in (h2_hi, h2_lo)],
                                             [v[:, k, n * BANK:(n + 1) * BANK] for v in w],
                                             i == 0 and k == 0, i == FFC - 1 and k == 1)
                        used(mm, k)

            def norm(L, event, src):
                for t in range(T):
                    pe.wait_ge(hat_ready, lap(L, 2 * event + t + 1, 6))
                    for g in range(2):
                        for k in range(4):
                            tr = pe.transpose(ps[:, 4 + 2 * t + g, k * P:(k + 1) * P],
                                              src[:, t, (4 * g + k) * P:(4 * g + k + 1) * P], ident)
                        tr.then_inc(hat_turned, 1)

            pe.wait_ge(in_loaded, 4 * 16)
            pe.wait_ge(rows1_loaded, 6 * 16)
            rows1 = wide[:, 0:2, :].rearrange("p a (b n) -> p (a b) n", n=P)
            pe.transpose(bank(4)[:, 0:88], rows1[0:88, 0, :], ident[0:88, 0:88])
            pe.transpose(bank(4)[:, 88:132], rows1[0:44, 1, :], ident[0:44, 0:44])
            pe.transpose(bank(4)[:, 132:132 + N_ROWS1], rows1[0:N_ROWS1, 2, :], ident[0:N_ROWS1, 0:N_ROWS1])\
                .then_inc(rows1_turned, 1)
            pe.wait_ge(cols_ready, 1)
            norm(None, 0, xhat)
            wait_xT(None, 1)
            norm(None, 1, xhat)

            def pair1(p):
                segs = (2, 4, 6)[(p >= 3) + (p >= 6)]
                pe.wait_ge(norm1_done, 2 * segs)
                if p >= 2:
                    pe.wait_ge(pair1_copied, p - 1)
                for a, col in enumerate((Q_COL[p], K_COL[p])):
                    for t in range(T):
                        tr = pe.transpose(ps[:, TB + p % 2, (2 * a + t) * P:(2 * a + t + 1) * P], tok1[:, t, col:col + P], ident)
                tr.then_inc(pair1_turned, 1)

            def keys1(u):
                return P if u % 2 == 0 and u // 2 < 6 else TOK

            def score1(u):
                p, qt, nk = u // 2, u % 2, keys1(u)
                pe.wait_ge(pair1_copied, p + 1)
                if u:
                    pe.wait_ge(masked1, u)
                for m in range(2):
                    r = slice(HD * m, HD * (m + 1))
                    mm = pe.matmul(ps[:, S0 + m, (u % 2) * TOK:(u % 2) * TOK + nk], qT[r, p, qt * P:(qt + 1) * P],
                                   kT[r, p, 0:nk], start=True, stop=True)
                mm.then_inc(score1_ready, 1)

            def turn1(u):
                nt = keys1(u) // P
                pe.wait_ge(prob1, u + 1)
                if u == 0:
                    pe.wait_ge(pair1_copied, PAIRS)
                else:
                    pe.wait_ge(prob1_copied, u)
                for m in range(2):
                    for k in range(nt):
                        tr = pe.transpose(ps[:, TB, (m * nt + k) * P:(m * nt + k + 1) * P],
                                          ex[:, u % 2, (m * nt + k) * P:(m * nt + k + 1) * P], ident)
                tr.then_inc(prob1_turned, 1)

            def out1_of(u):
                p, nt = u // 2, keys1(u) // P
                pe.wait_ge(prob1_copied, u + 1)
                if u == 0:
                    for c in head1[:6]:
                        wait_drained(pe, None, c)
                else:
                    pe.wait_ge(out1_copied, u)
                for m in range(2):
                    for k in range(nt):
                        v = V_COL[p] + HD * m
                        mm = pe.matmul(ps[HD * m:HD * (m + 1), OB, (u % 4) * P:(u % 4 + 1) * P], tok1[:, k, v:v + HD],
                                       wt[:, u % 2, (m * nt + k) * P:(m * nt + k + 1) * P],
                                       start=(k == 0), stop=(k == nt - 1))
                mm.then_inc(out1_ready, 1)

            for step in steps1:
                if step[0] == "half":
                    if step[1].act == "memT" and step[2:] == (0, 0):
                        wait_xT(None, 2)
                    half(None, *step[1:])
                elif step[0] == "pair1":
                    pair1(step[1])
                elif step[0] == "score1":
                    score1(step[1])
                elif step[0] == "turn1":
                    turn1(step[1])
                elif step[0] == "out1":
                    out1_of(step[1])
            pe.wait_ge(o1_split, 4)
            for c in head1[-2:]:
                wait_drained(pe, None, c)
            for j in range(4):
                s = branch1_slot0 + j
                if j >= 2:
                    pe.wait_ge(branch1_free, j - 1)
                w = block(s, TOK)
                for q in range(HALVES):
                    wait_block(None, s, q)
                    k0 = 0
                    for r, n in enumerate(BRANCH_TILES):
                        for k in range(k0, k0 + n):
                            mm = product(tiles(4 * (j % 2) + r)[:, q, :], [v[:, k, q * P:(q + 1) * P] for v in w],
                                         [a[:, k, :] for a in acts["o1T"]], k == k0, k == k0 + n - 1)
                        k0 += n
                    used(mm, q)
            pe.wait_ge(m_split, 4)
            for c in out1:
                for part in range(2 * HALVES):
                    half(None, c, part // HALVES, part % HALVES)
            norm(None, 2, xhat)
            ffn(None, ffn0, 3)
            norm(None, 3, x)

            with pe.Fori(0, LAYERS) as L:
                def turn_rows():
                    pe.wait_ge(rows_loaded, lap(L, 11 * 16, 11 * 16))
                    pe.transpose(bank(OB)[:, 0:N_ROWS2], rows[0:N_ROWS2, 0, :], ident[0:N_ROWS2, 0:N_ROWS2])
                    pe.transpose(bank(OB)[:, P:P + N_CONV2], rows[0:N_CONV2, 1, :], ident[0:N_CONV2, 0:N_CONV2])\
                        .then_inc(rows_turned, 1)

                def dt():
                    pe.wait_ge(par_loaded, lap(L, 5 * 16, 5 * 16))
                    for t in range(T):
                        for k in range(KD):
                            for part in acts["xT"]:
                                mm = pe.matmul(ps[:, OB, t * NH:(t + 1) * NH], part[:, k, t * P:(t + 1) * P].bitcast(F32), dtw[:, k, :],
                                               start=(k == 0 and part is xT_hi), stop=(k == KD - 1 and part is xT_lo))
                    mm.then_inc(dt_ready, 1)

                def turn_qk(j):
                    which, hp = j % 2, j // 2
                    src = (qa, ka)[which]
                    wait_drained(pe, L, mix[2 * which + hp // 2])
                    if hp == 0 and which == 1:
                        pe.wait_ge(dt_arg, lap(L, 1, 1))
                    if hp:
                        pe.wait_ge((q_copied, k_copied)[which], lap(L, hp, 4))
                    for h in range(2):
                        for t in range(T):
                            tr = pe.transpose(ps[:, TB + which, (2 * h + t) * P:(2 * h + t + 1) * P],
                                              src[:, t, (2 * hp + h) * P:(2 * hp + h + 1) * P], ident)
                    tr.then_inc((q_turned, k_turned)[which], 1)

                def dscore(u):
                    h, qt = u // 2, u % 2
                    nk = P * (1 + qt)
                    pe.wait_ge(q_copied, lap(L, h // 2 + 1, 4))
                    pe.wait_ge(k_copied, lap(L, h // 2 + 1, 4))
                    if u:
                        pe.wait_ge(d_masked, lap(L, u, 2 * DH))
                    for m in range(2):
                        r = slice(HD * m, HD * (m + 1))
                        mm = pe.matmul(ps[:, S0 + m, (u % 2) * TOK:(u % 2) * TOK + nk], qT[r, h, qt * P:(qt + 1) * P],
                                       kT[r, h, 0:nk], start=True, stop=True)
                    mm.then_inc(d_score, 1)

                def dturn(u):
                    pe.wait_ge(d_w, lap(L, u + 1, 2 * DH))
                    if u:
                        pe.wait_ge(d_copied, lap(L, u, 2 * DH))
                    else:
                        pe.wait_ge(q_copied, lap(L, 4, 4))
                    for k in range(1 + u % 2):
                        tr = pe.transpose(ps[:, TB, (u % 2) * TOK + k * P:(u % 2) * TOK + (k + 1) * P],
                                          ex[:, u % 2, k * P:(k + 1) * P], ident)
                    tr.then_inc(d_turned, 1)

                def dout(u):
                    h, nt = u // 2, 1 + u % 2
                    pe.wait_ge(d_copied, lap(L, u + 1, 2 * DH))
                    if u == 0:
                        for n in (4, 5):
                            wait_drained(pe, L, mix[n])
                        pe.wait_ge(k_copied, lap(L, 4, 4))
                    else:
                        pe.wait_ge(d_sq, lap(L, u, 2 * DH))
                    for k in range(nt):
                        mm = pe.matmul(ps[:, OB, (u % 4) * P:(u % 4 + 1) * P], wt[:, u % 2, k * P:(k + 1) * P],
                                       va[:, k, h * P:(h + 1) * P], start=(k == 0), stop=(k == nt - 1))
                    mm.then_inc(d_out, 1)

                def turn_oa(j):
                    if j < 2:
                        pe.wait_ge(d_norm, lap(L, T, T))
                    else:
                        pe.wait_ge(oa_copied, lap(L, j - 1, 4))
                    for h in range(2):
                        for t in range(T):
                            tr = pe.transpose(ps[:, TB + j % 2, (2 * h + t) * P:(2 * h + t + 1) * P],
                                              oA[:, t, (2 * j + h) * P:(2 * j + h + 1) * P], ident)
                    tr.then_inc(oa_turned, 1)

                def turn_xs(j):
                    if j < 2:
                        pe.wait_ge(oa_copied, lap(L, j + 3, 4))
                        pe.wait_ge(xbc_done, lap(L, 6, 6))
                    else:
                        pe.wait_ge(xs_copied, lap(L, j - 1, 4))
                    for t in range(T):
                        for f in range(2):
                            tr = pe.transpose(ps[:, TB + j % 2, (2 * t + f) * P:(2 * t + f + 1) * P],
                                              xbc[:, 2 * j + f, t * P:(t + 1) * P], ident)
                    tr.then_inc(xs_turned, 1)

                def causal_pair(out_bank, lhs0, lhs1, rhs):
                    pe.matmul(ps[:, out_bank, 0:TOK], lhs0, rhs[:, 0:TOK], start=True, stop=True)
                    return pe.matmul(ps[:, out_bank, TOK:CAUS], lhs1, rhs[:, P:TOK], start=True, stop=True)

                def causal_values(m, b, v0, v1, w):
                    r = slice(HD * m, HD * (m + 1))
                    pe.matmul(ps[r, b, 0:TOK], v0, w[:, 0:TOK], start=True, stop=False)
                    return pe.matmul(ps[r, b, P:TOK], v1, w[:, TOK:CAUS], start=False, stop=True)

                def cb(g):
                    if g == 0:
                        pe.wait_ge(d_masked, lap(L, 2 * DH, 2 * DH))
                        pe.wait_ge(xbc_done, lap(L, 6, 6))
                    causal_pair(S0 + g, xbc[:, 8 + g, 0:P], xbc[:, 8 + g, P:TOK], xbc[:, 10 + g, :]).then_inc(cb_ready, 1)

                def sdecay(u):
                    b = S0 + u % 2
                    pe.wait_ge(seg_built, lap(L, u + 1, NH))
                    if u < 2:
                        pe.wait_ge(cb_masked, lap(L, 2, 2))
                    else:
                        pe.wait_ge(seg_exp, lap(L, u - 1, NH))
                    w = seg_w[:, u % 2, :]
                    pe.matmul(ps[:, b, 0:TOK], w[:, 0:P], upto, start=True, stop=False)
                    pe.matmul(ps[:, b, P:TOK], w[:, 2 * P:3 * P], upto[:, 0:P], start=False, stop=True)
                    pe.matmul(ps[:, b, TOK:CAUS], w[:, P:2 * P], upto[:, 0:P], start=True, stop=True).then_inc(seg_ready, 1)

                def sout(u):
                    p = u // 2
                    pe.wait_ge(l_ready, lap(L, u + 1, NH))
                    if u == 0:
                        pe.wait_ge(xs_copied, lap(L, 4, 4))
                    if p >= 2 and u % 2 == 0:
                        pe.wait_ge(y_gated, lap(L, p - 1, NH // 2))
                    causal_values(u % 2, TB + p % 2, xs[:, 0, u * HD:(u + 1) * HD], xs[:, 1, u * HD:(u + 1) * HD],
                                  lmat[:, u % 2, :]).then_inc(y_ready, 1)

                def snorm(g):
                    pe.wait_ge(y_sq, lap(L, g + 1, 2))
                    pe.wait_ge(y_gated, lap(L, NH // 2, NH // 2))
                    w = wt[:, :, :].rearrange("p a (b n) -> p (a b) n", n=TOK)
                    for k in range(4):
                        mm = pe.matmul(ps[:, TB + g, 0:TOK], ones, w[:, k, :], start=(k == 0), stop=(k == 3))
                    mm.then_inc(y_sum, 1)

                def kscore(u):
                    r, pair = slice(HD * (u % 2), HD * (u % 2 + 1)), u // 2
                    if u == 0:
                        for c in mix:
                            if c.name in ("qc", "kc"):
                                wait_drained(pe, L, c)
                    if u < 2:
                        pe.wait_ge(seg_exp, lap(L, NH, NH))
                    else:
                        pe.wait_ge(s_masked, lap(L, u - 1, NH))
                    causal_pair(S0 + u % 2, kcT[r, pair, 0:P], kcT[r, pair, P:TOK], qcT[r, pair, :]).then_inc(s_score, 1)

                def ksum(u):
                    pe.wait_ge(s_soft, lap(L, u + 1, NH))
                    if u == 0:
                        pe.wait_ge(o_b, lap(L, 2, 2))
                    else:
                        pe.wait_ge(s_arg, lap(L, u, NH))
                    sp_ = lmat[:, u % 2, :]
                    pe.matmul(ps[:, TB, TOK:CAUS], from_on, sp_[:, TOK:CAUS], start=True, stop=True)
                    pe.matmul(ps[:, TB, 0:TOK], from_on, sp_[:, 0:TOK], start=True, stop=False)
                    pe.matmul(ps[:, TB, P:TOK], ones, sp_[:, TOK:CAUS], start=False, stop=True).then_inc(s_sum, 1)

                def kout(u):
                    p = u // 2
                    pe.wait_ge(s_exp, lap(L, u + 1, NH))
                    if u == 0:
                        for c in mix:
                            if c.name == "vc":
                                wait_drained(pe, L, c)
                    if u % 2 == 0:
                        if p:
                            pe.wait_ge(s_copied, lap(L, p, NH // 2))
                        else:
                            pe.wait_ge(o_b, lap(L, 2, 2))
                    causal_values(u % 2, OB, vc[:, 0, u * HD:(u + 1) * HD], vc[:, 1, u * HD:(u + 1) * HD],
                                  ex[:, u % 2, :]).then_inc(s_out, 1)

                attention = dict(turn_qk=turn_qk, dscore=dscore, dturn=dturn, dout=dout, turn_oa=turn_oa, turn_xs=turn_xs,
                                 cb=cb, sdecay=sdecay, sout=sout, snorm=snorm, kscore=kscore, ksum=ksum, kout=kout)
                ffn(L, ffn1, 4, turn_rows)
                pe.wait_ge(cols_ready, lap(L, 2, 1))
                norm(L, 4, xhat)
                wait_xT(L, 5)
                for step in mixed:
                    if step[0] == "half":
                        c = step[1]
                        if c.name == "branch" and c.index == 0 and step[2:] == (0, 0):
                            ready, n = ((oa_split, 4), (ob_split, 2), (oc_split, NH // 2))[c.r]
                            pe.wait_ge(ready, lap(L, n, n))
                        half(L, *step[1:])
                    elif step[0] == "dt":
                        dt()
                    elif step[0] in attention:
                        attention[step[0]](step[1])
                pe.wait_ge(m_split, lap(L, 8, 4))
                for c in out2:
                    for part in range(2 * HALVES):
                        half(L, c, part // HALVES, part % HALVES)
                norm(L, 5, xhat)
                ffn(L, ffn2, 6)
                norm(L, 6, xhat)

        @block.scalar
        def _(act):
            chain = Chain(act, act_chain)

            def norm_cols(L, event, g, b, dst, hi):
                for t in range(T):
                    act.wait_ge(hat_turned, lap(L, 4 * event + 2 * t + 1, 12))
                    for k in range(4):
                        o, i = dst[:, k, t * P:(t + 1) * P], ps[:, 4 + 2 * t, k * P:(k + 1) * P]
                        if g is None:
                            ins_ = act.activation(o, i, ACT.Copy)
                        elif b is None:
                            ins_ = act.activation(o, i, ACT.Copy, scale=g[:, k:k + 1])
                        else:
                            ins_ = act.activation(o, i, ACT.Identity, scale=g[:, k:k + 1], bias=b[:, k:k + 1])
                    chain.link(ins_)
                    chain.sync()
                    act.activation(hi[:, 0:4, t * P:(t + 1) * P], dst[:, 0:4, t * P:(t + 1) * P], ACT.Copy).then_inc(xT_act, 1)

            def split_half(L, s, q, it=0):
                if q == 0:
                    wait_loaded(act, L, s, it * 16)
                if L is not None or s >= HIGHS:
                    whole = q or (s in by_rows) != (s - HIGHS in by_rows)
                    act.wait_ge(multiplied if whole else first_used, lap(L, s - HIGHS + 1, SLOT_LAP) + it * SLOTS)
                act.activation(half_of(ring_hi[:, s % HIGHS, :], s, q), half_of(ring[:, s % SLOTS, :], s, q), ACT.Copy).then_inc(w_hi, 1)

            def split(L, s, it=0):
                for q in range(HALVES):
                    split_half(L, s, q, it)

            def down_splits(L, f):
                for s in range(f["slot0"] + 2 * FFC + HIGHS, f["slot0"] + 3 * FFC + f["ahead"]):
                    split(L, s)

            def sigmoid(places, done):
                for e in places:
                    chain.link(act.activation(e, e, ACT.Ln, bias=1.0))
                chain.sync()
                for e in places:
                    act.activation(e, e, ACT.Exp, scale=-1.0).then_inc(done, 1)

            def squares(src, event):
                for t in range(T):
                    if event >= 2:
                        act.wait_ge(x_added, t + 1)
                    if 2 * event + t:
                        act.wait_ge(sq_ready, 2 * event + t)
                    act.activation(wide[:, 4:8, :].rearrange("p a n -> p (a n)"), src[:, t, :], ACT.Square,
                                   accum_out=small[:, 64 + 2 * event + t:65 + 2 * event + t]).then_inc(sq_ready, 1)

            def ffn_silu(L, f):
                def up(it, js):
                    for j in js:
                        split(L, f["slot0"] + 2 * j + HIGHS, it)
                        act.wait_ge(multiplied, lap(L, f["slot0"] + 2 * j + 1, SLOT_LAP) + it * 4)
                        act.wait_ge(drained[2 * j + 1], lap(L, f["free0"][2 * j + 1], FREE_LAP[2 * j + 1]) + it)
                        act.activation(act_s[:, j, :], bank(2 * j), ACT.Silu).then_inc(drained[2 * j], 1)
                        split(L, f["slot0"] + 2 * j + 1 + HIGHS, it)

                with act.Fori(0, FFC // 2) as it:
                    up(it, range(2))
                up(FFC // 2, range(1))
                down_splits(L, f)

            def ffn_conv(f):
                def up(it, js):
                    for j in js:
                        for side in range(2):
                            split(None, f["slot0"] + 2 * j + side + HIGHS, it)
                        act.wait_ge(multiplied, f["slot0"] + 2 * j + 2 + it * 4)
                        if j == 0:
                            act.wait_ge(h_ready, it * 2 + 2)
                        for side, dst in enumerate((act_s, conv_s)):
                            for ft in range(2):
                                tile = it * 4 + (2 * j + ft + side * KF)
                                ins_ = act.activation(
                                    dst[:, j, ft * TOK:(ft + 1) * TOK], tiles(2 * j + side)[:, ft, :], ACT.Identity,
                                    scale=conv1[:, bass.ds(tile + 2 * 2 * KF, 1)],
                                    bias=conv1[:, bass.ds(tile + N_CONV1 + ROWS1["conv_b"], 1)])
                        ins_.then_inc(conv_begun, 1)
                        act.wait_ge(drained[2 * j], f["free0"][2 * j] + it + 1)
                        act.activation(act_s[:, j, :], act_s[:, j, :], ACT.Silu).then_inc(act_ready, 1)

                with act.Fori(0, FFC // 2) as it:
                    up(it, range(2))
                up(FFC // 2, range(1))
                down_splits(None, f)

            act.wait_ge(in_loaded, 4 * 16)
            squares(x, 0)
            squares(gb, 1)
            act.wait_ge(angle_ready, 1)
            act.activation(kcT[:, 7, 128:256], kcT[:, 7, 0:128], ACT.Sin).then_inc(sin_ready, 1)
            act.preload_act_table_set("natural_log_exp_and_others")
            act.wait_ge(cols_ready, 1)
            g1 = conv1[:, N_CONV1:N_CONV1 + N_ROWS1]
            norm_cols(None, 0, g1[:, 0:8], None, xT, xT_hi)
            for slot in range(HIGHS):
                split(None, slot)
            norm_cols(None, 1, g1[:, 8:16], None, memT, acts["memT"][0])

            def drain_tok(c):
                wait_products(act, None, c)
                col = c.index * BANK
                for t in range(T):
                    act.activation(tok1[:, t, col:col + BANK], bank(2 * c.pair + t), ACT.Copy).then_inc(drained[2 * c.pair + t], 1)

            def drain_gate1(c):
                wait_products(act, None, c)
                for j in range(2):
                    k = 4 * c.index + 2 * j
                    act.activation(wide[:, k:k + 2, :], tiles(2 * c.pair + j), ACT.Exp, scale=-1.0)\
                        .then_inc(drained[2 * c.pair + j], 1)
                wait_drained(act, None, c)
                sigmoid([wide[:, 4 * c.index + 2 * j:4 * c.index + 2 * j + 2, :] for j in range(2)], gate_ready)

            def pair1(p):
                act.wait_ge(pair1_turned, p + 1)
                act.activation(qT[:, p, :], ps[:, TB + p % 2, 0:TOK], ACT.Copy)
                act.activation(kT[:, p, :], ps[:, TB + p % 2, TOK:BANK], ACT.Copy).then_inc(pair1_copied, 1)

            def keys1(u):
                return P if u % 2 == 0 and u // 2 < 6 else TOK

            def score1(u):
                nk, at = keys1(u), (u % 4) * 16
                act.wait_ge(peak1, u + 1)
                if u >= 2:
                    act.wait_ge(prob1_turned, u - 1)
                for m in range(2):
                    ins_ = act.activation(ex[:, u % 2, m * nk:(m + 1) * nk], sm[:, u % 2, m * nk:(m + 1) * nk], ACT.Exp,
                                          bias=small[:, at + m:at + m + 1], accum_out=small[:, at + 2 + m:at + 3 + m])
                ins_.then_inc(exp1, 1)

            def turn1(u):
                act.wait_ge(prob1_turned, u + 1)
                if u >= 2:
                    act.wait_ge(out1_ready, u - 1)
                act.activation(wt[:, u % 2, 0:2 * keys1(u)], ps[:, TB, 0:2 * keys1(u)], ACT.Copy).then_inc(prob1_copied, 1)

            def out1_of(u):
                act.wait_ge(out1_ready, u + 1)
                for place in (o1T, acts["o1T"][0]):
                    ins_ = act.activation(place[:, u // 2, (u % 2) * P:(u % 2 + 1) * P], ps[:, OB, (u % 4) * P:(u % 4 + 1) * P], ACT.Copy)
                ins_.then_inc(out1_copied, 1)

            for step in steps1:
                if step[0] == "drain":
                    (drain_tok if step[1].name == "tok" else drain_gate1)(step[1])
                elif step[0] == "split":
                    split_half(None, *step[1:])
                elif step[0] == "pair1":
                    pair1(step[1])
                elif step[0] == "score1":
                    score1(step[1])
                elif step[0] == "turn1":
                    turn1(step[1])
                elif step[0] == "out1":
                    out1_of(step[1])
            for j in range(4):
                split(None, branch1_slot0 + j + HIGHS)
                act.wait_ge(mixed1, j + 1)
                act.activation(xT_hi[:, 2 * j:2 * j + 2, :], mT[:, 2 * j:2 * j + 2, :], ACT.Copy).then_inc(m_hi, 1)
            for slot in range(out1[0].slot0 + HIGHS, ffn0["slot0"] + 1):
                split(None, slot)
            squares(x, 2)
            norm_cols(None, 2, g1[:, 16:24], None, xT, xT_hi)
            split(None, ffn0["slot0"] + 1)
            ffn_conv(ffn0)
            norm_cols(None, 3, None, None, xT, xT_hi)

            with act.Fori(0, LAYERS) as L:
                chain.enter(L)

                def xhat_of(k):
                    for t in range(T):
                        act.wait_ge(stat_ready, lap(L, 2 * k + t + 1, 6))
                        s = small[:, 96 + 4 * t:96 + 4 * t + 4]
                        act.activation(xhat[:, t, :], x[:, t, :], ACT.Identity, scale=s[:, 2:3], bias=s[:, 3:4]).then_inc(hat_ready, 1)

                def layer_norm(k):
                    xhat_of(k)
                    g, b = ROWS2["ln_g"][k], ROWS2["ln_b"][k]
                    norm_cols(L, 4 + k, cols[:, g:g + 8], cols[:, b:b + 8], xT, xT_hi)

                def drain(c):
                    p = c.pair
                    if c.name in ("qa", "ka"):
                        dst = qa if c.name == "qa" else ka
                        wait_products(act, L, c)
                        for t in range(T):
                            o = dst[:, t, c.index * BANK:(c.index + 1) * BANK].rearrange("p (m d) -> p m d", d=HD)
                            i = bank(2 * p + t).rearrange("p (m d) -> p m d", d=HD)
                            act.activation(o[:, :, 16:HD], i[:, :, 16:HD], ACT.Copy).then_inc(drained[2 * p + t], 1)
                    elif c.name == "va":
                        wait_products(act, L, c)
                        for t in range(T):
                            act.activation(va[:, t, c.index * BANK:(c.index + 1) * BANK], bank(2 * p + t), ACT.Copy)\
                                .then_inc(drained[2 * p + t], 1)
                    elif c.name == "zb":
                        wait_products(act, L, c)
                        if c.index == 0:
                            act.wait_ge(xbc_done, lap(L, 6, 6))
                        else:
                            act.wait_ge(drained[2 * p + 1], lap(L, c.need[2 * p + 1], FREE_LAP[2 * p + 1]))
                            wait_drained(act, L, [d for d in mix if d.name == "zb"][0])
                        places = [conv_s[:, j, :] for j in range(2)]
                        for j in range(2):
                            chain.link(act.activation(places[j], bank(2 * p + j), ACT.Exp, scale=-1.0))
                        chain.sync()
                        sigmoid(places, z_exp)
                    elif c.name == "xbc":
                        wait_products(act, L, c)
                        if c.index:
                            act.wait_ge(xbc_done, lap(L, 2 * c.index, 6))
                        for j in range(2):
                            for f in range(2):
                                k = 4 * c.index + 2 * j + f
                                ins_ = act.activation(conv_s[:, j, f * TOK:(f + 1) * TOK], tiles(2 * p + j)[:, f, :], ACT.Identity,
                                                      scale=cols[:, P + 3 * N_XBC + k:P + 3 * N_XBC + k + 1],
                                                      bias=cols[:, P + 4 * N_XBC + k:P + 4 * N_XBC + k + 1])
                            ins_.then_inc(xbc_begun, 1)
                        for j in range(2):
                            act.wait_ge(drained[2 * p + j], lap(L, c.need[2 * p + j] + 1, FREE_LAP[2 * p + j]))
                            chain.link(act.activation(act_s[:, j, :], conv_s[:, j, :], ACT.Exp, scale=-1.0))
                        chain.sync()
                        sigmoid([act_s[:, j, :] for j in range(2)], xbc_exp)
                    elif c.name in ("qc", "kc"):
                        wait_products(act, L, c)
                        dst = qcT if c.name == "qc" else kcT
                        act.activation(dst[:, 4 * c.index:4 * c.index + 2, :], tiles(2 * p), ACT.Copy).then_inc(drained[2 * p], 1)
                    elif c.name == "vc":
                        wait_products(act, L, c)
                        act.wait_ge(x_ready, x_count(L, 2))
                        act.activation(vc[:, 0, c.index * BANK:(c.index + 1) * BANK], bank(2 * p), ACT.Copy).then_inc(drained[2 * p], 1)
                    elif c.name == "gate":
                        wait_products(act, L, c)
                        for j in range(2):
                            for f in range(2):
                                k = 4 * c.index + 2 * j + f
                                ins_ = act.activation(wide[:, k, :], tiles(2 * p + j)[:, f, :], ACT.Exp, scale=-1.0,
                                                      bias=small[:, 128 + k:129 + k])
                            ins_.then_inc(drained[2 * p + j], 1)
                        wait_drained(act, L, c)
                        sigmoid([wide[:, 4 * c.index + 2 * j:4 * c.index + 2 * j + 2, :] for j in range(2)], gate_ready)
                    elif c.name == "branch" and c.r == 2:
                        for j in range(2):
                            k = 4 * c.index + 2 * j
                            act.wait_ge(mixed_sem, lap(L, 2 * c.index + j + 1, 4))
                            act.activation(xT_hi[:, k:k + 2, :], mT[:, k:k + 2, :], ACT.Copy).then_inc(m_hi, 1)

                def dt():
                    act.wait_ge(par_loaded, lap(L, 5 * 16, 5 * 16))
                    chain.link(act.activation(dts[:, 5, 0:NH], bcast[:, 272:288], ACT.Exp))
                    act.wait_ge(lam_arg, lap(L, 1, 1))
                    act.activation(small[:, 162:164], small[:, 160:162], ACT.Exp).then_inc(lam_exp, 1)
                    act.wait_ge(dt_arg, lap(L, 1, 1))
                    chain.link(act.activation(dts[:, 2, :], dts[:, 1, :], ACT.Exp, scale=-1.0))
                    chain.sync()
                    act.activation(dts[:, 3, :], dts[:, 2, :], ACT.Ln, bias=1.0).then_inc(dt_log, 1)

                def turn_qk(j):
                    if j % 2 == 0:
                        act.wait_ge(q_turned, lap(L, j // 2 + 1, 4))
                        if j == 0:
                            act.wait_ge(x_ready, x_count(L, 2))
                        act.activation(qT[:, j:j + 2, :], tiles(TB), ACT.Copy).then_inc(q_copied, 1)

                def dscore(u):
                    nk, at = P * (1 + u % 2), (u % 4) * 16
                    act.wait_ge(d_peak, lap(L, u + 1, 2 * DH))
                    if u >= 2:
                        act.wait_ge(d_turned, lap(L, u - 1, 2 * DH))
                    for m in range(2):
                        ins_ = act.activation(ex[:, u % 2, m * nk:(m + 1) * nk], sm[:, u % 2, m * nk:(m + 1) * nk], ACT.Exp,
                                              bias=small[:, at + m:at + m + 1], accum_out=small[:, at + 2 + m:at + 3 + m])
                    ins_.then_inc(d_exp, 1)

                def dturn(u):
                    nk = P * (1 + u % 2)
                    act.wait_ge(d_turned, lap(L, u + 1, 2 * DH))
                    if u >= 2:
                        act.wait_ge(d_out, lap(L, u - 1, 2 * DH))
                    act.activation(wt[:, u % 2, 0:nk], ps[:, TB, (u % 2) * TOK:(u % 2) * TOK + nk], ACT.Copy).then_inc(d_copied, 1)

                def dout(u):
                    act.wait_ge(d_out, lap(L, u + 1, 2 * DH))
                    if u:
                        act.wait_ge(d_sq, lap(L, u, 2 * DH))
                    o = ps[:, OB, (u % 4) * P:(u % 4 + 1) * P]
                    act.activation(oA[:, u % 2, (u // 2) * P:(u // 2 + 1) * P], o, ACT.Copy)
                    n = 184 + (u % 2) * DH + u // 2
                    act.activation(act_j[:, :], o, ACT.Square, accum_out=small[:, n:n + 1]).then_inc(d_sq, 1)

                def turn_oa(j):
                    act.wait_ge(oa_turned, lap(L, j + 1, 4))
                    if j == 0:
                        act.wait_ge(lam_ready, lap(L, 1, 1))
                    for place in (qT, kT_r):
                        ins_ = act.activation(place[:, 2 * j:2 * j + 2, :], tiles(TB + j % 2), ACT.Copy, scale=small[:, 166:167])
                    ins_.then_inc(oa_copied, 1)

                def turn_xs(j):
                    act.wait_ge(xs_turned, lap(L, j + 1, 4))
                    act.activation(xs[:, :, 2 * j * P:(2 * j + 2) * P], tiles(TB + j % 2), ACT.Copy).then_inc(xs_copied, 1)

                def sdecay(u):
                    act.wait_ge(seg_ready, lap(L, u + 1, NH))
                    if u < 2:
                        act.wait_ge(d_turned, lap(L, 2 * DH, 2 * DH))
                    else:
                        act.wait_ge(l_ready, lap(L, u - 1, NH))
                    act.activation(ex[:, u % 2, 0:CAUS], ps[:, S0 + u % 2, 0:CAUS], ACT.Exp).then_inc(seg_exp, 1)

                def snorm(g):
                    act.wait_ge(y_gated, lap(L, 4 * (g + 1), NH // 2))
                    if g:
                        act.wait_ge(y_sum, lap(L, g, 2))
                    act.activation(wt[:, :, :].rearrange("p a n -> p (a n)"),
                                   zT[:, 4 * g:4 * g + 4, :].rearrange("p a n -> p (a n)"), ACT.Square).then_inc(y_sq, 1)
                    r = sm[:, g, 0:TOK]
                    act.wait_ge(y_sum, lap(L, g + 1, 2))
                    act.wait_ge(y_gated, lap(L, NH // 2, NH // 2))
                    chain.link(act.activation(r, ps[:, TB + g, 0:TOK], ACT.Ln, scale=1.0 / (4 * P), bias=cst("ln_eps")))
                    chain.sync()
                    act.activation(r, r, ACT.Exp, scale=-0.5).then_inc(y_root, 1)

                def bsplit(g):
                    act.wait_ge(o_b, lap(L, g + 1, 2))
                    act.activation(xbc_r[:, 4 * g:4 * g + 4, :], zT[:, 4 * g:4 * g + 4, :], ACT.Copy).then_inc(ob_hi, 1)

                def kscore(u):
                    b = lmat[:, u % 2, :]
                    act.wait_ge(s_abs, lap(L, u + 1, NH))
                    chain.link(act.activation(b, b, ACT.Exp, scale=-1.0))
                    chain.sync()
                    act.activation(b, b, ACT.Ln, bias=1.0).then_inc(s_log, 1)

                def ksum(u):
                    act.wait_ge(s_arg, lap(L, u + 1, NH))
                    if u < 2:
                        act.wait_ge(l_ready, lap(L, NH, NH))
                    else:
                        act.wait_ge(s_out, lap(L, u - 1, NH))
                    act.activation(ex[:, u % 2, 0:CAUS], sm[:, u % 2, 0:CAUS], ACT.Exp).then_inc(s_exp, 1)

                def kout(u):
                    if u % 2:
                        p = u // 2
                        act.wait_ge(s_out, lap(L, u + 1, NH))
                        for place in (qcT, kcT_r):
                            ins_ = act.activation(place[:, p, :], ps[:, OB, 0:TOK], ACT.Copy)
                        ins_.then_inc(s_copied, 1)

                attention = dict(turn_qk=turn_qk, dscore=dscore, dturn=dturn, dout=dout, turn_oa=turn_oa, turn_xs=turn_xs,
                                 sdecay=sdecay, snorm=snorm, bsplit=bsplit, kscore=kscore, ksum=ksum, kout=kout, drain=drain)
                for slot in range(HIGHS):
                    split(L, ffn1["slot0"] + slot)
                ffn_silu(L, ffn1)
                act.preload_act_table_set("natural_log_exp_and_others")
                act.wait_ge(cols_ready, lap(L, 2, 1))
                layer_norm(0)
                split(L, mix[0].slot0 + 1)
                for step in mixed:
                    if step[0] == "dt":
                        dt()
                    elif step[0] == "split":
                        split_half(L, *step[1:])
                    elif step[0] in attention:
                        attention[step[0]](step[1])
                for slot in range(out2[0].slot0 + HIGHS, ffn2["slot0"] + 1):
                    split(L, slot)
                act.preload_act_table(ACT.Silu)
                layer_norm(1)
                split(L, ffn2["slot0"] + 1)
                ffn_silu(L, ffn2)
                layer_norm(2)
                chain.leave()

        @block.vector
        def _(dve):
            chain = Chain(dve, dve_chain)
            link, sync = chain.link, chain.sync

            roots = [0]

            def ask_root(L, ins_):
                ins_.then_inc(root_asked, 1)
                roots[0] += 1
                dve.wait_ge(root_done, lap(L, roots[0], ROOTS_LAP))

            def low(lo, whole, hi):
                return dve.tensor_tensor(lo, whole, hi.bitcast(F32), ALU.subtract)

            def split_half(L, s, q, it=0):
                dve.wait_ge(w_hi, lap(L, HALVES * s + q + 1, HALVES * SLOT_LAP) + it * (HALVES * SLOTS))
                low(half_of(ring_lo[:, s % SLOTS, :], s, q), half_of(ring[:, s % SLOTS, :], s, q), half_of(ring_hi[:, s % HIGHS, :], s, q))\
                    .then_inc(w_lo, 1)

            def split(L, s, it=0):
                for q in range(HALVES):
                    split_half(L, s, q, it)

            def down_splits(L, f):
                for s in range(f["slot0"] + 2 * FFC + HIGHS, f["slot0"] + 3 * FFC + f["ahead"]):
                    split(L, s)

            def hidden_parts(L, f, it, j):
                k = bass.ds(it * 4 + 2 * j, 2)
                dve.tensor_copy(h2_hi[:, k, :], h2[:, k, :]).then_inc(h_hi, 1)
                dve.wait_ge(h_hi, lap(L, f["h0"] + j + 1, 2 * FFC) + it * 2)
                low(h2_lo[:, k, :], h2[:, k, :], h2_hi[:, k, :]).then_inc(h_lo, 1)

            def norm_cols(L, event, g, b, dst, hi, lo):
                for t in range(T):
                    dve.wait_ge(hat_turned, lap(L, 4 * event + 2 * t + 2, 12))
                    for k in range(4):
                        o, i = dst[:, 4 + k, t * P:(t + 1) * P], ps[:, 5 + 2 * t, k * P:(k + 1) * P]
                        if g is None:
                            ins_ = dve.tensor_copy(o, i)
                        elif b is None:
                            ins_ = dve.tensor_scalar(o, i, g[:, 4 + k:5 + k], None, ALU.mult)
                        else:
                            ins_ = dve.tensor_scalar(o, i, g[:, 4 + k:5 + k], b[:, 4 + k:5 + k], ALU.mult, ALU.add)
                    link(ins_)
                    sync()
                    n = slice(t * P, (t + 1) * P)
                    link(dve.tensor_copy(hi[:, 4:8, n], dst[:, 4:8, n]))
                    sync()
                    link(low(lo[:, 4:8, n], dst[:, 4:8, n], hi[:, 4:8, n]))
                    dve.wait_ge(xT_act, lap(L, 2 * event + t + 1, 6))
                    low(lo[:, 0:4, n], dst[:, 0:4, n], hi[:, 0:4, n]).then_inc(xT_dve, 1)

            def rms_rows(src, event):
                for t in range(T):
                    r = small[:, 64 + 2 * event + t:65 + 2 * event + t]
                    dve.wait_ge(sq_ready, 2 * event + t + 1)
                    ask_root(None, dve.tensor_scalar(r, r, D * RMS_EPS, None, ALU.add))
                    if event == 1:
                        dve.wait_ge(hat_turned, 2 * t + 2)
                    dve.tensor_scalar(xhat[:, t, :], src[:, t, :], r, float(D) ** 0.5, ALU.mult, ALU.mult).then_inc(hat_ready, 1)

            def ffn_mul(L, f):
                def up(it, js):
                    for j in js:
                        b = 2 * j
                        split(L, f["slot0"] + b + HIGHS, it)
                        split_half(L, f["slot0"] + b + 1 + HIGHS, 0, it)
                        dve.wait_ge(drained[b], lap(L, f["free0"][b] + 1, FREE_LAP[b]) + it)
                        dve.wait_ge(multiplied, lap(L, f["slot0"] + b + 2, SLOT_LAP) + it * 4)
                        dve.tensor_tensor(h2[:, bass.ds(it * 4 + 2 * j, 2), :].rearrange("p a n -> p (a n)"),
                                          act_s[:, j, :], bank(b + 1), ALU.mult).then_inc(drained[b + 1], 1)
                        split_half(L, f["slot0"] + b + 1 + HIGHS, 1, it)
                        dve.wait_ge(drained[b + 1], lap(L, f["free0"][b + 1] + 1, FREE_LAP[b + 1]) + it)
                        hidden_parts(L, f, it, j)

                with dve.Fori(0, FFC // 2) as it:
                    up(it, range(2))
                up(FFC // 2, range(1))
                down_splits(L, f)

            def ffn_conv(f):
                def up(it, js):
                    for j in js:
                        for side in range(2):
                            split(None, f["slot0"] + 2 * j + side + HIGHS, it)
                        dve.wait_ge(conv_begun, it * 2 + j + 1)
                        for tap in (1, 0):
                            s = 2 - tap
                            if tap == 0:
                                dve.wait_ge(conv_tap, it * 2 + j + 1)
                            for side, dst in enumerate((act_s, conv_s)):
                                for ft in range(2):
                                    tile = it * 4 + (2 * j + ft + side * KF)
                                    o = dst[:, j, ft * TOK + s:(ft + 1) * TOK]
                                    ins_ = dve.scalar_tensor_tensor(
                                        o, tiles(2 * j + side)[:, ft, 0:TOK - s],
                                        conv1[:, bass.ds(tile + tap * 2 * KF, 1)], o, ALU.mult, ALU.add)
                                if tap == 0:
                                    ins_.then_inc(drained[2 * j + side], 1)
                            if tap == 1:
                                ins_.then_inc(conv_tap, 1)
                        dve.wait_ge(act_ready, it * 2 + j + 1)
                        dve.wait_ge(drained[2 * j + 1], f["free0"][2 * j + 1] + it + 1)
                        dve.tensor_tensor(h2[:, bass.ds(it * 4 + 2 * j, 2), :].rearrange("p a n -> p (a n)"),
                                          act_s[:, j, :], conv_s[:, j, :], ALU.mult).then_inc(h_ready, 1)
                        dve.wait_ge(h_ready, it * 2 + j + 3)
                        hidden_parts(None, f, it, j)

                dve.sem_inc(h_ready, 2)
                with dve.Fori(0, FFC // 2) as it:
                    up(it, range(2))
                up(FFC // 2, range(1))
                down_splits(None, f)

            dve.wait_ge(in_loaded, 4 * 16)
            dve.wait_ge(rows1_turned, 1)
            dve.tensor_copy(conv1[:, :], ps[:, 4, 0:N_CONV1 + N_ROWS1]).then_inc(cols_ready, 1)
            dve.wait_ge(cols_ready, 1)
            rms_rows(x, 0)
            dve.wait_ge(par1_loaded, 8 * 16)
            posf, ang, turns, red = small[:, 80:82], kcT[:, 6, 0:64], kcT[:, 6, 64:128], kcT[:, 7, 0:128]
            link(dve.tensor_copy(posf, pos[:, :]))
            sync()
            for t in range(T):
                link(dve.tensor_scalar(ang[:, 32 * t:32 * t + 32], cst("freq"), posf[:, t:t + 1], None, ALU.mult))
            sync()
            link(dve.tensor_scalar(turns, ang, float(1 / (2 * np.pi)), 12582912.0, ALU.mult, ALU.add))
            sync()
            link(dve.tensor_scalar(turns, turns, 12582912.0, None, ALU.subtract))
            sync()
            c1 = 6.28125
            c2 = int((2 * np.pi - c1) * 2 ** 20) / 2 ** 20
            c3 = float(2 * np.pi - c1 - c2)
            for c in (c1, c2, c3):
                link(dve.scalar_tensor_tensor(ang, turns, -c, ang, ALU.mult, ALU.add))
                sync()
            halfpi = float(np.float32(np.pi / 2))
            pi_in = 3.1415925
            link(dve.tensor_scalar(red[:, 0:64], ang, pi_in, -pi_in, ALU.min, ALU.max))
            link(dve.tensor_scalar(red[:, 64:128], ang, halfpi, None, ALU.add))
            sync()
            link(dve.tensor_scalar(turns, red[:, 64:128], float(np.pi), -2 * float(np.pi), ALU.is_gt, ALU.mult))
            sync()
            link(dve.tensor_tensor(red[:, 64:128], red[:, 64:128], turns, ALU.add))
            sync()
            dve.tensor_scalar(red[:, 64:128], red[:, 64:128], pi_in, -pi_in, ALU.min, ALU.max).then_inc(angle_ready, 1)
            norm_cols(None, 0, conv1[:, N_CONV1:N_CONV1 + 8], None, xT, xT_hi, xT_lo)
            for slot in range(HIGHS):
                split(None, slot)
            rms_rows(gb, 1)
            norm_cols(None, 1, conv1[:, N_CONV1 + 8:N_CONV1 + 16], None, memT, *acts["memT"])
            dve.wait_ge(sin_ready, 1)
            sin, cos = kcT[:, 7, 128:192], kcT[:, 7, 192:256]
            gain = gains1.rearrange("p (a d) -> p a d", d=HD)
            link(dve.tensor_scalar(gains1, gains1, float(HD) ** 0.5, None, ALU.mult))
            sync()

            def rot(i, t):
                return qcT[:, i, t * HD:(t + 1) * HD], qcT[:, i, P + t * HD:P + (t + 1) * HD]

            for i in range(4):
                for t in range(T):
                    c_, s_ = rot(i, t)
                    ct, st = cos[:, 32 * t:32 * t + 32], sin[:, 32 * t:32 * t + 32]
                    lo, hi = slice(0, 32), slice(32, HD)
                    link(dve.tensor_tensor(c_[:, lo], gain[:, i, lo], ct, ALU.mult))
                    link(dve.tensor_tensor(c_[:, hi], gain[:, i, hi], ct, ALU.mult))
                    link(dve.scalar_tensor_tensor(s_[:, lo], gain[:, i, hi], -1.0, st, ALU.mult, ALU.mult))
                    link(dve.tensor_tensor(s_[:, hi], gain[:, i, lo], st, ALU.mult))
            sync()

            def norm1(n):
                col, heads, i, turned = NORMED[n]
                for t in range(T):
                    v = tok1[:, t, col:col + heads * HD].rearrange("p (h d) -> p h d", d=HD)
                    sq, xn, rx = (kcT[:, 2 * a:2 * a + 2, :].rearrange("p a n -> p (a n)")[:, 0:heads * HD]
                                  .rearrange("p (h d) -> p h d", d=HD) for a in range(3))
                    r = small[:, 84:84 + heads]
                    if n or t:
                        dve.wait_ge(norm1_done, 2 * n + t)
                    link(dve.tensor_tensor(sq, v, v, ALU.mult))
                    sync()
                    link(dve.tensor_reduce(r, sq, AX_X, ALU.add))
                    sync()
                    ask_root(None, dve.tensor_scalar(r, r, HD * RMS_EPS, None, ALU.add))
                    link(dve.tensor_tensor(xn, v, r.unsqueeze(2).to_broadcast([P, heads, HD]), ALU.mult))
                    sync()
                    if not turned:
                        dve.tensor_tensor(v, xn, gain[:, i, :].unsqueeze(1).to_broadcast([P, heads, HD]), ALU.mult).then_inc(norm1_done, 1)
                        continue
                    c_, s_ = (a.unsqueeze(1).to_broadcast([P, heads, HD]) for a in rot(i, t))
                    link(dve.tensor_tensor(sq, xn, c_, ALU.mult))
                    link(dve.tensor_tensor(rx[:, :, 0:32], xn[:, :, 32:HD], s_[:, :, 0:32], ALU.mult))
                    link(dve.tensor_tensor(rx[:, :, 32:HD], xn[:, :, 0:32], s_[:, :, 32:HD], ALU.mult))
                    sync()
                    dve.tensor_tensor(v, sq, rx, ALU.add).then_inc(norm1_done, 1)

            def drain1(c):
                if c.name == "tok":
                    wait_drained(dve, None, c)
                    norm1(c.index)

            def keys1(u):
                return P if u % 2 == 0 and u // 2 < 6 else TOK

            def peak(L, u, nk, per, masked, peak_):
                at = (u % 4) * 16
                dve.wait_ge(masked, lap(L, u + 1, per))
                link(dve.tensor_reduce(small[:, at + 4:at + 6], sm[:, u % 2, 0:2 * nk].rearrange("p (m k) -> p m k", k=nk), AX_X, ALU.max))
                sync()
                dve.tensor_scalar(small[:, at:at + 2], small[:, at + 4:at + 6], -1.0, None, ALU.mult).then_inc(peak_, 1)

            def score1(u):
                p, qt, nk = u // 2, u % 2, keys1(u)
                dve.wait_ge(score1_ready, u + 1)
                if u >= 2:
                    dve.wait_ge(exp1, u - 1)
                o = sm[:, u % 2, 0:2 * nk].rearrange("p (m k) -> p m k", k=nk)
                i = ps[:, S0:S0 + 2, (u % 2) * TOK:(u % 2) * TOK + nk]
                if p < 6:
                    m = cst("moba_neg" if p < 3 else "dil_add")[:, P * qt:P * qt + nk]
                    dve.scalar_tensor_tensor(o, i, SCALE, m.unsqueeze(1).to_broadcast([P, 2, nk]), ALU.mult, ALU.add).then_inc(masked1, 1)
                else:
                    dve.tensor_scalar(o, i, SCALE, None, ALU.mult).then_inc(masked1, 1)
                peak(None, u, nk, 0, masked1, peak1)

            def turn1(u):
                nk, at = keys1(u), (u % 4) * 16
                dve.wait_ge(exp1, u + 1)
                link(dve.reciprocal(small[:, at + 4:at + 6], small[:, at + 2:at + 4]))
                sync()
                for m in range(2):
                    e = ex[:, u % 2, m * nk:(m + 1) * nk]
                    ins_ = dve.tensor_scalar(e, e, small[:, at + 4 + m:at + 5 + m], None, ALU.mult)
                ins_.then_inc(prob1, 1)

            for step in steps1:
                if step[0] == "drain":
                    drain1(step[1])
                elif step[0] == "split":
                    split_half(None, *step[1:])
                elif step[0] == "score1":
                    score1(step[1])
                elif step[0] == "turn1":
                    turn1(step[1])
            for p in range(0, PAIRS, 2):
                dve.wait_ge(out1_copied, 2 * p + 4)
                low(acts["o1T"][1][:, p:p + 2, :], o1T[:, p:p + 2, :], acts["o1T"][0][:, p:p + 2, :]).then_inc(o1_split, 1)
            dve.wait_ge(gate_ready, 12)
            for j in range(4):
                b = 4 * (j % 2)
                dve.wait_ge(multiplied, branch1_slot0 + j + 1)
                if j:
                    dve.wait_ge(mixed1, j)
                parts = [mT[:, 2 * j:2 * j + 2, :].rearrange("p a n -> p (a n)"), act_s[:, 0, :], act_s[:, 1, :]]
                for r in range(3):
                    e = wide[:, 8 * r + 2 * j:8 * r + 2 * j + 2, :].rearrange("p a n -> p (a n)")
                    ins_ = dve.tensor_tensor(parts[r], bank(b + r), e, ALU.mult)
                    if r < 2:
                        link(ins_)
                ins_.then_inc(branch1_free, 1)
                sync()
                link(dve.tensor_tensor(parts[0], parts[0], parts[1], ALU.add))
                sync()
                dve.wait_ge(branch1_free, j + 1)
                dve.tensor_tensor(parts[0], parts[0], parts[2], ALU.add).then_inc(mixed1, 1)
                split(None, branch1_slot0 + j + HIGHS)
                dve.wait_ge(m_hi, j + 1)
                k = slice(2 * j, 2 * j + 2)
                low(mT_lo[:, k, :], mT[:, k, :], xT_hi[:, k, :]).then_inc(m_split, 1)
            for slot in range(out1[0].slot0 + HIGHS, ffn0["slot0"] + 1):
                split(None, slot)

            def add_x(L, slots, s, last=None):
                dve.wait_ge(multiplied, lap(L, slots, SLOT_LAP))
                for t in range(T):
                    for n in range(2):
                        xv = x[:, t, n * BANK:(n + 1) * BANK]
                        dve.scalar_tensor_tensor(xv, bank(2 * n + t), s, xv, ALU.mult, ALU.add).then_inc(drained[2 * n + t], 1)
                    yield t

            for t in add_x(None, out1[1].slot0 + 2, 1.0):
                for b in (t, 2 + t):
                    dve.wait_ge(drained[b], out1[b // 2].need[b] + 1)
                dve.sem_inc(x_added, 1)
            rms_rows(x, 2)
            norm_cols(None, 2, conv1[:, N_CONV1 + 16:N_CONV1 + 24], None, xT, xT_hi, xT_lo)
            split(None, ffn0["slot0"] + 1)
            ffn_conv(ffn0)
            for t in add_x(None, ffn0["slot0"] + 3 * FFC, 1.0):
                for b in (t, 2 + t):
                    dve.wait_ge(drained[b], start[1][b])
                dve.sem_inc(hat_ready, 1)
            norm_cols(None, 3, None, None, xT, xT_hi, xT_lo)

            with dve.Fori(0, LAYERS) as L:
                chain.enter(L)

                def layer_norm(k, slots, s, free):
                    dve.wait_ge(x_ready, x_count(L, 2 * k))
                    for t in add_x(L, slots, s):
                        for b in (t, 2 + t):
                            dve.wait_ge(drained[b], lap(L, free[b], FREE_LAP[b]))
                        st = stats[:, t, :]
                        v = small[:, 96 + 4 * t:100 + 4 * t]
                        for n in range(2):
                            link(dve.bn_stats(st[:, 6 * n:6 * n + 6], x[:, t, n * BANK:(n + 1) * BANK]))
                        sync()
                        dve.memset(small[:, 250:251], 0.0)
                        link(dve.bn_aggr(v[:, 0:2], st))
                        sync()
                        ask_root(L, dve.tensor_scalar(v[:, 2:3], v[:, 1:2], LN_EPS / ALPHA ** 2, None, ALU.add))
                        dve.scalar_tensor_tensor(v[:, 3:4], v[:, 0:1], -1.0, v[:, 2:3], ALU.mult, ALU.mult).then_inc(stat_ready, 1)
                    g, b = ROWS2["ln_g"][k], ROWS2["ln_b"][k]
                    norm_cols(L, 4 + k, cols[:, g:g + 8], cols[:, b:b + 8], xT, xT_hi, xT_lo)

                def turn_rows():
                    dve.wait_ge(rows_turned, lap(L, 1, 1))
                    dve.wait_ge(xT_act, lap(L, 8, 6))
                    dve.wait_ge(xT_dve, lap(L, 8, 6))
                    link(dve.tensor_copy(cols[:, 0:N_ROWS2], ps[:, OB, 0:N_ROWS2]))
                    link(dve.tensor_copy(cols[:, P:P + N_CONV2], ps[:, OB, P:P + N_CONV2]))
                    sync()
                    g = ROWS2["gate_b"]
                    dve.tensor_scalar(small[:, 128:152], cols[:, g:g + 24], -1.0, None, ALU.mult).then_inc(cols_ready, 1)

                def drain(c):
                    p = c.pair
                    if c.name in ("qa", "ka"):
                        dst = qa if c.name == "qa" else ka
                        wait_products(dve, L, c)
                        for t in range(T):
                            dve.wait_ge(drained[2 * p + t], lap(L, c.need[2 * p + t] + 1, FREE_LAP[2 * p + t]))
                            i = bank(2 * p + t).rearrange("p (m d) -> p m d", d=HD)
                            o = dst[:, t, c.index * BANK:(c.index + 1) * BANK].rearrange("p (m d) -> p m d", d=HD)
                            a, r = (sm[:, n, t * TOK:t * TOK + P].rearrange("p (m d) -> p m d", d=16) for n in range(2))
                            cs = cst("cos")[:, 16 * t:16 * t + 16].unsqueeze(1).to_broadcast([P, 8, 16])
                            sn = cst("sin")[:, 16 * t:16 * t + 16].unsqueeze(1).to_broadcast([P, 8, 16])
                            link(dve.tensor_tensor(a, i[:, :, 0:16], cs, ALU.mult))
                            link(dve.tensor_tensor(r[:, :, 0:8], i[:, :, 8:16], sn[:, :, 0:8], ALU.mult))
                            link(dve.tensor_tensor(r[:, :, 8:16], i[:, :, 0:8], sn[:, :, 8:16], ALU.mult))
                            sync()
                            dve.tensor_tensor(o[:, :, 0:16], a, r, ALU.add).then_inc(drained[2 * p + t], 1)
                    elif c.name == "zb":
                        for j in range(2):
                            dve.wait_ge(z_exp, lap(L, 2 * c.index + j + 1, 4))
                            k = 4 * c.index + 2 * j
                            dve.tensor_tensor(zT[:, k:k + 2, :], tiles(2 * p + j), feats_of(conv_s[:, j, :]), ALU.mult).then_inc(drained[2 * p + j], 1)
                    elif c.name == "xbc":
                        for j in range(2):
                            dve.wait_ge(xbc_begun, lap(L, 2 * c.index + j + 1, 6))
                            for s in (1, 2, 3):
                                for f in range(2):
                                    k = P + (3 - s) * N_XBC + 4 * c.index + 2 * j + f
                                    o = conv_s[:, j, f * TOK + s:(f + 1) * TOK]
                                    ins_ = dve.scalar_tensor_tensor(o, tiles(2 * p + j)[:, f, 0:TOK - s], cols[:, k:k + 1], o, ALU.mult, ALU.add)
                                    if s < 3:
                                        link(ins_)
                                if s < 3:
                                    sync()
                            ins_.then_inc(drained[2 * p + j], 1)
                        for j in range(2):
                            dve.wait_ge(xbc_exp, lap(L, 2 * c.index + j + 1, 6))
                            k = 4 * c.index + 2 * j
                            dve.tensor_tensor(xbc[:, k:k + 2, :], feats_of(act_s[:, j, :]), feats_of(conv_s[:, j, :]), ALU.mult).then_inc(xbc_done, 1)
                    elif c.name in ("qc", "kc"):
                        wait_products(dve, L, c)
                        dst = qcT if c.name == "qc" else kcT
                        dve.tensor_copy(dst[:, 4 * c.index + 2:4 * c.index + 4, :], tiles(2 * p + 1)).then_inc(drained[2 * p + 1], 1)
                    elif c.name == "vc":
                        wait_products(dve, L, c)
                        dve.wait_ge(x_ready, x_count(L, 2))
                        dve.tensor_copy(vc[:, 1, c.index * BANK:(c.index + 1) * BANK], bank(2 * p + 1)).then_inc(drained[2 * p + 1], 1)
                    elif c.name == "branch":
                        wait_products(dve, L, c)
                        if c.r == 0 and c.index == 0:
                            dve.wait_ge(gate_ready, lap(L, 24, 12))
                        for j in range(2):
                            k = 4 * c.index + 2 * j
                            e = wide[:, 8 * c.r + k:8 * c.r + k + 2, :].rearrange("p a n -> p (a n)")
                            m = mT[:, k:k + 2, :].rearrange("p a n -> p (a n)")
                            b = 2 * p + j
                            dve.tensor_tensor(m if c.r == 0 else conv_s[:, j, :], bank(b), e, ALU.mult).then_inc(drained[b], 1)
                            if c.r:
                                dve.wait_ge(drained[b], lap(L, c.need[b] + 1, FREE_LAP[b]))
                                ins_ = dve.tensor_tensor(m, m, conv_s[:, j, :], ALU.add)
                                if c.r == 2:
                                    ins_.then_inc(mixed_sem, 1)
                                else:
                                    link(ins_)
                                    sync()
                        if c.r == 2:
                            for j in range(2):
                                k = slice(4 * c.index + 2 * j, 4 * c.index + 2 * j + 2)
                                dve.wait_ge(m_hi, lap(L, 4 + 2 * c.index + j + 1, 4))
                                low(mT_lo[:, k, :], mT[:, k, :], xT_hi[:, k, :]).then_inc(m_split, 1)

                def dt():
                    dve.wait_ge(par_loaded, lap(L, 5 * 16, 5 * 16))
                    lf = bcast[:, 0:4 * HD].rearrange("p (a b d) -> p a b d", a=2, b=2)
                    pr = dts[:, 0:4, :].rearrange("p a n -> p (a n)").rearrange("p (a d) -> p a d", d=HD)
                    link(dve.tensor_tensor(pr, lf[:, :, 0, :], lf[:, :, 1, :], ALU.mult))
                    sync()
                    dve.tensor_reduce(small[:, 160:162], pr, AX_X, ALU.add).then_inc(lam_arg, 1)
                    link(dve.tensor_copy(small[:, 168:170], const[:, bass.ds(L * 2 + CONST["lam"][0], 2)]))
                    sync()
                    dve.wait_ge(lam_exp, lap(L, 1, 1))
                    link(dve.tensor_tensor(small[:, 164:165], small[:, 163:164], small[:, 162:163], ALU.subtract))
                    link(dve.tensor_scalar(small[:, 166:167], cols[:, ROWS2["subln"]:ROWS2["subln"] + 1], small[:, 169:170], None, ALU.mult))
                    sync()
                    dve.tensor_tensor(small[:, 165:166], small[:, 164:165], small[:, 168:169], ALU.subtract).then_inc(lam_ready, 1)
                    for m in range(2):
                        link(dve.tensor_copy(small[HD * m:HD * (m + 1), 168 + 32:176 + 32], bcast[HD * m:HD * (m + 1), 288 + m:304:2]))
                    dve.wait_ge(dt_ready, lap(L, 1, 1))
                    two = lambda n: dts[:, n, :].rearrange("p (t h) -> p t h", t=T)
                    over_t = lambda a: a.unsqueeze(1).to_broadcast([P, T, NH])
                    link(dve.tensor_tensor(two(0), ps[:, OB, 0:T * NH].rearrange("p (t h) -> p t h", t=T), over_t(bcast[:, 256:272]), ALU.add))
                    sync()
                    dve.scalar_tensor_tensor(dts[:, 1, :], dts[:, 0, :], -1.0, dts[:, 0, :], ALU.mult, ALU.max).then_inc(dt_arg, 1)
                    dve.wait_ge(dt_log, lap(L, 1, 1))
                    link(dve.scalar_tensor_tensor(dts[:, 2, :], dts[:, 0, :], 0.0, dts[:, 3, :], ALU.max, ALU.add))
                    sync()
                    dve.scalar_tensor_tensor(two(4), two(2), -1.0, over_t(dts[:, 5, 0:NH]), ALU.mult, ALU.mult).then_inc(dt_done, 1)

                def turn_qk(j):
                    if j % 2:
                        dve.wait_ge(k_turned, lap(L, j // 2 + 1, 4))
                        dve.tensor_copy(kT[:, j - 1:j + 1, :], tiles(OB)).then_inc(k_copied, 1)

                def dscore(u):
                    qt = u % 2
                    nk = P * (1 + qt)
                    dve.wait_ge(d_score, lap(L, u + 1, 2 * DH))
                    if u >= 2:
                        dve.wait_ge(d_exp, lap(L, u - 1, 2 * DH))
                    o = sm[:, u % 2, 0:2 * nk].rearrange("p (m k) -> p m k", k=nk)
                    i = ps[:, S0:S0 + 2, (u % 2) * TOK:(u % 2) * TOK + nk]
                    m = cst("chunk_neg")[:, P * qt:P * qt + nk].unsqueeze(1).to_broadcast([P, 2, nk])
                    dve.scalar_tensor_tensor(o, i, SCALE, m, ALU.mult, ALU.add).then_inc(d_masked, 1)
                    peak(L, u, nk, 2 * DH, d_masked, d_peak)

                def dturn(u):
                    nk, at = P * (1 + u % 2), (u % 4) * 16
                    dve.wait_ge(d_exp, lap(L, u + 1, 2 * DH))
                    if u == 0:
                        dve.wait_ge(lam_ready, lap(L, 1, 1))
                    e0, e1 = (ex[:, u % 2, m * nk:(m + 1) * nk] for m in range(2))
                    link(dve.reciprocal(small[:, at + 4:at + 6], small[:, at + 2:at + 4]))
                    sync()
                    link(dve.tensor_scalar(e0, e0, small[:, at + 4:at + 5], None, ALU.mult))
                    link(dve.tensor_tensor(small[:, at + 6:at + 7], small[:, at + 5:at + 6], small[:, 165:166], ALU.mult))
                    sync()
                    dve.scalar_tensor_tensor(e0, e1, small[:, at + 6:at + 7], e0, ALU.mult, ALU.add).then_inc(d_w, 1)

                def dnorm(_):
                    r = small[:, 184:184 + 2 * DH]
                    dve.wait_ge(d_sq, lap(L, 2 * DH, 2 * DH))
                    ask_root(L, dve.tensor_scalar(r, r, 1.0 / P, LN_EPS, ALU.mult, ALU.add))
                    for t in range(T):
                        o = oA[:, t, :].rearrange("p (h d) -> p h d", d=P)
                        dve.tensor_tensor(o, o, r[:, t * DH:(t + 1) * DH].unsqueeze(2).to_broadcast([P, DH, P]), ALU.mult).then_inc(d_norm, 1)

                def turn_oa(j):
                    dve.wait_ge(oa_copied, lap(L, j + 1, 4))
                    k = slice(2 * j, 2 * j + 2)
                    low(qT_r[:, k, :], qT[:, k, :], kT_r[:, k, :]).then_inc(oa_split, 1)

                def bsplit(g):
                    k = slice(4 * g, 4 * g + 4)
                    dve.wait_ge(ob_hi, lap(L, g + 1, 2))
                    low(zT_lo[:, k, :], zT[:, k, :], xbc_r[:, k, :]).then_inc(ob_split, 1)

                def osplit(u):
                    if u % 2:
                        p = u // 2
                        dve.wait_ge(s_copied, lap(L, p + 1, NH // 2))
                        low(qcT_r[:, p, :], qcT[:, p, :], kcT_r[:, p, :]).then_inc(oc_split, 1)

                def cb(g):
                    dve.wait_ge(cb_ready, lap(L, g + 1, 2))
                    dve.tensor_tensor(cbm[:, g, :], ps[:, S0 + g, 0:CAUS], cst("causal"), ALU.mult).then_inc(cb_masked, 1)

                def sdecay(u):
                    dve.wait_ge(seg_exp, lap(L, u + 1, NH))
                    if u == 0:
                        dve.wait_ge(cb_masked, lap(L, 2, 2))
                    if u >= 2:
                        dve.wait_ge(y_ready, lap(L, u - 1, NH))
                    g = u // (NH // 2)
                    for t, r in enumerate((slice(0, TOK), slice(TOK, CAUS))):
                        ins_ = dve.scalar_tensor_tensor(lmat[:, u % 2, r], ex[:, u % 2, r], dts[:, 2, t * NH + u:t * NH + u + 1],
                                                        cbm[:, g, r], ALU.mult, ALU.mult)
                    ins_.then_inc(l_ready, 1)

                def sout(u):
                    if u % 2:
                        p = u // 2
                        dve.wait_ge(y_ready, lap(L, u + 1, NH))
                        d = small[:, 200 + p:201 + p]
                        s = sm[:, p % 2, 0:TOK]
                        link(dve.scalar_tensor_tensor(s, xbc[:, p, :], d, ps[:, TB + p % 2, 0:TOK], ALU.mult, ALU.add))
                        sync()
                        dve.tensor_tensor(zT[:, p, :], s, zT[:, p, :], ALU.mult).then_inc(y_gated, 1)

                def snorm(g):
                    dve.wait_ge(y_root, lap(L, g + 1, 2))
                    r = sm[:, g, 0:TOK]
                    for k in range(4 * g, 4 * g + 4):
                        w = cols[:, ROWS2["norm"] + k:ROWS2["norm"] + k + 1]
                        ins_ = dve.scalar_tensor_tensor(zT[:, k, :], zT[:, k, :], w, r, ALU.mult, ALU.mult)
                    ins_.then_inc(o_b, 1)

                def kscore(u):
                    z = sm[:, u % 2, 0:CAUS]
                    if u == 0:
                        dve.wait_ge(o_b, lap(L, 2, 2))
                    dve.wait_ge(s_score, lap(L, u + 1, NH))
                    if u >= 2:
                        dve.wait_ge(s_exp, lap(L, u - 1, NH))
                        dve.wait_ge(s_sum, lap(L, u - 1, NH))
                    dve.scalar_tensor_tensor(z, ps[:, S0 + u % 2, 0:CAUS], SCALE, cst("strict_neg"), ALU.mult, ALU.add).then_inc(s_masked, 1)
                    dve.wait_ge(s_masked, lap(L, u + 1, NH))
                    dve.scalar_tensor_tensor(lmat[:, u % 2, :], z, -1.0, z, ALU.mult, ALU.max).then_inc(s_abs, 1)

                def ksoft(u):
                    dve.wait_ge(s_log, lap(L, u + 1, NH))
                    b = lmat[:, u % 2, :]
                    dve.scalar_tensor_tensor(b, sm[:, u % 2, 0:CAUS], 0.0, b, ALU.max, ALU.add).then_inc(s_soft, 1)

                def ksum(u):
                    z = sm[:, u % 2, 0:CAUS]
                    dve.wait_ge(s_sum, lap(L, u + 1, NH))
                    dve.tensor_tensor(z, z, ps[:, TB, 0:CAUS], ALU.subtract).then_inc(s_arg, 1)

                attention = dict(turn_qk=turn_qk, dscore=dscore, dturn=dturn, dnorm=dnorm, cb=cb, sdecay=sdecay, sout=sout,
                                 turn_oa=turn_oa, bsplit=bsplit, osplit=osplit, snorm=snorm, kscore=kscore, ksoft=ksoft, ksum=ksum, drain=drain)
                for slot in range(HIGHS):
                    split(L, ffn1["slot0"] + slot)
                ffn_mul(L, ffn1)
                turn_rows()
                layer_norm(0, ffn1["slot0"] + 3 * FFC, FFN_RES / ALPHA, ffn1["after"])
                split(L, mix[0].slot0 + 1)
                for step in mixed:
                    if step[0] == "dt":
                        dt()
                    elif step[0] == "split":
                        split_half(L, *step[1:])
                    elif step[0] in attention:
                        attention[step[0]](step[1])
                for slot in range(out2[0].slot0 + HIGHS, ffn2["slot0"] + 1):
                    split(L, slot)
                layer_norm(1, out2[1].slot0 + 2, 1 / ALPHA, out2[1].after)
                split(L, ffn2["slot0"] + 1)
                ffn_mul(L, ffn2)
                layer_norm(2, ffn2["slot0"] + 3 * FFC, FFN_RES / ALPHA, list(plan.free))
                chain.leave()

        @block.gpsimd
        def _(pool):
            chain = Chain(pool, pool_chain)
            link, sync = chain.link, chain.sync
            pool.sem_inc(x_ready, 1)
            rows1 = wide[:, 0:2, :].rearrange("p a (b n) -> p (a b) n", n=P)
            cw = ins["ffn_conv_w"][0].rearrange("j (a b) -> (j a) b", b=P)
            pool.dma_start(rows1[0:88, 0, :], cw[0:88, :]).then_inc(rows1_loaded, 16)
            pool.dma_start(rows1[0:44, 1, :], cw[88:132, :]).then_inc(rows1_loaded, 16)
            for name, key, n in (("mix_norm_g", "mix", 8), ("mem_norm_g", "mem", 8), ("ffn_norm_g", "ffn", 8), ("ffn_conv_b", "conv_b", 44)):
                pool.dma_start(rows1[ROWS1[key]:ROWS1[key] + n, 2, :], ins[name][0].rearrange("(a b) -> a b", b=P)).then_inc(rows1_loaded, 16)
            with nc.allow_non_contiguous_dma(reason="256 positions, one per partition"):
                for t in range(T):
                    pool.dma_start(pos[:, t:t + 1], ins["positions"][0, t * P:(t + 1) * P].unsqueeze(1)).then_inc(par1_loaded, 16)
            for i, name in enumerate(("moba_q_norm_g", "moba_k_norm_g", "dil_q_norm_g", "dil_k_norm_g", "mem_q_norm_g", "mem_k_norm_g")):
                pool.dma_start(gains1[:, i * HD:(i + 1) * HD], ins[name][0:1, :].to_broadcast([P, HD])).then_inc(par1_loaded, 16)

            roots = [0]

            def root(L, a):
                roots[0] += 1
                pool.wait_ge(root_asked, lap(L, roots[0], ROOTS_LAP))
                n = a.shape[-1]
                pool.tensor_tensor(a, a, cst("minus_half").to_broadcast([P, n]), ALU.pow).then_inc(root_done, 1)

            pool.wait_ge(in_loaded, 4 * 16)
            for event in range(2):
                for t in range(T):
                    root(None, small[:, 64 + 2 * event + t:65 + 2 * event + t])
            for step in steps1:
                if step[0] == "drain" and step[1].name == "tok":
                    for t in range(T):
                        root(None, small[:, 84:84 + NORMED[step[1].index][1]])
            for t in range(T):
                root(None, small[:, 64 + 4 + t:65 + 4 + t])
            with pool.Fori(0, LAYERS) as L:
                chain.enter(L)

                def residual(k):
                    for t in range(T):
                        root(L, small[:, 98 + 4 * t:99 + 4 * t])
                    pool.wait_ge(gb_loaded, lap(L, 32 * (k + 1), 96))
                    for t in range(T):
                        pool.wait_ge(hat_ready, lap(L, 2 * (4 + k) + t + 1, 6))
                        link(pool.tensor_tensor(x[:, t, :], xhat[:, t, :], gb[:, 0, :], ALU.mult))
                        sync()
                        pool.tensor_tensor(x[:, t, :], x[:, t, :], gb[:, 1, :], ALU.add).then_inc(x_ready, 1)

                def sdecay(u):
                    if u == 0:
                        pool.wait_ge(dt_done, lap(L, 1, 1))
                        pool.wait_ge(xbc_done, lap(L, 6, 6))
                    if u >= 2:
                        pool.wait_ge(seg_ready, lap(L, u - 1, NH))
                    for n, (m, t) in enumerate(((after, 0), (after, 1), (ones, 1))):
                        ins_ = pool.tensor_tensor(seg_w[:, u % 2, n * P:(n + 1) * P], m,
                                                  dts[:, 4, t * NH + u:t * NH + u + 1].to_broadcast([P, P]), ALU.mult)
                    ins_.then_inc(seg_built, 1)

                residual(0)
                for step in mixed:
                    if step[0] == "sdecay":
                        sdecay(step[1])
                    elif step[0] == "dnorm":
                        root(L, small[:, 184:184 + 2 * DH])
                residual(1)
                residual(2)
                chain.leave()
            pool.wait_ge(x_ready, x_count(LAYERS, 0))
            pool.dma_start(out[0].rearrange("(t p) n -> p t n", p=P), x[:, :, :]).then_inc(out_stored, 16)
            pool.wait_ge(out_stored, 16)

    return nc


INPUTS = ["x", "mem", "positions", "mix_norm_g", "mem_norm_g", "w_in", "moba_q_norm_g", "moba_k_norm_g", "dil_q_norm_g",
          "dil_k_norm_g", "mem_q_norm_g", "mem_k_norm_g", "w_mem_kv", "w_branch_moba", "w_branch_dil", "w_branch_mem", "w_out",
          "ffn_norm_g", "w_ffn_up", "ffn_conv_w", "ffn_conv_b", "w_ffn_down", "ffn1_w_in_2", "ffn1_w_out_2", "ln1_g_2",
          "ln1_b_2", "w_mix_in_2", "gate_bias_2", "diff_lambda_2", "diff_subln_g_2", "ssm_conv_w_2", "ssm_conv_b_2",
          "ssm_dt_bias_2", "ssm_A_log_2", "ssm_D_2", "ssm_norm_g_2", "w_branch_2", "w_mix_out_2", "ln2_g_2", "ln2_b_2",
          "ffn2_w_in_2", "ffn2_w_out_2", "ln3_g_2", "ln3_b_2"]


def kernel(**inputs):
    import concourse.bacc as bacc
    from concourse.bass_utils import run_bass_kernel_spmd

    nc = bacc.Bacc("TRN2", target_bir_lowering=False, num_devices=1)
    arrays, aps = {}, {}
    for name in INPUTS:
        a = np.ascontiguousarray(inputs[name])
        arrays["in_" + name] = a
        aps[name] = nc.dram_tensor("in_" + name, a.shape, mybir.dt.from_np(a.dtype), kind="ExternalInput").ap()
    arrays["const_table"] = constants()
    aps["const"] = nc.dram_tensor("const_table", (P, CONST_ALL), F32, kind="ExternalInput").ap()
    out = nc.dram_tensor("out", (1, TOK, D), F32, kind="ExternalOutput").ap()
    program(nc, aps, out)
    return run_bass_kernel_spmd(nc, [arrays], core_ids=[0]).results[0]["out"]
```

```python
from contextlib import ExitStack

import numpy as np

import concourse.bass as bass
from concourse import mybir

ALU = mybir.AluOpType
ACT = mybir.ActivationFunctionType
F32 = mybir.dt.float32
F32R = mybir.dt.float32r
I32 = mybir.dt.int32
AX_X = mybir.AxisListType.X

P = 128
D = 1024
TOK = 256
T = TOK // P
KD = D // P
FF = 2816
KF = FF // P
FFC = KF // 2
HD = 64
BANK = 512
LAYERS = 2
SLOTS = 4
HIGHS = 2
HALVES = 2
PARTS = 2 * HALVES
SLOT = 2048
RATE1, RATE2 = 1.0, 0.9
ALPHA = (2 * LAYERS) ** 0.25
FFN_RES = 0.5
RMS_EPS = 1e-6
LN_EPS = 1e-5
SCALE = HD ** -0.5
NEG = -1e30

QKV1 = 2560
GATE1 = QKV1
TOKW = 3072
NORMED = [(0, 6, 0, True), (384, 6, 1, True), (1152, 6, 2, True), (1536, 6, 3, True),
          (2304, 4, 4, False), (2560, 4, 5, False)]
Q_COL = [0, 128, 256, 1152, 1280, 1408, 2304, 2432]
K_COL = [384, 512, 640, 1536, 1664, 1792, 2560, 2688]
V_COL = [768, 896, 1024, 1920, 2048, 2176, 2816, 2944]
PAIRS = 8
BRANCH_TILES = (3, 3, 2)

MIX = dict(qa=0, ka=1024, va=2048, zb=3072, xbc=4096, dt=5632, qc=5648, kc=6672, vc=7696, gate=8720)
NH = 16
DH = 8
N_XBC = 12
CAUS = 384

CONST = {}
_at = 0
for _name, _n in (("ident", 128), ("ones", 128), ("after", 128), ("from_on", 128),
                  ("strict_neg", CAUS), ("causal", CAUS), ("chunk_far", CAUS), ("cos", T * 16), ("sin", T * 16),
                  ("freq", 32), ("lam", 4), ("minus_half", 1), ("ln_eps", 1), ("moba_far", CAUS), ("dil_far", CAUS)):
    CONST[_name] = (_at, _at + _n)
    _at += _n
CONST_ALL = _at
CONST_W = CONST["moba_far"][0]

ROWS1 = dict(mix=0, mem=8, ffn=16, conv_b=24)
N_ROWS1 = 68
N_CONV1 = 3 * 2 * KF
ROWS2 = dict(ln_g=(0, 16, 32), ln_b=(8, 24, 40), gate_b=48, norm=72, subln=80)
N_ROWS2 = 81
N_CONV2 = 5 * N_XBC


def constants():
    i = np.arange(P)[:, None]
    j = np.arange(P)[None, :]
    t = np.arange(TOK)[None, :]
    c = np.zeros((P, CONST_ALL), np.float32)

    def put(name, a):
        c[:, CONST[name][0]:CONST[name][1]] = a

    def queries(rule):
        return np.concatenate([rule(i, j), rule(i + P, t)], axis=1)

    def keys(rule):
        return np.concatenate([rule(i, t), rule(i, j)], axis=1)

    put("ident", i == j)
    put("ones", 1.0)
    put("after", i > j)
    put("from_on", i >= j)
    put("strict_neg", keys(lambda k, q: np.where(k < q, 0.0, NEG)))
    put("causal", keys(lambda k, q: k <= q))
    put("chunk_far", queries(lambda q, k: np.where(k // HD <= q // HD, 0.0, -NEG)))
    put("moba_far", queries(lambda q, k: np.where(k <= q, 0.0, -NEG)))

    def dilated(q, k):
        n = (k <= q) * ((q - k <= 128) * 1 + ((q - k) % 4 == 0) * 1 + ((q - k) % 16 == 0) * 1)
        return np.where(n > 0, -np.log(np.maximum(n, 1)), -NEG)

    put("dil_far", queries(dilated))
    half = 8
    inv = (np.float32(500000.0) ** (-np.arange(half, dtype=np.float32) * np.float32(2.0) / np.float32(16))).astype(np.float32)
    ang = (np.arange(TOK, dtype=np.float32)[:, None] * inv[None, :]).astype(np.float32)
    for name, f in (("cos", np.cos), ("sin", np.sin)):
        v = f(ang).astype(np.float32).reshape(T, P, half).transpose(1, 0, 2)
        first = -v if name == "sin" else v
        put(name, np.concatenate([first, v], axis=2).reshape(P, T * 16))
    put("freq", np.float32(10000.0) ** (-np.arange(32, dtype=np.float32) / np.float32(32)))
    lam = [0.8 - 0.6 * np.exp(-0.3 * layer) for layer in range(LAYERS)]
    put("minus_half", -0.5)
    put("ln_eps", LN_EPS)
    put("lam", np.array([[lam[0], 1 - lam[0], lam[1], 1 - lam[1]]]))
    return c



class Chunk:

    def __init__(self, name, index, mode, srcs, act, pair, evacs=1):
        self.name, self.index, self.mode, self.srcs, self.act = name, index, mode, srcs, act
        self.pair, self.evacs = pair, evacs
        self.event = None
        self.tail = False


class Plan:

    def __init__(self):
        self.slot = 0
        self.hidden = 0
        self.free = [0, 0, 0, 0]

    def chunk(self, c):
        c.slot0 = self.slot
        c.slots = (self.slot, self.slot + 1)
        self.slot += 2
        c.need = {b: self.free[b] for b in (2 * c.pair, 2 * c.pair + 1)}
        for b in c.need:
            self.free[b] += c.evacs
        return c

    def out(self, chunks):
        a, b = (self.chunk(c) for c in chunks)
        s = a.slot0
        a.slots, b.slots = (s, s + 2), (s + 1, s + 3)
        b.tail = True
        return [a, b]

    def ffn(self, f):
        f["slot0"], f["free0"], f["h0"] = self.slot, list(self.free), self.hidden
        self.hidden += FFC
        self.slot += 3 * FFC
        f["ahead"] = 1 if f["index"] == 0 else 0
        self.free = [n + FFC // 2 + (1 if b < 2 else 0) for b, n in enumerate(self.free)]
        return f


def beats_of(n, stages, lags):
    return [[(s, i - lag) for s, lag in zip(stages, lags) if 0 <= i - lag < n]
            for i in range(n + max(lags))]


def woven(chunks, beats, first, rate, end):
    steps, done, halves, prev = [], 0, 0, None
    for n, c in enumerate(chunks):
        for part in range(PARTS):
            h, q = part // HALVES, part % HALVES
            steps.append(("half", c, h, q))
            turn = []
            if n >= first:
                halves += 1
                while done < len(beats) and done < rate * halves:
                    turn += beats[done]
                    done += 1
            s = c.slot0 + h + HIGHS
            steps += turn[:-1] + ([("split", s, q)] if s < end else []) + turn[-1:]
            if prev is not None:
                steps.append(("drain", prev, part))
        prev = c
    return steps + [("drain", prev, part) for part in range(PARTS)], beats[done:]


def split_later(steps):
    order, moved = list(steps), set()
    for i in range(len(order) - 1):
        if order[i][0] == "split" and i not in moved and order[i + 1][0] not in ("half", "drain", "split"):
            order[i], order[i + 1] = order[i + 1], order[i]
            moved.add(i + 1)
    return order


def plan_block1(plan):
    chunks = [Chunk("tok", n, "A", [("w_in", h, n * BANK) for h in range(2)], "xT", n % 2) for n in range(5)]
    chunks += [Chunk("tok", 5, "A", [("w_mem_kv", h, 0) for h in range(2)], "memT", 1)]
    chunks += [Chunk("gate1", n, "B", [("w_in", None, GATE1 + n * BANK + h * TOK) for h in range(2)], "xT", n % 2)
               for n in range(6)]
    head = [plan.chunk(c) for c in chunks]
    head[0].event = 1
    beats = [[("pair1", p), ("pair1", p + 1)] for p in range(0, PAIRS, 2)]
    beats += beats_of(2 * PAIRS, ("out1", "weigh1", "turn1", "score1"), (3, 1, 2, 0))
    return head, beats


def plan_layer(plan):
    def a(name, n, pair, evacs=1, w="w_mix_in_2", act="xT"):
        return Chunk(name, n, "A", [(w, h, MIX.get(name, 0) + n * BANK) for h in range(2)], act, pair, evacs)

    def b(name, n, pair, w="w_mix_in_2", act="xT"):
        return Chunk(name, n, "B", [(w, None, MIX.get(name, 0) + n * BANK + h * TOK) for h in range(2)], act, pair)

    jobs = [(a, "qa", n, 2) for n in range(2)] + [(a, "ka", n, 2) for n in range(2)] + [(b, "xbc", n) for n in range(2)]
    jobs += [(a, "va", n, 1) for n in range(2)] + [(b, "xbc", 2)] + [(b, "gate", n) for n in range(4)] + [(b, "zb", n) for n in range(2)]
    for n in range(2):
        jobs += [(b, "qc", n), (b, "kc", n), (a, "vc", n, 1)]
    jobs += [(b, "gate", n) for n in (4, 5)]
    ffn1 = plan.ffn({"index": 0})
    mix = [plan.chunk(j[0](j[1], j[2], i % 2, *j[3:])) for i, j in enumerate(jobs)]
    mix[0].event = 5
    for r, act in enumerate(("oAT", "oBT", "oCT")):
        for n in range(2):
            c = b("branch", n, (len(mix)) % 2, w=("w_branch_2", r), act=act)
            c.r = r
            mix.append(plan.chunk(c))
    out = plan.out(a("out", n, 1 - n, w="w_mix_out_2", act="mT") for n in range(2))
    out[1].after = list(plan.free)
    ffn2 = plan.ffn({"index": 1})
    return ffn1, mix, out, ffn2


def mixer_steps(mix, end):
    beats = [[("turn_qk", 2 * j), ("turn_qk", 2 * j + 1)] for j in range(4)]
    beats += beats_of(2 * DH, ("dout", "dweigh", "dturn", "dscore"), (3, 1, 2, 0))
    beats += [[("dnorm", 0)]]
    beats += [[("turn_xs", 0), ("turn_xs", 1)], [("turn_xs", 2), ("turn_xs", 3)]]
    beats += [[("turn_oa", 0), ("turn_oa", 1)], [("turn_oa", 2), ("turn_oa", 3)], [("cb", 0), ("cb", 1)]]
    beats += beats_of(NH, ("sout", "sdecay"), (2, 0))
    beats += [[("ysquare", 0)], [("snorm", 0), ("ysquare", 1)], [("snorm", 1)]]
    tail = beats_of(NH, ("osplit", "kout", "ksum", "ksoft", "kscore"), (4, 3, 2, 1, 0))
    tail[1].append(("bsplit", 0))
    tail[1].append(("bsplit", 1))
    beats += tail
    steps, rest = woven(mix, beats, 7, RATE2, end)
    assert not rest
    steps.insert(steps.index(("half", mix[6], 0, 0)), ("dt",))

    def before(a, b):
        assert steps.index(a) < steps.index(b), (a, b)

    z = [c for c in mix if c.name == "zb"]
    qc, kc, vc, branch = ([c for c in mix if c.name == name] for name in ("qc", "kc", "vc", "branch"))
    for n in range(2):
        before(("drain", qc[n], 0), ("kscore", NH // 2 * n))
        before(("drain", kc[n], 0), ("kscore", NH // 2 * n))
        before(("drain", vc[n], 0), ("kout", NH // 2 * n))
    before(("drain", [c for c in mix if c.name == "va"][1], 0), ("dout", 0))
    before(("drain", [c for c in mix if c.name == "xbc"][2], 3), ("turn_xs", 0))
    before(("dout", 2 * DH - 1), ("drain", z[0], 1))
    before(("drain", z[0], 1), ("sout", 1))
    before(("drain", z[1], 1), ("sout", NH // 2 + 1))
    before(("sout", NH - 1), ("drain", branch[0], 0))
    for b, last in ((0, ("turn_oa", 3)), (2, ("bsplit", 1)), (4, ("osplit", NH - 1))):
        before(last, ("half", branch[b], 0, 0))
    return steps


def program(nc, ins, out):
    plan = Plan()
    head1, beats1 = plan_block1(plan)
    branch1_slot0 = plan.slot
    plan.slot += 4
    out1 = plan.out(Chunk("out1", n, "A", [("w_out", h, n * BANK) for h in range(2)], "mT", n) for n in range(2))
    ffn0 = plan.ffn({"index": None})
    start = (plan.slot, list(plan.free))
    ffn1, mix, out2, ffn2 = plan_layer(plan)
    SLOT_LAP = plan.slot - start[0]
    FREE_LAP = [n - m for n, m in zip(plan.free, start[1])]
    assert SLOT_LAP % SLOTS == 0
    steps1, rest1 = woven(head1, beats1, 6, RATE1, out1[0].slot0)
    steps1 += [step for beat in rest1 for step in beat]
    for step, chunk, part in (("angles", 0, 1), ("rotations", 0, 3), ("memory", 3, 1)):
        steps1.insert(steps1.index(("half", head1[chunk], part // HALVES, part % HALVES)) - 1, (step,))
    mixed = mixer_steps(mix, out2[0].slot0 + 2)

    ctx = ExitStack()
    with ctx:
        def sb(name, shape, dt=F32):
            return ctx.enter_context(nc.sbuf_tensor(name, shape, dt))

        def sem(name):
            return ctx.enter_context(nc.semaphore(name))

        def both(name, shape):
            with nc.sbuf_tensor(name, shape, F32) as plain:
                pass
            return plain, sb(name + "_r", shape, F32R)

        ring, ring_lo = both("ring", [P, SLOTS, SLOT])
        ring_hi = sb("ring_hi", [P, HIGHS, SLOT], F32R)
        const = sb("const", [P, CONST_W])
        x = sb("x", [P, T, D])
        xT_hi = sb("xT_hi", [P, KD, TOK], F32R)
        xT, xT_lo = both("xT", [P, KD, TOK])
        wide, wide_r = both("wide", [P, 24, TOK])
        tok, tok_r = both("tok", [P, 3 * T * D])
        qT, qT_r = both("qT", [P, KD, TOK])
        kT, kT_r = both("kT", [P, KD, TOK])
        xbc, xbc_r = both("xbc", [P, N_XBC, TOK])
        qcT, qcT_r = both("qcT", [P, KD, TOK])
        kcT, kcT_r = both("kcT", [P, KD, TOK])
        vc_, vc_r = both("vc", [P, T * D])

        def rows_of(a):
            return a.rearrange("p (t n) -> p t n", t=T)

        def feats_of(a):
            return a.rearrange("p (k n) -> p k n", n=TOK)

        vc = rows_of(vc_[:, :])
        xhat = vc
        gb = qT[:, :, :].rearrange("p a n -> p (a n)").rearrange("p (t n) -> p t n", t=2)
        tok1 = tok[:, :].rearrange("p (t n) -> p t n", t=T)
        qa, ka, va = (rows_of(tok[:, i * T * D:(i + 1) * T * D]) for i in range(3))
        oA, xs = qa, ka
        mT, zT = (feats_of(tok[:, i * T * D:(i + 1) * T * D]) for i in (1, 2))
        mT_lo, zT_lo = (feats_of(tok_r[:, i * T * D:(i + 1) * T * D]) for i in (1, 2))
        h2, h2_lo, h2_hi = feats_of(tok[:, 0:KF * TOK]), feats_of(tok_r[:, 0:KF * TOK]), wide_r[:, 0:KF, :]
        o1T = feats_of(vc_[:, :])
        memT = wide[:, 16:24, :]
        acts = {"xT": (xT_hi, xT_lo), "memT": (xbc_r[:, 0:KD, :], wide_r[:, 16:24, :]), "o1T": (xbc_r[:, 0:KD, :], feats_of(vc_r[:, :])),
                "oAT": (kT_r, qT_r), "oBT": (xbc_r[:, 0:KD, :], zT_lo), "oCT": (kcT_r, qcT_r), "mT": (xT_hi, mT_lo)}
        const1 = xbc[:, KD:KD + 3, :].rearrange("p a n -> p (a n)")
        gains1 = qcT[:, 4:6, :].rearrange("p a n -> p (a n)")[:, 0:6 * HD]
        act_s = sb("act_s", [P, 2, BANK])
        conv_s = sb("conv_s", [P, 2, BANK])
        sm = sb("sm", [P, 2, BANK])
        ex = sb("ex", [P, 2, BANK])
        wt = sb("wt", [P, 2, BANK])
        lmat, cbm = (tok[:, i * 2 * CAUS:(i + 1) * 2 * CAUS].rearrange("p (a n) -> p a n", a=2) for i in range(2))
        seg_w = act_s[:, :, 0:3 * P]
        small = sb("small", [P, 256])
        cols = sb("cols", [P, 256])
        rows = sb("rows", [P, 2, P])
        bcast = sb("bcast", [P, 4 * HD + 3 * NH])
        dtw = sb("dtw", [P, KD, NH])
        dts = sb("dts", [P, 6, T * NH])
        conv1 = sb("conv1", [P, N_CONV1 + N_ROWS1])
        stats = sb("stats", [P, T, 12])
        act_j = sb("act_j", [P, P])
        pos = sb("pos", [P, T], I32)
        ps = ctx.enter_context(nc.psum_tensor("ps", [P, 8, BANK], F32))
        S0, S1, TB, OB = 4, 5, 6, 7
        DOWN = 4

        def cst(name):
            a, b = CONST[name]
            return const[:, a:b] if b <= CONST_W else const1[:, a - CONST_W:b - CONST_W]

        ident, ones, after, from_on = (cst(n) for n in ("ident", "ones", "after", "from_on"))
        upto = cst("causal")[:, 0:TOK]

        w_loaded = [sem(f"w_loaded{i}") for i in range(SLOTS)]
        drained = [sem(f"drained{b}") for b in range(4)]
        multiplied, in_loaded, par1_loaded, par_loaded, rows1_loaded = (sem(n) for n in ("multiplied", "in_loaded", "par1_loaded", "par_loaded", "rows1_loaded"))
        rows_loaded, gb_loaded, rows1_turned, rows_turned, cols_ready = (sem(n) for n in ("rows_loaded", "gb_loaded", "rows1_turned", "rows_turned", "cols_ready"))
        sq_ready, stat_ready, hat_ready, hat_turned, xT_act = (sem(n) for n in ("sq_ready", "stat_ready", "hat_ready", "hat_turned", "xT_act"))
        xT_dve, x_ready, x_added, conv_begun, conv_tap = (sem(n) for n in ("xT_dve", "x_ready", "x_added", "conv_begun", "conv_tap"))
        act_ready, h_ready, dve_chain, act_chain, pool_chain = (sem(n) for n in ("act_ready", "h_ready", "dve_chain", "act_chain", "pool_chain"))
        angle_ready, sin_ready, norm1_done, pair1_turned, pair1_copied = (sem(n) for n in ("angle_ready", "sin_ready", "norm1_done", "pair1_turned", "pair1_copied"))
        score1_ready, masked1, peak1, exp1, prob1 = (sem(n) for n in ("score1_ready", "masked1", "peak1", "exp1", "prob1"))
        prob1_turned, prob1_copied, out1_ready, out1_copied, branch1_free = (sem(n) for n in ("prob1_turned", "prob1_copied", "out1_ready", "out1_copied", "branch1_free"))
        mixed1, q_turned, q_copied, k_turned, k_copied = (sem(n) for n in ("mixed1", "q_turned", "q_copied", "k_turned", "k_copied"))
        d_score, d_masked, d_peak, d_exp, d_w = (sem(n) for n in ("d_score", "d_masked", "d_peak", "d_exp", "d_w"))
        d_turned, d_copied, d_out, d_sq, d_norm = (sem(n) for n in ("d_turned", "d_copied", "d_out", "d_sq", "d_norm"))
        oa_turned, oa_copied, lam_arg, lam_exp, lam_ready = (sem(n) for n in ("oa_turned", "oa_copied", "lam_arg", "lam_exp", "lam_ready"))
        dt_ready, dt_arg, dt_log, dt_done, z_exp = (sem(n) for n in ("dt_ready", "dt_arg", "dt_log", "dt_done", "z_exp"))
        xbc_begun, xbc_exp, xbc_done, xs_turned, xs_copied = (sem(n) for n in ("xbc_begun", "xbc_exp", "xbc_done", "xs_turned", "xs_copied"))
        cb_ready, cb_masked, seg_built, seg_ready, seg_exp = (sem(n) for n in ("cb_ready", "cb_masked", "seg_built", "seg_ready", "seg_exp"))
        l_ready, y_ready, y_gated, y_sq, y_sum = (sem(n) for n in ("l_ready", "y_ready", "y_gated", "y_sq", "y_sum"))
        o_b, s_score, s_masked, s_abs, s_log = (sem(n) for n in ("o_b", "s_score", "s_masked", "s_abs", "s_log"))
        s_soft, s_sum, s_arg, s_exp, s_out = (sem(n) for n in ("s_soft", "s_sum", "s_arg", "s_exp", "s_out"))
        s_copied, mixed_sem, out_stored = (sem(n) for n in ("s_copied", "mixed_sem", "out_stored"))
        w_hi, w_lo, h_hi, h_lo, gate_ready, first_used = (sem(n) for n in ("w_hi", "w_lo", "h_hi", "h_lo", "gate_ready", "first_used"))
        mem_loaded, sq1_done = sem("mem_loaded"), sem("sq1_done")
        tile_done = sem("tile_done")
        o1_split, m_hi, m_split, y_root = (sem(n) for n in ("o1_split", "m_hi", "m_split", "y_root"))
        oa_split, ob_hi, ob_split, oc_split = (sem(n) for n in ("oa_split", "ob_hi", "ob_split", "oc_split"))
        root_asked, root_done = sem("root_asked"), sem("root_done")
        ROOTS_LAP = 3 * T + 1

        def lap(L, k, per):
            return k if L is None else L * per + k

        def x_count(L, k):
            return lap(L, k + 1, 6)

        CHAIN_LAP = 2000

        class Chain:

            def __init__(self, eng, s):
                self.eng, self.sem, self.n, self.L = eng, s, 0, None

            def link(self, ins):
                self.n += 1
                ins.then_inc(self.sem, 1)

            def sync(self):
                self.eng.wait_ge(self.sem, lap(self.L, self.n, CHAIN_LAP))

            def enter(self, L):
                self.L, self.n0 = L, self.n

            def leave(self):
                self.eng.sem_inc(self.sem, CHAIN_LAP - (self.n - self.n0))

        block = ctx.enter_context(nc.Block())

        @block.sync
        def _(sp):
            sp.dma_start(x[:, :, :], ins["x"][0].rearrange("(t p) n -> p t n", p=P)).then_inc(in_loaded, 16)
            sp.dma_start(const[:, :], ins["const"][:, 0:CONST_W]).then_inc(in_loaded, 16)
            rows1 = wide[:, 0:2, :].rearrange("p a (b n) -> p (a b) n", n=P)
            cw = ins["ffn_conv_w"][0].rearrange("j (a b) -> (j a) b", b=P)
            sp.dma_start(rows1[0:88, 0, :], cw[0:88, :]).then_inc(rows1_loaded, 16)
            sp.dma_start(rows1[0:44, 1, :], cw[88:132, :]).then_inc(rows1_loaded, 16)
            for name, key, n in (("mix_norm_g", "mix", 8), ("mem_norm_g", "mem", 8), ("ffn_norm_g", "ffn", 8), ("ffn_conv_b", "conv_b", 44)):
                sp.dma_start(rows1[ROWS1[key]:ROWS1[key] + n, 2, :], ins[name][0].rearrange("(a b) -> a b", b=P)).then_inc(rows1_loaded, 16)

            def slot_wait(L, s, more=0):
                if L is not None or s >= SLOTS:
                    sp.wait_ge(multiplied, lap(L, s - SLOTS + 1, SLOT_LAP) + more)

            def matrix(L, w):
                if isinstance(w, tuple):
                    return ins[w[0]][bass.ds(L, 1), w[1]].rearrange("a k n -> (a k) n")
                if L is None:
                    return ins[w][0]
                return ins[w][bass.ds(L, 1)].rearrange("a k n -> (a k) n")

            def load(L, s, src):
                w, half, c0 = src
                m = matrix(L, w)
                if s != mix[0].slot0:
                    slot_wait(L, s)
                if half is None:
                    a = m[:, c0:c0 + TOK].rearrange("(k p) n -> p k n", p=P)
                    d = ring[:, s % SLOTS, :].rearrange("p (k n) -> p k n", n=TOK)
                else:
                    a = m[half * 4 * P:(half + 1) * 4 * P, c0:c0 + BANK].rearrange("(k p) n -> p k n", p=P)
                    d = ring[:, s % SLOTS, :].rearrange("p (k n) -> p k n", n=BANK)
                sp.dma_start(d, a).then_inc(w_loaded[s % SLOTS], 16)

            def chunk_loads(L, chunks):
                for s, src in sorted((c.slots[h], c.srcs[h]) for c in chunks for h in range(2)):
                    load(L, s, src)

            def ffn_loads(L, f, up, down, between=None):
                s0 = f["slot0"]
                wu, wd = matrix(L, up), matrix(L, down)

                def up_loads(it, js):
                    for j in js:
                        if len(js) == 1:
                            slot_wait(L, s0 + 2 * j + 1, it * 4)
                        for side in range(2):
                            s = s0 + 2 * j + side
                            if len(js) > 1:
                                slot_wait(L, s, it * 4)
                            a = wu[:, bass.ds(it * BANK + (j * TOK + side * FF), TOK)].rearrange("(k p) n -> p k n", p=P)
                            sp.dma_start(ring[:, s % SLOTS, :].rearrange("p (k n) -> p k n", n=TOK), a)\
                                .then_inc(w_loaded[s % SLOTS], 16)

                with sp.Fori(0, FFC // 2) as it:
                    up_loads(it, range(2))
                up_loads(FFC // 2, range(1))
                if between:
                    between()
                for i in range(FFC):
                    s = s0 + 2 * FFC + i
                    slot_wait(L, s + (i == FFC - 1))
                    a = wd[i * 2 * P:(i + 1) * 2 * P, :].rearrange("(k p) n -> p k n", p=P)
                    sp.dma_start(ring[:, s % SLOTS, :].rearrange("p (k n) -> p k n", n=D), a)\
                        .then_inc(w_loaded[s % SLOTS], 16)

            chunk_loads(None, head1[:1])
            with nc.allow_non_contiguous_dma(reason="256 positions, one per partition"):
                for t in range(T):
                    sp.dma_start(pos[:, t:t + 1], ins["positions"][0, t * P:(t + 1) * P].unsqueeze(1)).then_inc(par1_loaded, 16)
            for i, name in enumerate(("moba_q_norm_g", "moba_k_norm_g", "dil_q_norm_g", "dil_k_norm_g", "mem_q_norm_g", "mem_k_norm_g")):
                sp.dma_start(gains1[:, i * HD:(i + 1) * HD], ins[name][0:1, :].to_broadcast([P, HD])).then_inc(par1_loaded, 16)

            sp.dma_start(gb[:, :, :], ins["mem"][0].rearrange("(t p) n -> p t n", p=P)).then_inc(mem_loaded, 16)
            sp.dma_start(const1, ins["const"][:, CONST_W:CONST_ALL]).then_inc(mem_loaded, 16)
            chunk_loads(None, head1[1:])
            for j in range(4):
                s = branch1_slot0 + j
                slot_wait(None, s)
                d = ring[:, s % SLOTS, :].rearrange("p (k n) -> p k n", n=TOK)
                k0 = 0
                for w, n in zip(("w_branch_moba", "w_branch_dil", "w_branch_mem"), BRANCH_TILES):
                    sp.dma_start(d[:, k0:k0 + n, :], ins[w][0][:, j * TOK:(j + 1) * TOK].rearrange("(k p) n -> p k n", p=P))\
                        .then_inc(w_loaded[s % SLOTS], 16)
                    k0 += n
            chunk_loads(None, out1)
            ffn_loads(None, ffn0, "w_ffn_up", "w_ffn_down")
            with sp.Fori(0, LAYERS) as L:
                def row(name):
                    return ins[name][bass.ds(L, 1)].rearrange("l (a b) -> (l a) b", b=P)

                def load_rows():
                    sp.wait_ge(cols_ready, lap(L, 1, 1))
                    for k in range(3):
                        for s, at in (("g", ROWS2["ln_g"][k]), ("b", ROWS2["ln_b"][k])):
                            sp.dma_start(rows[at:at + 8, 0, :], row(f"ln{k + 1}_{s}_2")).then_inc(rows_loaded, 16)
                    at = ROWS2["gate_b"]
                    sp.dma_start(rows[at:at + 24, 0, :], ins["gate_bias_2"][bass.ds(L, 1)].rearrange("l r (a b) -> (l r a) b", b=P)).then_inc(rows_loaded, 16)
                    at = ROWS2["norm"]
                    sp.dma_start(rows[at:at + 8, 0, :], row("ssm_norm_g_2")).then_inc(rows_loaded, 16)
                    at = ROWS2["subln"]
                    sp.dma_start(rows[at:at + 1, 0, :], ins["diff_subln_g_2"][bass.ds(L, 1)]).then_inc(rows_loaded, 16)
                    sp.dma_start(rows[0:4 * N_XBC, 1, :], ins["ssm_conv_w_2"][bass.ds(L, 1)].rearrange("l j (a b) -> (l j a) b", b=P)).then_inc(rows_loaded, 16)
                    sp.dma_start(rows[4 * N_XBC:5 * N_XBC, 1, :], row("ssm_conv_b_2")).then_inc(rows_loaded, 16)
                    sp.wait_ge(x_ready, x_count(L, 0))
                    sp.dma_start(bcast[:, 0:256], ins["diff_lambda_2"][bass.ds(L, 1)].rearrange("l a d -> l (a d)").to_broadcast([P, 256])).then_inc(par_loaded, 16)
                    sp.dma_start(bcast[:, 256:272], ins["ssm_dt_bias_2"][bass.ds(L, 1)].to_broadcast([P, NH])).then_inc(par_loaded, 16)
                    sp.dma_start(bcast[:, 272:288], ins["ssm_A_log_2"][bass.ds(L, 1)].to_broadcast([P, NH])).then_inc(par_loaded, 16)
                    sp.dma_start(bcast[:, 288:304], ins["ssm_D_2"][bass.ds(L, 1)].to_broadcast([P, NH])).then_inc(par_loaded, 16)
                    sp.dma_start(dtw[:, :, :], ins["w_mix_in_2"][bass.ds(L, 1), :, MIX["dt"]:MIX["dt"] + NH].rearrange("l (k p) n -> p (l k) n", p=P))\
                        .then_inc(par_loaded, 16)

                def load_gb(k):
                    sp.wait_ge(x_ready, x_count(L, 2 * k))
                    for i, side in enumerate("gb"):
                        sp.dma_start(gb[:, i, :], ins[f"ln{k + 1}_{side}_2"][bass.ds(L, 1)].to_broadcast([P, D])).then_inc(gb_loaded, 16)

                ffn_loads(L, ffn1, "ffn1_w_in_2", "ffn1_w_out_2", lambda: (load_rows(), load_gb(0)))
                second = 1 + max(n for n, c in enumerate(mix) if c.name == "branch" and c.r == 1)
                chunk_loads(L, mix[:second])
                load_gb(1)
                chunk_loads(L, mix[second:] + out2)
                ffn_loads(L, ffn2, "ffn2_w_in_2", "ffn2_w_out_2", lambda: load_gb(2))

        def squares1(n, t):
            heads = NORMED[n][1]
            return kcT[:, 2 * t:2 * t + 2, :].rearrange("p a n -> p (a n)")[:, 0:heads * HD]

        def bank(b):
            return ps[:, b, :]

        def tiles(b):
            return ps[:, b, :].rearrange("p (f n) -> p f n", n=TOK)

        def wait_drained(eng, L, c):
            for b, n in c.need.items():
                eng.wait_ge(drained[b], lap(L, n + c.evacs, FREE_LAP[b]))

        def wait_products(eng, L, c):
            eng.wait_ge(multiplied, lap(L, c.slot0 + 2, SLOT_LAP))

        by_rows = {c.slots[h] for c in head1 + out1 + mix + out2 if c.mode == "A" for h in range(2)}
        by_rows |= {f["slot0"] + 2 * FFC + i for f in (ffn0, ffn1, ffn2) for i in range(FFC)}

        after_norm = {ffn1["slot0"] + h for h in range(HIGHS)}

        def split_by_rows(s):
            if s in after_norm:
                return s in by_rows
            return (s if s < HIGHS else s - HIGHS) in by_rows

        def half_of(place, s, q):
            if split_by_rows(s):
                return place[:, q * SLOT // HALVES:(q + 1) * SLOT // HALVES]
            return place.rearrange("p (k n) -> p k n", n=TOK)[:, :, q * P:(q + 1) * P]

        def wait_loaded(eng, L, s, more=0):
            extra = 16 * (len(BRANCH_TILES) - 1) if s >= branch1_slot0 else 0
            eng.wait_ge(w_loaded[s % SLOTS], lap(L, 16 * (s // SLOTS + 1) + extra, 16 * SLOT_LAP // SLOTS) + more)

        @block.tensor
        def _(pe):
            def wait_block(L, s, q, it=0):
                last = HALVES - 1 if split_by_rows(s) != (s in by_rows) else q
                pe.wait_ge(w_lo, lap(L, HALVES * s + last + 1, HALVES * SLOT_LAP) + it * (HALVES * SLOTS))

            def used(mm, q):
                mm.then_inc(multiplied if q else first_used, 1)

            def block(s, n):
                return [a.rearrange("p (k n) -> p k n", n=n) for a in (ring_hi[:, s % HIGHS, :], ring_lo[:, s % SLOTS, :])]

            def product(out_, stat, mov, first, last):
                pe.matmul(out_, stat[0], mov[0], start=first, stop=False)
                pe.matmul(out_, stat[0], mov[1], start=False, stop=False)
                return pe.matmul(out_, stat[1], mov[0], start=False, stop=last)

            def wait_xT(L, event, t=T - 1):
                pe.wait_ge(xT_act, lap(L, 2 * event + t - 1, 6))
                pe.wait_ge(xT_dve, lap(L, 2 * event + t - 1, 6))

            def by_tiles(L, c, h, s):
                act, w = acts[c.act], block(s, BANK)
                for q in range(HALVES):
                    wait_block(L, s, q)
                for t in range(T):
                    if h == 0:
                        wait_xT(L, c.event, t)
                    for k in range(4):
                        mm = product(bank(2 * c.pair + t), [a[:, 4 * h + k, t * P:(t + 1) * P] for a in act], [v[:, k, :] for v in w],
                                     h == 0 and k == 0, h == 1 and k == 3)
                        if t == T - 1 and k % 2:
                            used(mm, k // 2)
                    if t == 0 and h == 1:
                        mm.then_inc(tile_done, 1)

            def half(L, c, h, q):
                act = acts[c.act]
                if h == 0 and q == 0:
                    for b, n in c.need.items():
                        if n:
                            pe.wait_ge(drained[b], lap(L, n, FREE_LAP[b]))
                s = c.slots[h]
                if h == 0 and c.event is not None or h == 1 and c.tail:
                    if q == 0:
                        by_tiles(L, c, h, s)
                    return
                wait_block(L, s, q)
                if c.mode == "A":
                    w = block(s, BANK)
                    for t in range(T):
                        for k in (2 * q, 2 * q + 1):
                            mm = product(bank(2 * c.pair + t), [a[:, 4 * h + k, t * P:(t + 1) * P] for a in act], [v[:, k, :] for v in w],
                                         h == 0 and k == 0, h == 1 and k == 3)
                else:
                    w = block(s, TOK)
                    for k in range(KD):
                        mm = product(tiles(2 * c.pair + h)[:, q, :], [v[:, k, q * P:(q + 1) * P] for v in w], [a[:, k, :] for a in act],
                                     k == 0, k == KD - 1)
                used(mm, q)

            def ffn(L, f, event, before_down=None):
                s0 = f["slot0"]

                def up(it, js, first=False):
                    for j in js:
                        for side in range(2):
                            b = 2 * j + side
                            s = s0 + b
                            if not first:
                                pe.wait_ge(drained[b], lap(L, f["free0"][b], FREE_LAP[b]) + it)
                            elif f["free0"][b]:
                                pe.wait_ge(drained[b], lap(L, f["free0"][b], FREE_LAP[b]))
                            w = block(s, TOK)
                            if first and b == 0:
                                wait_xT(L, event)
                            for q in range(HALVES):
                                if first:
                                    wait_block(L, s, q)
                                else:
                                    pe.wait_ge(w_lo, lap(L, HALVES * s + q + 1, HALVES * SLOT_LAP) + it * (HALVES * SLOTS))
                                for k in range(KD):
                                    mm = product(tiles(b)[:, q, :], [v[:, k, q * P:(q + 1) * P] for v in w],
                                                 [a[:, k, :] for a in acts["xT"]], k == 0, k == KD - 1)
                                used(mm, q)

                up(0, range(2), True)
                with pe.Fori(1, FFC // 2) as it:
                    up(it, range(2))
                up(FFC // 2, range(1))
                if before_down:
                    before_down()
                for i in range(FFC):
                    s = s0 + 2 * FFC + i
                    w = block(s, D)
                    pe.wait_ge(h_lo, lap(L, f["h0"] + i + 1, 2 * FFC))
                    last = i == FFC - 1
                    for k, t in [(k, t) for t in range(T) for k in range(HALVES)] if last else [(k, t) for k in range(HALVES) for t in range(T)]:
                        if t == 0:
                            wait_block(L, s, k)
                        for n in range(2):
                            mm = product(bank(DOWN + 2 * n + t), [a[:, 2 * i + k, t * P:(t + 1) * P] for a in (h2_hi, h2_lo)],
                                         [v[:, k, n * BANK:(n + 1) * BANK] for v in w], i == 0 and k == 0, last and k == 1)
                        if t == T - 1:
                            used(mm, k)
                        elif last and k == HALVES - 1:
                            mm.then_inc(tile_done, 1)

            def norm(L, event, src, base=4):
                for t in range(T):
                    pe.wait_ge(hat_ready, lap(L, 2 * event + t + 1, 6))
                    for g in range(2):
                        for k in range(4):
                            tr = pe.transpose(ps[:, base + 2 * t + g, k * P:(k + 1) * P],
                                              src[:, t, (4 * g + k) * P:(4 * g + k + 1) * P], ident)
                        tr.then_inc(hat_turned, 1)

            pe.wait_ge(in_loaded, 2 * 16)
            pe.wait_ge(rows1_loaded, 6 * 16)
            rows1 = wide[:, 0:2, :].rearrange("p a (b n) -> p (a b) n", n=P)
            pe.transpose(bank(4)[:, 0:88], rows1[0:88, 0, :], ident[0:88, 0:88])
            pe.transpose(bank(4)[:, 88:132], rows1[0:44, 1, :], ident[0:44, 0:44])
            pe.transpose(bank(4)[:, 132:132 + N_ROWS1], rows1[0:N_ROWS1, 2, :], ident[0:N_ROWS1, 0:N_ROWS1])\
                .then_inc(rows1_turned, 1)
            pe.wait_ge(cols_ready, 1)
            norm(None, 0, xhat)
            def pair1(p):
                segs = (2, 4, 6)[(p >= 3) + (p >= 6)]
                pe.wait_ge(norm1_done, 2 * segs)
                if p >= 2:
                    pe.wait_ge(pair1_copied, p - 1)
                for a, col in enumerate((Q_COL[p], K_COL[p])):
                    for t in range(T):
                        tr = pe.transpose(ps[:, TB + p % 2, (2 * a + t) * P:(2 * a + t + 1) * P], tok1[:, t, col:col + P], ident)
                tr.then_inc(pair1_turned, 1)

            def keys1(u):
                return P if u % 2 == 0 and u // 2 < 6 else TOK

            def score1(u):
                p, qt, nk = u // 2, u % 2, keys1(u)
                pe.wait_ge(pair1_copied, p + 1)
                if u:
                    pe.wait_ge(masked1, u)
                for m in range(2):
                    r = slice(HD * m, HD * (m + 1))
                    mm = pe.matmul(ps[:, S0 + m, (u % 2) * TOK:(u % 2) * TOK + nk], qT[r, p, qt * P:(qt + 1) * P],
                                   kT[r, p, 0:nk], start=True, stop=True)
                mm.then_inc(score1_ready, 1)

            def turn1(u):
                nt = keys1(u) // P
                pe.wait_ge(prob1, u + 1)
                if u == 0:
                    pe.wait_ge(pair1_copied, PAIRS)
                else:
                    pe.wait_ge(prob1_copied, u)
                for m in range(2):
                    for k in range(nt):
                        tr = pe.transpose(ps[:, TB, (m * nt + k) * P:(m * nt + k + 1) * P],
                                          ex[:, u % 2, (m * nt + k) * P:(m * nt + k + 1) * P], ident)
                tr.then_inc(prob1_turned, 1)

            def out1_of(u):
                p, nt = u // 2, keys1(u) // P
                pe.wait_ge(prob1_copied, u + 1)
                if u == 0:
                    for c in head1[:6]:
                        wait_drained(pe, None, c)
                else:
                    pe.wait_ge(out1_copied, u)
                for m in range(2):
                    for k in range(nt):
                        v = V_COL[p] + HD * m
                        mm = pe.matmul(ps[HD * m:HD * (m + 1), OB, (u % 4) * P:(u % 4 + 1) * P], tok1[:, k, v:v + HD],
                                       wt[:, u % 2, (m * nt + k) * P:(m * nt + k + 1) * P],
                                       start=(k == 0), stop=(k == nt - 1))
                mm.then_inc(out1_ready, 1)

            for step in steps1:
                if step[0] == "half":
                    if step[1].act == "memT" and step[2:] == (0, 0):
                        wait_xT(None, 2)
                    half(None, *step[1:])
                elif step[0] == "memory":
                    norm(None, 1, xhat)
                elif step[0] == "pair1":
                    pair1(step[1])
                elif step[0] == "score1":
                    score1(step[1])
                elif step[0] == "turn1":
                    turn1(step[1])
                elif step[0] == "out1":
                    out1_of(step[1])
            pe.wait_ge(o1_split, PAIRS)
            for c in head1[-2:]:
                wait_drained(pe, None, c)
            for j in range(4):
                s = branch1_slot0 + j
                if j >= 2:
                    pe.wait_ge(branch1_free, j - 1)
                w = block(s, TOK)
                for q in range(HALVES):
                    wait_block(None, s, q)
                    k0 = 0
                    for r, n in enumerate(BRANCH_TILES):
                        for k in range(k0, k0 + n):
                            mm = product(tiles(4 * (j % 2) + r)[:, q, :], [v[:, k, q * P:(q + 1) * P] for v in w],
                                         [a[:, k, :] for a in acts["o1T"]], k == k0, k == k0 + n - 1)
                        k0 += n
                    used(mm, q)
            for h in range(2):
                pe.wait_ge(m_split, 2 * h + 2)
                for c in out1:
                    for q in range(HALVES):
                        half(None, c, h, q)
            norm(None, 2, xhat)
            ffn(None, ffn0, 3)
            norm(None, 3, x, 0)

            with pe.Fori(0, LAYERS) as L:
                def turn_rows():
                    pe.wait_ge(rows_loaded, lap(L, 11 * 16, 11 * 16))
                    b = ffn1["free0"][3] + FFC // 2
                    pe.wait_ge(drained[3], lap(L, b, FREE_LAP[3]))
                    pe.transpose(bank(3)[:, 0:N_ROWS2], rows[0:N_ROWS2, 0, :], ident[0:N_ROWS2, 0:N_ROWS2])
                    pe.transpose(bank(3)[:, P:P + N_CONV2], rows[0:N_CONV2, 1, :], ident[0:N_CONV2, 0:N_CONV2])\
                        .then_inc(rows_turned, 1)

                def dt():
                    pe.wait_ge(par_loaded, lap(L, 5 * 16, 5 * 16))
                    for t in range(T):
                        for k in range(KD):
                            for part in acts["xT"]:
                                mm = pe.matmul(ps[:, OB, t * NH:(t + 1) * NH], part[:, k, t * P:(t + 1) * P].bitcast(F32), dtw[:, k, :],
                                               start=(k == 0 and part is xT_hi), stop=(k == KD - 1 and part is xT_lo))
                    mm.then_inc(dt_ready, 1)

                def turn_qk(j):
                    which, hp = j % 2, j // 2
                    src = (qa, ka)[which]
                    wait_drained(pe, L, mix[2 * which + hp // 2])
                    if hp == 0 and which == 1:
                        pe.wait_ge(dt_arg, lap(L, 1, 1))
                    if hp:
                        pe.wait_ge((q_copied, k_copied)[which], lap(L, hp, 4))
                    for h in range(2):
                        for t in range(T):
                            tr = pe.transpose(ps[:, TB + which, (2 * h + t) * P:(2 * h + t + 1) * P],
                                              src[:, t, (2 * hp + h) * P:(2 * hp + h + 1) * P], ident)
                    tr.then_inc((q_turned, k_turned)[which], 1)

                def dscore(u):
                    h, qt = u // 2, u % 2
                    nk = P * (1 + qt)
                    pe.wait_ge(q_copied, lap(L, h // 2 + 1, 4))
                    pe.wait_ge(k_copied, lap(L, h // 2 + 1, 4))
                    if u:
                        pe.wait_ge(d_masked, lap(L, u, 2 * DH))
                    for m in range(2):
                        r = slice(HD * m, HD * (m + 1))
                        mm = pe.matmul(ps[:, S0 + m, (u % 2) * TOK:(u % 2) * TOK + nk], qT[r, h, qt * P:(qt + 1) * P],
                                       kT[r, h, 0:nk], start=True, stop=True)
                    mm.then_inc(d_score, 1)

                def dturn(u):
                    pe.wait_ge(d_w, lap(L, u + 1, 2 * DH))
                    if u:
                        pe.wait_ge(d_copied, lap(L, u, 2 * DH))
                    else:
                        pe.wait_ge(q_copied, lap(L, 4, 4))
                    for k in range(1 + u % 2):
                        tr = pe.transpose(ps[:, TB, (u % 2) * TOK + k * P:(u % 2) * TOK + (k + 1) * P],
                                          ex[:, u % 2, k * P:(k + 1) * P], ident)
                    tr.then_inc(d_turned, 1)

                def dout(u):
                    h, nt = u // 2, 1 + u % 2
                    pe.wait_ge(d_copied, lap(L, u + 1, 2 * DH))
                    if u == 0:
                        for c in mix:
                            if c.name == "va":
                                wait_drained(pe, L, c)
                        pe.wait_ge(k_copied, lap(L, 4, 4))
                    else:
                        pe.wait_ge(d_sq, lap(L, u, 2 * DH))
                    for k in range(nt):
                        mm = pe.matmul(ps[:, OB, (u % 4) * P:(u % 4 + 1) * P], wt[:, u % 2, k * P:(k + 1) * P],
                                       va[:, k, h * P:(h + 1) * P], start=(k == 0), stop=(k == nt - 1))
                    mm.then_inc(d_out, 1)

                def turn_oa(j):
                    if j < 2:
                        pe.wait_ge(d_norm, lap(L, T, T))
                        pe.wait_ge(xs_copied, lap(L, j + 3, 4))
                    else:
                        pe.wait_ge(oa_copied, lap(L, j - 1, 4))
                    for h in range(2):
                        for t in range(T):
                            tr = pe.transpose(ps[:, TB + j % 2, (2 * h + t) * P:(2 * h + t + 1) * P],
                                              oA[:, t, (2 * j + h) * P:(2 * j + h + 1) * P], ident)
                    tr.then_inc(oa_turned, 1)

                def turn_xs(j):
                    if j < 2:
                        pe.wait_ge((d_copied, d_sq)[j], lap(L, 2 * DH, 2 * DH))
                        pe.wait_ge(xbc_done, lap(L, 6, 6))
                    else:
                        pe.wait_ge(xs_copied, lap(L, j - 1, 4))
                    for t in range(T):
                        for f in range(2):
                            tr = pe.transpose(ps[:, TB + j % 2, (2 * t + f) * P:(2 * t + f + 1) * P],
                                              xbc[:, 2 * j + f, t * P:(t + 1) * P], ident)
                    tr.then_inc(xs_turned, 1)

                def causal_pair(out_bank, lhs0, lhs1, rhs):
                    pe.matmul(ps[:, out_bank, 0:TOK], lhs0, rhs[:, 0:TOK], start=True, stop=True)
                    return pe.matmul(ps[:, out_bank, TOK:CAUS], lhs1, rhs[:, P:TOK], start=True, stop=True)

                def causal_values(m, b, v0, v1, w):
                    r = slice(HD * m, HD * (m + 1))
                    pe.matmul(ps[r, b, 0:TOK], v0, w[:, 0:TOK], start=True, stop=False)
                    return pe.matmul(ps[r, b, P:TOK], v1, w[:, TOK:CAUS], start=False, stop=True)

                def cb(g):
                    if g == 0:
                        pe.wait_ge(d_masked, lap(L, 2 * DH, 2 * DH))
                        pe.wait_ge(xbc_done, lap(L, 6, 6))
                    causal_pair(S0 + g, xbc[:, 8 + g, 0:P], xbc[:, 8 + g, P:TOK], xbc[:, 10 + g, :]).then_inc(cb_ready, 1)

                def sdecay(u):
                    b = S0 + u % 2
                    pe.wait_ge(seg_built, lap(L, u + 1, NH))
                    if u < 2:
                        pe.wait_ge(cb_masked, lap(L, 2, 2))
                    else:
                        pe.wait_ge(seg_exp, lap(L, u - 1, NH))
                    w = seg_w[:, u % 2, :]
                    pe.matmul(ps[:, b, 0:TOK], w[:, 0:P], upto, start=True, stop=False)
                    pe.matmul(ps[:, b, P:TOK], w[:, 2 * P:3 * P], upto[:, 0:P], start=False, stop=True)
                    pe.matmul(ps[:, b, TOK:CAUS], w[:, P:2 * P], upto[:, 0:P], start=True, stop=True).then_inc(seg_ready, 1)

                def sout(u):
                    p = u // 2
                    pe.wait_ge(l_ready, lap(L, u + 1, NH))
                    if u == 0:
                        pe.wait_ge(xs_copied, lap(L, 4, 4))
                        pe.wait_ge(oa_copied, lap(L, 4, 4))
                    if p >= 2 and u % 2 == 0:
                        pe.wait_ge(y_gated, lap(L, p - 1, NH // 2))
                    causal_values(u % 2, TB + p % 2, xs[:, 0, u * HD:(u + 1) * HD], xs[:, 1, u * HD:(u + 1) * HD],
                                  lmat[:, u % 2, :]).then_inc(y_ready, 1)

                def snorm(g):
                    pe.wait_ge(y_sq, lap(L, g + 1, 2))
                    pe.wait_ge(y_gated, lap(L, NH // 2, NH // 2))
                    w = wt[:, :, :].rearrange("p a (b n) -> p (a b) n", n=TOK)
                    for k in range(4):
                        mm = pe.matmul(ps[:, TB + g, 0:TOK], ones, w[:, k, :], start=(k == 0), stop=(k == 3))
                    mm.then_inc(y_sum, 1)

                def kscore(u):
                    r, pair = slice(HD * (u % 2), HD * (u % 2 + 1)), u // 2
                    if u % (NH // 2) == 0:
                        for c in mix:
                            if c.name in ("qc", "kc") and c.index == u // (NH // 2):
                                wait_drained(pe, L, c)
                    if u < 2:
                        pe.wait_ge(seg_exp, lap(L, NH, NH))
                    else:
                        pe.wait_ge(s_masked, lap(L, u - 1, NH))
                    causal_pair(S0 + u % 2, kcT[r, pair, 0:P], kcT[r, pair, P:TOK], qcT[r, pair, :]).then_inc(s_score, 1)

                def ksum(u):
                    pe.wait_ge(s_soft, lap(L, u + 1, NH))
                    if u == 0:
                        pe.wait_ge(o_b, lap(L, 2, 2))
                    else:
                        pe.wait_ge(s_arg, lap(L, u, NH))
                    sp_ = lmat[:, u % 2, :]
                    pe.matmul(ps[:, TB, TOK:CAUS], from_on, sp_[:, TOK:CAUS], start=True, stop=True)
                    pe.matmul(ps[:, TB, 0:TOK], from_on, sp_[:, 0:TOK], start=True, stop=False)
                    pe.matmul(ps[:, TB, P:TOK], ones, sp_[:, TOK:CAUS], start=False, stop=True).then_inc(s_sum, 1)

                def kout(u):
                    p = u // 2
                    pe.wait_ge(s_exp, lap(L, u + 1, NH))
                    if u % (NH // 2) == 0:
                        for c in mix:
                            if c.name == "vc" and c.index == u // (NH // 2):
                                wait_drained(pe, L, c)
                    if u % 2 == 0:
                        if p:
                            pe.wait_ge(s_copied, lap(L, p, NH // 2))
                        else:
                            pe.wait_ge(o_b, lap(L, 2, 2))
                    causal_values(u % 2, OB, vc[:, 0, u * HD:(u + 1) * HD], vc[:, 1, u * HD:(u + 1) * HD],
                                  ex[:, u % 2, :]).then_inc(s_out, 1)

                attention = dict(turn_qk=turn_qk, dscore=dscore, dturn=dturn, dout=dout, turn_oa=turn_oa, turn_xs=turn_xs,
                                 cb=cb, sdecay=sdecay, sout=sout, snorm=snorm, kscore=kscore, ksum=ksum, kout=kout)
                ffn(L, ffn1, 4, turn_rows)
                pe.wait_ge(cols_ready, lap(L, 2, 1))
                norm(L, 4, xhat, 0)
                for step in mixed:
                    if step[0] == "half":
                        c = step[1]
                        if c.name == "branch" and c.index == 0 and step[2:] == (0, 0):
                            ready, n = ((oa_split, 4), (ob_split, 2), (oc_split, NH // 2))[c.r]
                            pe.wait_ge(ready, lap(L, n, n))
                        half(L, *step[1:])
                    elif step[0] == "dt":
                        dt()
                    elif step[0] in attention:
                        attention[step[0]](*step[1:])
                for h in range(2):
                    pe.wait_ge(m_split, lap(L, 4 + 2 * h + 2, 4))
                    for c in out2:
                        for q in range(HALVES):
                            half(L, c, h, q)
                norm(L, 5, xhat)
                ffn(L, ffn2, 6)
                norm(L, 6, xhat, 0)

        @block.scalar
        def _(act):
            chain = Chain(act, act_chain)
            def norm_cols(L, event, g, b, dst, hi, base=4):
                for t in range(T):
                    act.wait_ge(hat_turned, lap(L, 4 * event + 2 * t + 1, 12))
                    for k in range(4):
                        o, i = dst[:, k, t * P:(t + 1) * P], ps[:, base + 2 * t, k * P:(k + 1) * P]
                        if g is None:
                            ins_ = act.activation(o, i, ACT.Copy)
                        elif b is None:
                            ins_ = act.activation(o, i, ACT.Copy, scale=g[:, k:k + 1])
                        else:
                            ins_ = act.activation(o, i, ACT.Identity, scale=g[:, k:k + 1], bias=b[:, k:k + 1])
                    chain.link(ins_)
                    chain.sync()
                    act.activation(hi[:, 0:4, t * P:(t + 1) * P], dst[:, 0:4, t * P:(t + 1) * P], ACT.Copy).then_inc(xT_act, 1)

            def split_half(L, s, q, it=0):
                if q == 0:
                    wait_loaded(act, L, s, it * 16)
                if L is not None or s >= HIGHS:
                    act.wait_ge(multiplied if q or s in after_norm else first_used, lap(L, s - HIGHS + 1, SLOT_LAP) + it * SLOTS)
                act.activation(half_of(ring_hi[:, s % HIGHS, :], s, q), half_of(ring[:, s % SLOTS, :], s, q), ACT.Copy).then_inc(w_hi, 1)

            def split(L, s, it=0):
                for q in range(HALVES):
                    split_half(L, s, q, it)

            def down_splits(L, f):
                for s in range(f["slot0"] + 2 * FFC + HIGHS, f["slot0"] + 3 * FFC + f["ahead"]):
                    split(L, s)

            def sigmoid(places, done):
                for e in places:
                    chain.link(act.activation(e, e, ACT.Ln, bias=1.0))
                chain.sync()
                for e in places:
                    act.activation(e, e, ACT.Exp, scale=-1.0).then_inc(done, 1)

            def drain_gate(L, c, part, bias):
                if part == 0:
                    wait_products(act, L, c)
                if part < 2:
                    for f in range(2):
                        k = 4 * c.index + 2 * part + f
                        ins_ = act.activation(wide[:, k, :], tiles(2 * c.pair + part)[:, f, :], ACT.Exp, scale=-1.0, **bias(k))
                    ins_.then_inc(drained[2 * c.pair + part], 1)
                    return
                places = [wide[:, 4 * c.index + 2 * j:4 * c.index + 2 * j + 2, :] for j in range(2)]
                if part == 2:
                    wait_drained(act, L, c)
                    for e in places:
                        ins_ = act.activation(e, e, ACT.Ln, bias=1.0)
                    chain.link(ins_)
                else:
                    chain.sync()
                    for e in places:
                        act.activation(e, e, ACT.Exp, scale=-1.0).then_inc(gate_ready, 1)

            def squares(src, event):
                for t in range(T):
                    if event >= 2:
                        act.wait_ge(x_added, t + 1)
                    if 2 * event + t:
                        act.wait_ge(sq_ready, 2 * event + t)
                    act.activation(wide[:, 4:8, :].rearrange("p a n -> p (a n)"), src[:, t, :], ACT.Square,
                                   accum_out=small[:, 64 + 2 * event + t:65 + 2 * event + t]).then_inc(sq_ready, 1)

            def ffn_silu(L, f):
                def up(it, js):
                    for j in js:
                        split(L, f["slot0"] + 2 * j + HIGHS, it)
                        act.wait_ge(multiplied, lap(L, f["slot0"] + 2 * j + 1, SLOT_LAP) + it * 4)
                        act.wait_ge(drained[2 * j + 1], lap(L, f["free0"][2 * j + 1], FREE_LAP[2 * j + 1]) + it)
                        act.activation(act_s[:, j, :], bank(2 * j), ACT.Silu).then_inc(drained[2 * j], 1)
                        split(L, f["slot0"] + 2 * j + 1 + HIGHS, it)

                with act.Fori(0, FFC // 2) as it:
                    up(it, range(2))
                up(FFC // 2, range(1))
                down_splits(L, f)

            def ffn_conv(f):
                def up(it, js):
                    for j in js:
                        for side in range(2):
                            split(None, f["slot0"] + 2 * j + side + HIGHS, it)
                        act.wait_ge(multiplied, f["slot0"] + 2 * j + 2 + it * 4)
                        if j == 0:
                            act.wait_ge(h_ready, it * 2 + 2)
                        for side, dst in enumerate((act_s, conv_s)):
                            for ft in range(2):
                                tile = it * 4 + (2 * j + ft + side * KF)
                                ins_ = act.activation(
                                    dst[:, j, ft * TOK:(ft + 1) * TOK], tiles(2 * j + side)[:, ft, :], ACT.Identity,
                                    scale=conv1[:, bass.ds(tile + 2 * 2 * KF, 1)],
                                    bias=conv1[:, bass.ds(tile + N_CONV1 + ROWS1["conv_b"], 1)])
                        ins_.then_inc(conv_begun, 1)
                        act.wait_ge(drained[2 * j], f["free0"][2 * j] + it + 1)
                        act.activation(act_s[:, j, :], act_s[:, j, :], ACT.Silu).then_inc(act_ready, 1)

                with act.Fori(0, FFC // 2) as it:
                    up(it, range(2))
                up(FFC // 2, range(1))
                down_splits(None, f)

            act.wait_ge(in_loaded, 2 * 16)
            squares(x, 0)
            for slot in range(HIGHS):
                split(None, slot)
            act.wait_ge(cols_ready, 1)
            g1 = conv1[:, N_CONV1:N_CONV1 + N_ROWS1]
            norm_cols(None, 0, g1[:, 0:8], None, xT, xT_hi)

            def memory():
                act.wait_ge(mem_loaded, 2 * 16)
                squares(gb, 1)
                norm_cols(None, 1, g1[:, 8:16], None, memT, acts["memT"][0])

            def angles():
                act.wait_ge(angle_ready, 1)
                act.activation(kcT[:, 7, 128:256], kcT[:, 7, 0:128], ACT.Sin).then_inc(sin_ready, 1)
                act.preload_act_table_set("natural_log_exp_and_others")

            def drain_tok(c, part):
                if part:
                    return
                wait_products(act, None, c)
                col = c.index * BANK
                for t in range(T):
                    act.activation(tok1[:, t, col:col + BANK], bank(2 * c.pair + t), ACT.Copy).then_inc(drained[2 * c.pair + t], 1)
                wait_drained(act, None, c)
                for t in range(T):
                    first, heads = NORMED[c.index][0:2]
                    if c.index:
                        act.wait_ge(norm1_done, 2 * c.index - 1 + t)
                    act.activation(squares1(c.index, t), tok1[:, t, first:first + heads * HD], ACT.Square).then_inc(sq1_done, 1)

            def pair1(p):
                act.wait_ge(pair1_turned, p + 1)
                act.activation(qT[:, p, :], ps[:, TB + p % 2, 0:TOK], ACT.Copy)
                act.activation(kT[:, p, :], ps[:, TB + p % 2, TOK:BANK], ACT.Copy).then_inc(pair1_copied, 1)

            def keys1(u):
                return P if u % 2 == 0 and u // 2 < 6 else TOK

            def score1(u):
                nk, at = keys1(u), (u % 4) * 16
                act.wait_ge(peak1, u + 1)
                if u >= 2:
                    act.wait_ge(prob1_turned, u - 1)
                for m in range(2):
                    ins_ = act.activation(ex[:, u % 2, m * nk:(m + 1) * nk], sm[:, u % 2, m * nk:(m + 1) * nk], ACT.Exp,
                                          scale=-1.0, bias=small[:, at + m:at + m + 1], accum_out=small[:, at + 2 + m:at + 3 + m])
                ins_.then_inc(exp1, 1)

            def turn1(u):
                act.wait_ge(prob1_turned, u + 1)
                if u >= 2:
                    act.wait_ge(out1_ready, u - 1)
                act.activation(wt[:, u % 2, 0:2 * keys1(u)], ps[:, TB, 0:2 * keys1(u)], ACT.Copy).then_inc(prob1_copied, 1)

            def out1_of(u):
                act.wait_ge(out1_ready, u + 1)
                for place in (o1T, acts["o1T"][0]):
                    ins_ = act.activation(place[:, u // 2, (u % 2) * P:(u % 2 + 1) * P], ps[:, OB, (u % 4) * P:(u % 4 + 1) * P], ACT.Copy)
                ins_.then_inc(out1_copied, 1)

            for step in steps1:
                if step[0] == "memory":
                    memory()
                elif step[0] == "angles":
                    angles()
                elif step[0] == "drain":
                    if step[1].name == "tok":
                        drain_tok(*step[1:])
                    else:
                        drain_gate(None, *step[1:], lambda k: {})
                elif step[0] == "split":
                    split_half(None, *step[1:])
                elif step[0] == "pair1":
                    pair1(step[1])
                elif step[0] == "score1":
                    score1(step[1])
                elif step[0] == "turn1":
                    turn1(step[1])
                elif step[0] == "out1":
                    out1_of(step[1])
            for j in range(4):
                split(None, branch1_slot0 + j + HIGHS)
                act.wait_ge(mixed1, j + 1)
                act.activation(xT_hi[:, 2 * j:2 * j + 2, :], mT[:, 2 * j:2 * j + 2, :], ACT.Copy).then_inc(m_hi, 1)
            for slot in range(out1[0].slot0 + HIGHS, ffn0["slot0"] + 1):
                split(None, slot)
            squares(x, 2)
            norm_cols(None, 2, g1[:, 16:24], None, xT, xT_hi)
            split(None, ffn0["slot0"] + 1)
            ffn_conv(ffn0)
            norm_cols(None, 3, None, None, xT, xT_hi, 0)

            with act.Fori(0, LAYERS) as L:
                chain.enter(L)

                def xhat_of(k):
                    for t in range(T):
                        act.wait_ge(stat_ready, lap(L, 2 * k + t + 1, 6))
                        s = small[:, 96 + 4 * t:96 + 4 * t + 4]
                        act.activation(xhat[:, t, :], x[:, t, :], ACT.Identity, scale=s[:, 2:3], bias=s[:, 3:4]).then_inc(hat_ready, 1)

                def layer_norm(k):
                    xhat_of(k)
                    g, b = ROWS2["ln_g"][k], ROWS2["ln_b"][k]
                    norm_cols(L, 4 + k, cols[:, g:g + 8], cols[:, b:b + 8], xT, xT_hi, 4 if k == 1 else 0)

                def drain(c, part):
                    p = c.pair
                    if part and c.name in ("qa", "ka", "va", "zb", "qc", "kc", "vc"):
                        return
                    if c.name in ("qa", "ka"):
                        dst = qa if c.name == "qa" else ka
                        wait_products(act, L, c)
                        for t in range(T):
                            o = dst[:, t, c.index * BANK:(c.index + 1) * BANK].rearrange("p (m d) -> p m d", d=HD)
                            i = bank(2 * p + t).rearrange("p (m d) -> p m d", d=HD)
                            act.activation(o[:, :, 16:HD], i[:, :, 16:HD], ACT.Copy).then_inc(drained[2 * p + t], 1)
                    elif c.name == "va":
                        wait_products(act, L, c)
                        for t in range(T):
                            act.activation(va[:, t, c.index * BANK:(c.index + 1) * BANK], bank(2 * p + t), ACT.Copy)\
                                .then_inc(drained[2 * p + t], 1)
                    elif c.name == "zb":
                        wait_products(act, L, c)
                        if c.index == 0:
                            act.wait_ge(xbc_done, lap(L, 6, 6))
                        else:
                            act.wait_ge(drained[2 * p + 1], lap(L, c.need[2 * p + 1], FREE_LAP[2 * p + 1]))
                            wait_drained(act, L, [d for d in mix if d.name == "zb"][0])
                        places = [conv_s[:, j, :] for j in range(2)]
                        for j in range(2):
                            chain.link(act.activation(places[j], bank(2 * p + j), ACT.Exp, scale=-1.0))
                        chain.sync()
                        sigmoid(places, z_exp)
                    elif c.name == "xbc" and part == 0:
                        wait_products(act, L, c)
                        if c.index:
                            act.wait_ge(xbc_done, lap(L, 2 * c.index, 6))
                        for j in range(2):
                            for f in range(2):
                                k = 4 * c.index + 2 * j + f
                                ins_ = act.activation(conv_s[:, j, f * TOK:(f + 1) * TOK], tiles(2 * p + j)[:, f, :], ACT.Identity,
                                                      scale=cols[:, P + 3 * N_XBC + k:P + 3 * N_XBC + k + 1],
                                                      bias=cols[:, P + 4 * N_XBC + k:P + 4 * N_XBC + k + 1])
                            ins_.then_inc(xbc_begun, 1)
                    elif c.name == "xbc" and part < 3:
                        j = part - 1
                        act.wait_ge(drained[2 * p + j], lap(L, c.need[2 * p + j] + 1, FREE_LAP[2 * p + j]))
                        chain.link(act.activation(act_s[:, j, :], conv_s[:, j, :], ACT.Exp, scale=-1.0))
                        chain.sync()
                        sigmoid([act_s[:, j, :]], xbc_exp)
                    elif c.name in ("qc", "kc"):
                        wait_products(act, L, c)
                        dst = qcT if c.name == "qc" else kcT
                        act.activation(dst[:, 4 * c.index:4 * c.index + 2, :], tiles(2 * p), ACT.Copy).then_inc(drained[2 * p], 1)
                    elif c.name == "vc":
                        wait_products(act, L, c)
                        act.wait_ge(x_ready, x_count(L, 2))
                        act.activation(vc[:, 0, c.index * BANK:(c.index + 1) * BANK], bank(2 * p), ACT.Copy).then_inc(drained[2 * p], 1)
                    elif c.name == "gate":
                        drain_gate(L, c, part, lambda k: {"bias": small[:, 128 + k:129 + k]})
                    elif c.name == "branch" and c.r == 2 and part == 0:
                        for j in range(2):
                            k = 4 * c.index + 2 * j
                            act.wait_ge(mixed_sem, lap(L, 2 * c.index + j + 1, 4))
                            act.activation(xT_hi[:, k:k + 2, :], mT[:, k:k + 2, :], ACT.Copy).then_inc(m_hi, 1)

                def dt():
                    act.wait_ge(par_loaded, lap(L, 5 * 16, 5 * 16))
                    chain.link(act.activation(dts[:, 5, 0:NH], bcast[:, 272:288], ACT.Exp))
                    act.wait_ge(lam_arg, lap(L, 1, 1))
                    act.activation(small[:, 162:164], small[:, 160:162], ACT.Exp).then_inc(lam_exp, 1)
                    act.wait_ge(dt_arg, lap(L, 1, 1))
                    chain.link(act.activation(dts[:, 2, :], dts[:, 1, :], ACT.Exp, scale=-1.0))
                    chain.sync()
                    act.activation(dts[:, 3, :], dts[:, 2, :], ACT.Ln, bias=1.0).then_inc(dt_log, 1)

                def turn_qk(j):
                    if j % 2 == 0:
                        act.wait_ge(q_turned, lap(L, j // 2 + 1, 4))
                        if j == 0:
                            act.wait_ge(x_ready, x_count(L, 2))
                        act.activation(qT[:, j:j + 2, :], tiles(TB), ACT.Copy).then_inc(q_copied, 1)

                def dscore(u):
                    nk, at = P * (1 + u % 2), (u % 4) * 16
                    act.wait_ge(d_peak, lap(L, u + 1, 2 * DH))
                    if u >= 2:
                        act.wait_ge(d_turned, lap(L, u - 1, 2 * DH))
                    for m in range(2):
                        ins_ = act.activation(ex[:, u % 2, m * nk:(m + 1) * nk], sm[:, u % 2, m * nk:(m + 1) * nk], ACT.Exp,
                                              scale=-1.0, bias=small[:, at + m:at + m + 1], accum_out=small[:, at + 2 + m:at + 3 + m])
                    ins_.then_inc(d_exp, 1)

                def dturn(u):
                    nk = P * (1 + u % 2)
                    act.wait_ge(d_turned, lap(L, u + 1, 2 * DH))
                    if u >= 2:
                        act.wait_ge(d_out, lap(L, u - 1, 2 * DH))
                    act.activation(wt[:, u % 2, 0:nk], ps[:, TB, (u % 2) * TOK:(u % 2) * TOK + nk], ACT.Copy).then_inc(d_copied, 1)

                def dout(u):
                    act.wait_ge(d_out, lap(L, u + 1, 2 * DH))
                    if u:
                        act.wait_ge(d_sq, lap(L, u, 2 * DH))
                    o = ps[:, OB, (u % 4) * P:(u % 4 + 1) * P]
                    act.activation(oA[:, u % 2, (u // 2) * P:(u // 2 + 1) * P], o, ACT.Copy)
                    n = 184 + (u % 2) * DH + u // 2
                    act.activation(act_j[:, :], o, ACT.Square, accum_out=small[:, n:n + 1]).then_inc(d_sq, 1)

                def turn_oa(j):
                    act.wait_ge(oa_turned, lap(L, j + 1, 4))
                    if j == 0:
                        act.wait_ge(lam_ready, lap(L, 1, 1))
                    for place in (qT, kT_r):
                        ins_ = act.activation(place[:, 2 * j:2 * j + 2, :], tiles(TB + j % 2), ACT.Copy, scale=small[:, 166:167])
                    ins_.then_inc(oa_copied, 1)

                def turn_xs(j):
                    act.wait_ge(xs_turned, lap(L, j + 1, 4))
                    act.activation(xs[:, :, 2 * j * P:(2 * j + 2) * P], tiles(TB + j % 2), ACT.Copy).then_inc(xs_copied, 1)

                def sdecay(u):
                    act.wait_ge(seg_ready, lap(L, u + 1, NH))
                    if u < 2:
                        act.wait_ge(d_turned, lap(L, 2 * DH, 2 * DH))
                    else:
                        act.wait_ge(l_ready, lap(L, u - 1, NH))
                    act.activation(ex[:, u % 2, 0:CAUS], ps[:, S0 + u % 2, 0:CAUS], ACT.Exp).then_inc(seg_exp, 1)

                def ysquare(g):
                    act.wait_ge(y_gated, lap(L, 4 * (g + 1), NH // 2))
                    if g:
                        act.wait_ge(y_sum, lap(L, g, 2))
                    act.activation(wt[:, :, :].rearrange("p a n -> p (a n)"),
                                   zT[:, 4 * g:4 * g + 4, :].rearrange("p a n -> p (a n)"), ACT.Square).then_inc(y_sq, 1)

                def snorm(g):
                    r = sm[:, g, 0:TOK]
                    act.wait_ge(y_sum, lap(L, g + 1, 2))
                    act.wait_ge(y_gated, lap(L, NH // 2, NH // 2))
                    chain.link(act.activation(r, ps[:, TB + g, 0:TOK], ACT.Ln, scale=1.0 / (4 * P), bias=cst("ln_eps")))
                    chain.sync()
                    act.activation(r, r, ACT.Exp, scale=-0.5).then_inc(y_root, 1)

                def bsplit(g):
                    act.wait_ge(o_b, lap(L, g + 1, 2))
                    act.activation(xbc_r[:, 4 * g:4 * g + 4, :], zT[:, 4 * g:4 * g + 4, :], ACT.Copy).then_inc(ob_hi, 1)

                def kscore(u):
                    b = lmat[:, u % 2, :]
                    act.wait_ge(s_abs, lap(L, u + 1, NH))
                    chain.link(act.activation(b, b, ACT.Exp, scale=-1.0))
                    chain.sync()
                    act.activation(b, b, ACT.Ln, bias=1.0).then_inc(s_log, 1)

                def ksum(u):
                    act.wait_ge(s_arg, lap(L, u + 1, NH))
                    if u < 2:
                        act.wait_ge(l_ready, lap(L, NH, NH))
                    else:
                        act.wait_ge(s_out, lap(L, u - 1, NH))
                    act.activation(ex[:, u % 2, 0:CAUS], sm[:, u % 2, 0:CAUS], ACT.Exp).then_inc(s_exp, 1)

                def kout(u):
                    if u % 2:
                        p = u // 2
                        act.wait_ge(s_out, lap(L, u + 1, NH))
                        for place in (qcT, kcT_r):
                            ins_ = act.activation(place[:, p, :], ps[:, OB, 0:TOK], ACT.Copy)
                        ins_.then_inc(s_copied, 1)

                attention = dict(turn_qk=turn_qk, dscore=dscore, dturn=dturn, dout=dout, turn_oa=turn_oa, turn_xs=turn_xs,
                                 sdecay=sdecay, ysquare=ysquare, snorm=snorm, bsplit=bsplit, kscore=kscore, ksum=ksum, kout=kout, drain=drain)
                for slot in range(HIGHS):
                    split(L, ffn1["slot0"] + slot)
                ffn_silu(L, ffn1)
                act.preload_act_table_set("natural_log_exp_and_others")
                act.wait_ge(cols_ready, lap(L, 2, 1))
                layer_norm(0)
                split(L, mix[0].slot0 + 1)
                for step in mixed:
                    if step[0] == "dt":
                        dt()
                    elif step[0] == "split":
                        split_half(L, *step[1:])
                    elif step[0] in attention:
                        attention[step[0]](*step[1:])
                for slot in range(out2[0].slot0 + HIGHS, ffn2["slot0"] + 1):
                    split(L, slot)
                act.preload_act_table(ACT.Silu)
                layer_norm(1)
                split(L, ffn2["slot0"] + 1)
                ffn_silu(L, ffn2)
                layer_norm(2)
                chain.leave()

        @block.vector
        def _(dve):
            chain = Chain(dve, dve_chain)
            link, sync = chain.link, chain.sync

            roots = [0]

            def ask(ins_):
                ins_.then_inc(root_asked, 1)
                roots[0] += 1
                return roots[0]

            def ask_root(L, ins_):
                dve.wait_ge(root_done, lap(L, ask(ins_), ROOTS_LAP))

            def low(lo, whole, hi):
                return dve.tensor_tensor(lo, whole, hi.bitcast(F32), ALU.subtract)

            def split_half(L, s, q, it=0):
                dve.wait_ge(w_hi, lap(L, HALVES * s + q + 1, HALVES * SLOT_LAP) + it * (HALVES * SLOTS))
                low(half_of(ring_lo[:, s % SLOTS, :], s, q), half_of(ring[:, s % SLOTS, :], s, q), half_of(ring_hi[:, s % HIGHS, :], s, q))\
                    .then_inc(w_lo, 1)

            def split(L, s, it=0):
                for q in range(HALVES):
                    split_half(L, s, q, it)

            def down_splits(L, f):
                for s in range(f["slot0"] + 2 * FFC + HIGHS, f["slot0"] + 3 * FFC + f["ahead"]):
                    split(L, s)

            def hidden_parts(L, f, it, j):
                k = bass.ds(it * 4 + 2 * j, 2)
                dve.tensor_copy(h2_hi[:, k, :], h2[:, k, :]).then_inc(h_hi, 1)
                dve.wait_ge(h_hi, lap(L, f["h0"] + j + 1, 2 * FFC) + it * 2)
                low(h2_lo[:, k, :], h2[:, k, :], h2_hi[:, k, :]).then_inc(h_lo, 1)

            def norm_cols(L, event, g, b, dst, hi, lo, base=4):
                for t in range(T):
                    dve.wait_ge(hat_turned, lap(L, 4 * event + 2 * t + 2, 12))
                    for k in range(4):
                        o, i = dst[:, 4 + k, t * P:(t + 1) * P], ps[:, base + 1 + 2 * t, k * P:(k + 1) * P]
                        if g is None:
                            ins_ = dve.tensor_copy(o, i)
                        elif b is None:
                            ins_ = dve.tensor_scalar(o, i, g[:, 4 + k:5 + k], None, ALU.mult)
                        else:
                            ins_ = dve.tensor_scalar(o, i, g[:, 4 + k:5 + k], b[:, 4 + k:5 + k], ALU.mult, ALU.add)
                    link(ins_)
                    sync()
                    n = slice(t * P, (t + 1) * P)
                    link(dve.tensor_copy(hi[:, 4:8, n], dst[:, 4:8, n]))
                    sync()
                    link(low(lo[:, 4:8, n], dst[:, 4:8, n], hi[:, 4:8, n]))
                    dve.wait_ge(xT_act, lap(L, 2 * event + t + 1, 6))
                    low(lo[:, 0:4, n], dst[:, 0:4, n], hi[:, 0:4, n]).then_inc(xT_dve, 1)

            def rms_rows(src, event):
                for t in range(T):
                    r = small[:, 64 + 2 * event + t:65 + 2 * event + t]
                    dve.wait_ge(sq_ready, 2 * event + t + 1)
                    ask_root(None, dve.tensor_scalar(r, r, D * RMS_EPS, None, ALU.add))
                    if event == 1:
                        dve.wait_ge(hat_turned, 2 * t + 2)
                    dve.tensor_scalar(xhat[:, t, :], src[:, t, :], r, float(D) ** 0.5, ALU.mult, ALU.mult).then_inc(hat_ready, 1)

            def ffn_mul(L, f):
                def up(it, js):
                    for j in js:
                        b = 2 * j
                        split(L, f["slot0"] + b + HIGHS, it)
                        split_half(L, f["slot0"] + b + 1 + HIGHS, 0, it)
                        dve.wait_ge(drained[b], lap(L, f["free0"][b] + 1, FREE_LAP[b]) + it)
                        dve.wait_ge(multiplied, lap(L, f["slot0"] + b + 2, SLOT_LAP) + it * 4)
                        dve.tensor_tensor(h2[:, bass.ds(it * 4 + 2 * j, 2), :].rearrange("p a n -> p (a n)"),
                                          act_s[:, j, :], bank(b + 1), ALU.mult).then_inc(drained[b + 1], 1)
                        split_half(L, f["slot0"] + b + 1 + HIGHS, 1, it)
                        dve.wait_ge(drained[b + 1], lap(L, f["free0"][b + 1] + 1, FREE_LAP[b + 1]) + it)
                        hidden_parts(L, f, it, j)

                with dve.Fori(0, FFC // 2) as it:
                    up(it, range(2))
                up(FFC // 2, range(1))
                down_splits(L, f)

            def ffn_conv(f):
                def up(it, js):
                    for j in js:
                        for side in range(2):
                            split(None, f["slot0"] + 2 * j + side + HIGHS, it)
                        dve.wait_ge(conv_begun, it * 2 + j + 1)
                        for tap in (1, 0):
                            s = 2 - tap
                            if tap == 0:
                                dve.wait_ge(conv_tap, it * 2 + j + 1)
                            for side, dst in enumerate((act_s, conv_s)):
                                for ft in range(2):
                                    tile = it * 4 + (2 * j + ft + side * KF)
                                    o = dst[:, j, ft * TOK + s:(ft + 1) * TOK]
                                    ins_ = dve.scalar_tensor_tensor(
                                        o, tiles(2 * j + side)[:, ft, 0:TOK - s],
                                        conv1[:, bass.ds(tile + tap * 2 * KF, 1)], o, ALU.mult, ALU.add)
                                if tap == 0:
                                    ins_.then_inc(drained[2 * j + side], 1)
                            if tap == 1:
                                ins_.then_inc(conv_tap, 1)
                        dve.wait_ge(act_ready, it * 2 + j + 1)
                        dve.wait_ge(drained[2 * j + 1], f["free0"][2 * j + 1] + it + 1)
                        dve.tensor_tensor(h2[:, bass.ds(it * 4 + 2 * j, 2), :].rearrange("p a n -> p (a n)"),
                                          act_s[:, j, :], conv_s[:, j, :], ALU.mult).then_inc(h_ready, 1)
                        dve.wait_ge(h_ready, it * 2 + j + 3)
                        hidden_parts(None, f, it, j)

                dve.sem_inc(h_ready, 2)
                with dve.Fori(0, FFC // 2) as it:
                    up(it, range(2))
                up(FFC // 2, range(1))
                down_splits(None, f)

            dve.wait_ge(in_loaded, 2 * 16)
            for slot in range(HIGHS):
                split(None, slot)
            dve.wait_ge(rows1_turned, 1)
            dve.tensor_copy(conv1[:, :], ps[:, 4, 0:N_CONV1 + N_ROWS1]).then_inc(cols_ready, 1)
            dve.wait_ge(cols_ready, 1)
            rms_rows(x, 0)
            norm_cols(None, 0, conv1[:, N_CONV1:N_CONV1 + 8], None, xT, xT_hi, xT_lo)
            gain = gains1.rearrange("p (a d) -> p a d", d=HD)

            def angles():
                dve.wait_ge(par1_loaded, 8 * 16)
                posf, ang, turns, red = small[:, 80:82], kcT[:, 6, 0:64], kcT[:, 6, 64:128], kcT[:, 7, 0:128]
                link(dve.tensor_copy(posf, pos[:, :]))
                sync()
                for t in range(T):
                    link(dve.tensor_scalar(ang[:, 32 * t:32 * t + 32], cst("freq"), posf[:, t:t + 1], None, ALU.mult))
                sync()
                link(dve.tensor_scalar(turns, ang, float(1 / (2 * np.pi)), 12582912.0, ALU.mult, ALU.add))
                sync()
                link(dve.tensor_scalar(turns, turns, 12582912.0, None, ALU.subtract))
                sync()
                c1 = 6.28125
                c2 = int((2 * np.pi - c1) * 2 ** 20) / 2 ** 20
                c3 = float(2 * np.pi - c1 - c2)
                for c in (c1, c2, c3):
                    link(dve.scalar_tensor_tensor(ang, turns, -c, ang, ALU.mult, ALU.add))
                    sync()
                halfpi = float(np.float32(np.pi / 2))
                pi_in = 3.1415925
                link(dve.tensor_scalar(red[:, 0:64], ang, pi_in, -pi_in, ALU.min, ALU.max))
                link(dve.tensor_scalar(red[:, 64:128], ang, halfpi, None, ALU.add))
                sync()
                link(dve.tensor_scalar(turns, red[:, 64:128], float(np.pi), -2 * float(np.pi), ALU.is_gt, ALU.mult))
                sync()
                link(dve.tensor_tensor(red[:, 64:128], red[:, 64:128], turns, ALU.add))
                sync()
                dve.tensor_scalar(red[:, 64:128], red[:, 64:128], pi_in, -pi_in, ALU.min, ALU.max).then_inc(angle_ready, 1)

            def memory():
                rms_rows(gb, 1)
                norm_cols(None, 1, conv1[:, N_CONV1 + 8:N_CONV1 + 16], None, memT, *acts["memT"])

            def rot(i, t):
                return qcT[:, i, t * HD:(t + 1) * HD], qcT[:, i, P + t * HD:P + (t + 1) * HD]

            def rotations():
                dve.wait_ge(sin_ready, 1)
                sin, cos = kcT[:, 7, 128:192], kcT[:, 7, 192:256]
                link(dve.tensor_scalar(gains1, gains1, float(HD) ** 0.5, None, ALU.mult))
                sync()

                for i in range(4):
                    for t in range(T):
                        c_, s_ = rot(i, t)
                        ct, st = cos[:, 32 * t:32 * t + 32], sin[:, 32 * t:32 * t + 32]
                        lo, hi = slice(0, 32), slice(32, HD)
                        link(dve.tensor_tensor(c_[:, lo], gain[:, i, lo], ct, ALU.mult))
                        link(dve.tensor_tensor(c_[:, hi], gain[:, i, hi], ct, ALU.mult))
                        link(dve.scalar_tensor_tensor(s_[:, lo], gain[:, i, hi], -1.0, st, ALU.mult, ALU.mult))
                        link(dve.tensor_tensor(s_[:, hi], gain[:, i, lo], st, ALU.mult))
                sync()

            def norm1(n, t):
                col, heads, i, turned = NORMED[n]
                v = tok1[:, t, col:col + heads * HD].rearrange("p (h d) -> p h d", d=HD)
                turn, rx = (a.rearrange("p a n -> p (a n)")[:, 0:heads * HD].rearrange("p (h d) -> p h d", d=HD)
                            for a in (kcT[:, 4:6, :], qcT[:, 6:8, :]))
                r = small[:, 84:84 + heads]
                dve.wait_ge(sq1_done, 2 * n + t + 1)
                if n or t:
                    dve.wait_ge(norm1_done, 2 * n + t)
                link(dve.tensor_reduce(r, squares1(n, t).rearrange("p (h d) -> p h d", d=HD), AX_X, ALU.add))
                sync()
                root_at = ask(dve.tensor_scalar(r, r, HD * RMS_EPS, None, ALU.add))
                if turned:
                    c_, s_ = (a.unsqueeze(1).to_broadcast([P, heads, HD]) for a in rot(i, t))
                    link(dve.tensor_tensor(turn, v, c_, ALU.mult))
                    link(dve.tensor_tensor(rx[:, :, 0:32], v[:, :, 32:HD], s_[:, :, 0:32], ALU.mult))
                    link(dve.tensor_tensor(rx[:, :, 32:HD], v[:, :, 0:32], s_[:, :, 32:HD], ALU.mult))
                    sync()
                    link(dve.tensor_tensor(turn, turn, rx, ALU.add))
                else:
                    link(dve.tensor_tensor(turn, v, gain[:, i, :].unsqueeze(1).to_broadcast([P, heads, HD]), ALU.mult))
                sync()
                dve.wait_ge(root_done, root_at)
                dve.tensor_tensor(v, turn, r.unsqueeze(2).to_broadcast([P, heads, HD]), ALU.mult).then_inc(norm1_done, 1)

            def drain1(c, part):
                if c.name == "tok" and part % 2 == 0:
                    wait_drained(dve, None, c)
                    norm1(c.index, part // 2)

            def keys1(u):
                return P if u % 2 == 0 and u // 2 < 6 else TOK

            def peak(L, u, nk, per, masked, peak_):
                at = (u % 4) * 16
                dve.wait_ge(masked, lap(L, u + 1, per))
                dve.tensor_reduce(small[:, at:at + 2], sm[:, u % 2, 0:2 * nk].rearrange("p (m k) -> p m k", k=nk), AX_X, ALU.min).then_inc(peak_, 1)

            def score1(u):
                p, qt, nk = u // 2, u % 2, keys1(u)
                dve.wait_ge(score1_ready, u + 1)
                if u >= 2:
                    dve.wait_ge(exp1, u - 1)
                o = sm[:, u % 2, 0:2 * nk].rearrange("p (m k) -> p m k", k=nk)
                i = ps[:, S0:S0 + 2, (u % 2) * TOK:(u % 2) * TOK + nk]
                if p < 6:
                    m = cst("moba_far" if p < 3 else "dil_far")[:, P * qt:P * qt + nk]
                    dve.scalar_tensor_tensor(o, i, -SCALE, m.unsqueeze(1).to_broadcast([P, 2, nk]), ALU.mult, ALU.add).then_inc(masked1, 1)
                else:
                    dve.tensor_scalar(o, i, -SCALE, None, ALU.mult).then_inc(masked1, 1)
                peak(None, u, nk, 0, masked1, peak1)

            def weigh1(u):
                nk, at = keys1(u), (u % 4) * 16
                dve.wait_ge(exp1, u + 1)
                link(dve.reciprocal(small[:, at + 4:at + 6], small[:, at + 2:at + 4]))
                sync()
                for m in range(2):
                    e = ex[:, u % 2, m * nk:(m + 1) * nk]
                    ins_ = dve.tensor_scalar(e, e, small[:, at + 4 + m:at + 5 + m], None, ALU.mult)
                ins_.then_inc(prob1, 1)

            def split_out1(p):
                dve.wait_ge(out1_copied, 2 * p + 2)
                low(acts["o1T"][1][:, p, :], o1T[:, p, :], acts["o1T"][0][:, p, :]).then_inc(o1_split, 1)

            preparations = dict(angles=angles, memory=memory, rotations=rotations)
            for step in split_later(steps1):
                if step[0] in preparations:
                    preparations[step[0]]()
                elif step[0] == "drain":
                    drain1(*step[1:])
                elif step[0] == "split":
                    split_half(None, *step[1:])
                elif step[0] == "score1":
                    score1(step[1])
                elif step[0] == "weigh1":
                    weigh1(step[1])
                elif step[0] == "out1" and step[1] % 2 and step[1] > 1:
                    split_out1(step[1] // 2 - 1)
            split_out1(PAIRS - 1)
            dve.wait_ge(gate_ready, 12)
            for j in range(4):
                b = 4 * (j % 2)
                dve.wait_ge(multiplied, branch1_slot0 + j + 1)
                if j:
                    dve.wait_ge(mixed1, j)
                parts = [mT[:, 2 * j:2 * j + 2, :].rearrange("p a n -> p (a n)"), act_s[:, 0, :], act_s[:, 1, :]]
                for r in range(3):
                    e = wide[:, 8 * r + 2 * j:8 * r + 2 * j + 2, :].rearrange("p a n -> p (a n)")
                    ins_ = dve.tensor_tensor(parts[r], bank(b + r), e, ALU.mult)
                    if r < 2:
                        link(ins_)
                ins_.then_inc(branch1_free, 1)
                sync()
                link(dve.tensor_tensor(parts[0], parts[0], parts[1], ALU.add))
                sync()
                dve.wait_ge(branch1_free, j + 1)
                dve.tensor_tensor(parts[0], parts[0], parts[2], ALU.add).then_inc(mixed1, 1)
                split(None, branch1_slot0 + j + HIGHS)
                dve.wait_ge(m_hi, j + 1)
                k = slice(2 * j, 2 * j + 2)
                low(mT_lo[:, k, :], mT[:, k, :], xT_hi[:, k, :]).then_inc(m_split, 1)
            for slot in range(out1[0].slot0 + HIGHS, ffn0["slot0"] + 1):
                split(None, slot)

            def add_x(L, slots, event, s, t, base):
                if t == 0:
                    dve.wait_ge(tile_done, lap(L, event - 1, 3))
                else:
                    dve.wait_ge(multiplied, lap(L, slots, SLOT_LAP))
                out_pair = {c.index: c.pair for c in (out1 if L is None else out2)}
                for n in range(2):
                    xv = x[:, t, n * BANK:(n + 1) * BANK]
                    b = base + 2 * n + t if base == DOWN else 2 * out_pair[n] + t
                    ins_ = dve.scalar_tensor_tensor(xv, bank(b), s, xv, ALU.mult, ALU.add)
                    if base == DOWN:
                        link(ins_)
                    else:
                        ins_.then_inc(drained[b], 1)

            def wait_added(L, t, base, free):
                if base == DOWN:
                    sync()
                else:
                    for b in (t, 2 + t):
                        dve.wait_ge(drained[b], lap(L, free[b], FREE_LAP[b]))

            for t in range(T):
                add_x(None, out1[1].slot0 + 2, 2, 1.0, t, 0)
                wait_added(None, t, 0, ffn0["free0"])
                dve.sem_inc(x_added, 1)
            rms_rows(x, 2)
            norm_cols(None, 2, conv1[:, N_CONV1 + 16:N_CONV1 + 24], None, xT, xT_hi, xT_lo)
            split(None, ffn0["slot0"] + 1)
            ffn_conv(ffn0)
            for t in range(T):
                add_x(None, ffn0["slot0"] + 3 * FFC, 3, 1.0, t, DOWN)
                wait_added(None, t, DOWN, None)
                dve.sem_inc(hat_ready, 1)
            norm_cols(None, 3, None, None, xT, xT_hi, xT_lo, 0)

            with dve.Fori(0, LAYERS) as L:
                chain.enter(L)

                def layer_norm(k, slots, s, free=None):
                    dve.wait_ge(x_ready, x_count(L, 2 * k))
                    base = 0 if k == 1 else DOWN
                    for t in range(T):
                        add_x(L, slots, 4 + k, s, t, base)
                        wait_added(L, t, base, free)
                        st = stats[:, t, :]
                        v = small[:, 96 + 4 * t:100 + 4 * t]
                        for n in range(2):
                            link(dve.bn_stats(st[:, 6 * n:6 * n + 6], x[:, t, n * BANK:(n + 1) * BANK]))
                        sync()
                        dve.memset(small[:, 250:251], 0.0)
                        link(dve.bn_aggr(v[:, 0:2], st))
                        sync()
                        ask_root(L, dve.tensor_scalar(v[:, 2:3], v[:, 1:2], LN_EPS / ALPHA ** 2, None, ALU.add))
                        dve.scalar_tensor_tensor(v[:, 3:4], v[:, 0:1], -1.0, v[:, 2:3], ALU.mult, ALU.mult).then_inc(stat_ready, 1)
                    g, b = ROWS2["ln_g"][k], ROWS2["ln_b"][k]
                    norm_cols(L, 4 + k, cols[:, g:g + 8], cols[:, b:b + 8], xT, xT_hi, xT_lo, 4 if k == 1 else 0)

                def turn_rows():
                    dve.wait_ge(rows_turned, lap(L, 1, 1))
                    dve.wait_ge(xT_act, lap(L, 8, 6))
                    dve.wait_ge(xT_dve, lap(L, 8, 6))
                    link(dve.tensor_copy(cols[:, 0:N_ROWS2], ps[:, 3, 0:N_ROWS2]))
                    link(dve.tensor_copy(cols[:, P:P + N_CONV2], ps[:, 3, P:P + N_CONV2]))
                    sync()
                    g = ROWS2["gate_b"]
                    dve.tensor_scalar(small[:, 128:152], cols[:, g:g + 24], -1.0, None, ALU.mult).then_inc(cols_ready, 1)

                def drain(c, part):
                    p = c.pair
                    if part and c.name in ("qc", "kc", "vc"):
                        return
                    if c.name in ("qa", "ka") and part < T:
                        dst = qa if c.name == "qa" else ka
                        if part == 0:
                            wait_products(dve, L, c)
                        for t in (part,):
                            dve.wait_ge(drained[2 * p + t], lap(L, c.need[2 * p + t] + 1, FREE_LAP[2 * p + t]))
                            i = bank(2 * p + t).rearrange("p (m d) -> p m d", d=HD)
                            o = dst[:, t, c.index * BANK:(c.index + 1) * BANK].rearrange("p (m d) -> p m d", d=HD)
                            a, r = (sm[:, n, t * TOK:t * TOK + P].rearrange("p (m d) -> p m d", d=16) for n in range(2))
                            cs = cst("cos")[:, 16 * t:16 * t + 16].unsqueeze(1).to_broadcast([P, 8, 16])
                            sn = cst("sin")[:, 16 * t:16 * t + 16].unsqueeze(1).to_broadcast([P, 8, 16])
                            link(dve.tensor_tensor(a, i[:, :, 0:16], cs, ALU.mult))
                            link(dve.tensor_tensor(r[:, :, 0:8], i[:, :, 8:16], sn[:, :, 0:8], ALU.mult))
                            link(dve.tensor_tensor(r[:, :, 8:16], i[:, :, 0:8], sn[:, :, 8:16], ALU.mult))
                            sync()
                            dve.tensor_tensor(o[:, :, 0:16], a, r, ALU.add).then_inc(drained[2 * p + t], 1)
                    elif c.name == "zb" and part == 1:
                        for j in range(2):
                            dve.wait_ge(z_exp, lap(L, 2 * c.index + j + 1, 4))
                            k = 4 * c.index + 2 * j
                            dve.tensor_tensor(zT[:, k:k + 2, :], tiles(2 * p + j), feats_of(conv_s[:, j, :]), ALU.mult).then_inc(drained[2 * p + j], 1)
                    elif c.name == "xbc" and part < 2:
                        j = part
                        dve.wait_ge(xbc_begun, lap(L, 2 * c.index + j + 1, 6))
                        for s in (1, 2, 3):
                            for f in range(2):
                                k = P + (3 - s) * N_XBC + 4 * c.index + 2 * j + f
                                o = conv_s[:, j, f * TOK + s:(f + 1) * TOK]
                                ins_ = dve.scalar_tensor_tensor(o, tiles(2 * p + j)[:, f, 0:TOK - s], cols[:, k:k + 1], o, ALU.mult, ALU.add)
                                if s < 3:
                                    link(ins_)
                            if s < 3:
                                sync()
                        ins_.then_inc(drained[2 * p + j], 1)
                    elif c.name == "xbc":
                        j = part - 2
                        dve.wait_ge(xbc_exp, lap(L, 2 * c.index + j + 1, 6))
                        k = 4 * c.index + 2 * j
                        dve.tensor_tensor(xbc[:, k:k + 2, :], feats_of(act_s[:, j, :]), feats_of(conv_s[:, j, :]), ALU.mult).then_inc(xbc_done, 1)
                    elif c.name in ("qc", "kc"):
                        wait_products(dve, L, c)
                        dst = qcT if c.name == "qc" else kcT
                        dve.tensor_copy(dst[:, 4 * c.index + 2:4 * c.index + 4, :], tiles(2 * p + 1)).then_inc(drained[2 * p + 1], 1)
                    elif c.name == "vc":
                        wait_products(dve, L, c)
                        dve.wait_ge(x_ready, x_count(L, 2))
                        dve.tensor_copy(vc[:, 1, c.index * BANK:(c.index + 1) * BANK], bank(2 * p + 1)).then_inc(drained[2 * p + 1], 1)
                    elif c.name == "branch" and (part == 0 or c.r < 2 and part == 1):
                        if part == 0:
                            wait_products(dve, L, c)
                        if c.r == 0 and c.index == 0 and part == 0:
                            dve.wait_ge(gate_ready, lap(L, 24, 12))
                        for j in range(2) if c.r == 2 else (part,):
                            k = 4 * c.index + 2 * j
                            e = wide[:, 8 * c.r + k:8 * c.r + k + 2, :].rearrange("p a n -> p (a n)")
                            m = mT[:, k:k + 2, :].rearrange("p a n -> p (a n)")
                            b = 2 * p + j
                            dve.tensor_tensor(m if c.r == 0 else conv_s[:, j, :], bank(b), e, ALU.mult).then_inc(drained[b], 1)
                            if c.r:
                                dve.wait_ge(drained[b], lap(L, c.need[b] + 1, FREE_LAP[b]))
                                ins_ = dve.tensor_tensor(m, m, conv_s[:, j, :], ALU.add)
                                if c.r == 2:
                                    ins_.then_inc(mixed_sem, 1)
                                else:
                                    link(ins_)
                                    sync()
                    elif c.name == "branch" and c.r == 2 and part == 1:
                        for j in range(2):
                            k = slice(4 * c.index + 2 * j, 4 * c.index + 2 * j + 2)
                            dve.wait_ge(m_hi, lap(L, 4 + 2 * c.index + j + 1, 4))
                            low(mT_lo[:, k, :], mT[:, k, :], xT_hi[:, k, :]).then_inc(m_split, 1)

                def dt():
                    dve.wait_ge(par_loaded, lap(L, 5 * 16, 5 * 16))
                    lf = bcast[:, 0:4 * HD].rearrange("p (a b d) -> p a b d", a=2, b=2)
                    pr = dts[:, 0:4, :].rearrange("p a n -> p (a n)").rearrange("p (a d) -> p a d", d=HD)
                    link(dve.tensor_tensor(pr, lf[:, :, 0, :], lf[:, :, 1, :], ALU.mult))
                    sync()
                    dve.tensor_reduce(small[:, 160:162], pr, AX_X, ALU.add).then_inc(lam_arg, 1)
                    link(dve.tensor_copy(small[:, 168:170], const[:, bass.ds(L * 2 + CONST["lam"][0], 2)]))
                    sync()
                    dve.wait_ge(lam_exp, lap(L, 1, 1))
                    link(dve.tensor_tensor(small[:, 164:165], small[:, 163:164], small[:, 162:163], ALU.subtract))
                    link(dve.tensor_scalar(small[:, 166:167], cols[:, ROWS2["subln"]:ROWS2["subln"] + 1], small[:, 169:170], None, ALU.mult))
                    sync()
                    dve.tensor_tensor(small[:, 165:166], small[:, 164:165], small[:, 168:169], ALU.subtract).then_inc(lam_ready, 1)
                    for m in range(2):
                        link(dve.tensor_copy(small[HD * m:HD * (m + 1), 168 + 32:176 + 32], bcast[HD * m:HD * (m + 1), 288 + m:304:2]))
                    dve.wait_ge(dt_ready, lap(L, 1, 1))
                    two = lambda n: dts[:, n, :].rearrange("p (t h) -> p t h", t=T)
                    over_t = lambda a: a.unsqueeze(1).to_broadcast([P, T, NH])
                    link(dve.tensor_tensor(two(0), ps[:, OB, 0:T * NH].rearrange("p (t h) -> p t h", t=T), over_t(bcast[:, 256:272]), ALU.add))
                    sync()
                    dve.scalar_tensor_tensor(dts[:, 1, :], dts[:, 0, :], -1.0, dts[:, 0, :], ALU.mult, ALU.max).then_inc(dt_arg, 1)
                    dve.wait_ge(dt_log, lap(L, 1, 1))
                    link(dve.scalar_tensor_tensor(dts[:, 2, :], dts[:, 0, :], 0.0, dts[:, 3, :], ALU.max, ALU.add))
                    sync()
                    dve.scalar_tensor_tensor(two(4), two(2), -1.0, over_t(dts[:, 5, 0:NH]), ALU.mult, ALU.mult).then_inc(dt_done, 1)

                def turn_qk(j):
                    if j % 2:
                        dve.wait_ge(k_turned, lap(L, j // 2 + 1, 4))
                        dve.tensor_copy(kT[:, j - 1:j + 1, :], tiles(OB)).then_inc(k_copied, 1)

                def dscore(u):
                    qt = u % 2
                    nk = P * (1 + qt)
                    dve.wait_ge(d_score, lap(L, u + 1, 2 * DH))
                    if u >= 2:
                        dve.wait_ge(d_exp, lap(L, u - 1, 2 * DH))
                    o = sm[:, u % 2, 0:2 * nk].rearrange("p (m k) -> p m k", k=nk)
                    i = ps[:, S0:S0 + 2, (u % 2) * TOK:(u % 2) * TOK + nk]
                    m = cst("chunk_far")[:, P * qt:P * qt + nk].unsqueeze(1).to_broadcast([P, 2, nk])
                    dve.scalar_tensor_tensor(o, i, -SCALE, m, ALU.mult, ALU.add).then_inc(d_masked, 1)
                    peak(L, u, nk, 2 * DH, d_masked, d_peak)

                def dweigh(u):
                    nk, at = P * (1 + u % 2), (u % 4) * 16
                    dve.wait_ge(d_exp, lap(L, u + 1, 2 * DH))
                    if u == 0:
                        dve.wait_ge(lam_ready, lap(L, 1, 1))
                    e0, e1 = (ex[:, u % 2, m * nk:(m + 1) * nk] for m in range(2))
                    link(dve.reciprocal(small[:, at + 4:at + 6], small[:, at + 2:at + 4]))
                    sync()
                    link(dve.tensor_scalar(e0, e0, small[:, at + 4:at + 5], None, ALU.mult))
                    link(dve.tensor_tensor(small[:, at + 6:at + 7], small[:, at + 5:at + 6], small[:, 165:166], ALU.mult))
                    sync()
                    dve.scalar_tensor_tensor(e0, e1, small[:, at + 6:at + 7], e0, ALU.mult, ALU.add).then_inc(d_w, 1)

                def dnorm(_):
                    r = small[:, 184:184 + 2 * DH]
                    dve.wait_ge(d_sq, lap(L, 2 * DH, 2 * DH))
                    ask_root(L, dve.tensor_scalar(r, r, 1.0 / P, LN_EPS, ALU.mult, ALU.add))
                    for t in range(T):
                        o = oA[:, t, :].rearrange("p (h d) -> p h d", d=P)
                        dve.tensor_tensor(o, o, r[:, t * DH:(t + 1) * DH].unsqueeze(2).to_broadcast([P, DH, P]), ALU.mult).then_inc(d_norm, 1)

                def turn_oa(j):
                    dve.wait_ge(oa_copied, lap(L, j + 1, 4))
                    k = slice(2 * j, 2 * j + 2)
                    low(qT_r[:, k, :], qT[:, k, :], kT_r[:, k, :]).then_inc(oa_split, 1)

                def bsplit(g):
                    k = slice(4 * g, 4 * g + 4)
                    dve.wait_ge(ob_hi, lap(L, g + 1, 2))
                    low(zT_lo[:, k, :], zT[:, k, :], xbc_r[:, k, :]).then_inc(ob_split, 1)

                def osplit(u):
                    if u % 2:
                        p = u // 2
                        dve.wait_ge(s_copied, lap(L, p + 1, NH // 2))
                        low(qcT_r[:, p, :], qcT[:, p, :], kcT_r[:, p, :]).then_inc(oc_split, 1)

                def cb(g):
                    dve.wait_ge(cb_ready, lap(L, g + 1, 2))
                    dve.tensor_tensor(cbm[:, g, :], ps[:, S0 + g, 0:CAUS], cst("causal"), ALU.mult).then_inc(cb_masked, 1)

                def sdecay(u):
                    dve.wait_ge(seg_exp, lap(L, u + 1, NH))
                    if u == 0:
                        dve.wait_ge(cb_masked, lap(L, 2, 2))
                    if u >= 2:
                        dve.wait_ge(y_ready, lap(L, u - 1, NH))
                    g = u // (NH // 2)
                    for t, r in enumerate((slice(0, TOK), slice(TOK, CAUS))):
                        ins_ = dve.scalar_tensor_tensor(lmat[:, u % 2, r], ex[:, u % 2, r], dts[:, 2, t * NH + u:t * NH + u + 1],
                                                        cbm[:, g, r], ALU.mult, ALU.mult)
                    ins_.then_inc(l_ready, 1)

                def sout(u):
                    if u % 2:
                        p = u // 2
                        dve.wait_ge(y_ready, lap(L, u + 1, NH))
                        d = small[:, 200 + p:201 + p]
                        s = sm[:, p % 2, 0:TOK]
                        link(dve.scalar_tensor_tensor(s, xbc[:, p, :], d, ps[:, TB + p % 2, 0:TOK], ALU.mult, ALU.add))
                        sync()
                        dve.tensor_tensor(zT[:, p, :], s, zT[:, p, :], ALU.mult).then_inc(y_gated, 1)

                def snorm(g):
                    dve.wait_ge(y_root, lap(L, g + 1, 2))
                    r = sm[:, g, 0:TOK]
                    for k in range(4 * g, 4 * g + 4):
                        w = cols[:, ROWS2["norm"] + k:ROWS2["norm"] + k + 1]
                        ins_ = dve.scalar_tensor_tensor(zT[:, k, :], zT[:, k, :], w, r, ALU.mult, ALU.mult)
                    ins_.then_inc(o_b, 1)

                def kscore(u):
                    z = sm[:, u % 2, 0:CAUS]
                    if u == 0:
                        dve.wait_ge(o_b, lap(L, 2, 2))
                    dve.wait_ge(s_score, lap(L, u + 1, NH))
                    if u >= 2:
                        dve.wait_ge(s_exp, lap(L, u - 1, NH))
                        dve.wait_ge(s_sum, lap(L, u - 1, NH))
                    dve.scalar_tensor_tensor(z, ps[:, S0 + u % 2, 0:CAUS], SCALE, cst("strict_neg"), ALU.mult, ALU.add).then_inc(s_masked, 1)
                    dve.wait_ge(s_masked, lap(L, u + 1, NH))
                    dve.scalar_tensor_tensor(lmat[:, u % 2, :], z, -1.0, z, ALU.mult, ALU.max).then_inc(s_abs, 1)

                def ksoft(u):
                    dve.wait_ge(s_log, lap(L, u + 1, NH))
                    b = lmat[:, u % 2, :]
                    dve.scalar_tensor_tensor(b, sm[:, u % 2, 0:CAUS], 0.0, b, ALU.max, ALU.add).then_inc(s_soft, 1)

                def ksum(u):
                    z = sm[:, u % 2, 0:CAUS]
                    dve.wait_ge(s_sum, lap(L, u + 1, NH))
                    dve.tensor_tensor(z, z, ps[:, TB, 0:CAUS], ALU.subtract).then_inc(s_arg, 1)

                attention = dict(turn_qk=turn_qk, dscore=dscore, dweigh=dweigh, dnorm=dnorm, cb=cb, sdecay=sdecay, sout=sout,
                                 turn_oa=turn_oa, bsplit=bsplit, osplit=osplit, snorm=snorm, kscore=kscore, ksoft=ksoft, ksum=ksum, drain=drain)
                for slot in range(HIGHS):
                    split(L, ffn1["slot0"] + slot)
                ffn_mul(L, ffn1)
                turn_rows()
                layer_norm(0, ffn1["slot0"] + 3 * FFC, FFN_RES / ALPHA)
                split(L, mix[0].slot0 + 1)
                for step in split_later(mixed):
                    if step[0] == "dt":
                        dt()
                    elif step[0] == "split":
                        split_half(L, *step[1:])
                    elif step[0] in attention:
                        attention[step[0]](*step[1:])
                for slot in range(out2[0].slot0 + HIGHS, ffn2["slot0"] + 1):
                    split(L, slot)
                layer_norm(1, out2[1].slot0 + 2, 1 / ALPHA, out2[1].after)
                split(L, ffn2["slot0"] + 1)
                ffn_mul(L, ffn2)
                layer_norm(2, ffn2["slot0"] + 3 * FFC, FFN_RES / ALPHA)
                chain.leave()

        @block.gpsimd
        def _(pool):
            chain = Chain(pool, pool_chain)
            link, sync = chain.link, chain.sync
            pool.sem_inc(x_ready, 1)
            roots = [0]

            def root(L, a):
                roots[0] += 1
                pool.wait_ge(root_asked, lap(L, roots[0], ROOTS_LAP))
                n = a.shape[-1]
                pool.tensor_tensor(a, a, cst("minus_half").to_broadcast([P, n]), ALU.pow).then_inc(root_done, 1)

            pool.wait_ge(in_loaded, 2 * 16)
            for t in range(T):
                root(None, small[:, 64 + t:65 + t])
            for step in steps1:
                if step[0] == "memory":
                    for t in range(T):
                        root(None, small[:, 66 + t:67 + t])
                elif step[0] == "drain" and step[1].name == "tok" and step[2] % 2 == 0:
                    root(None, small[:, 84:84 + NORMED[step[1].index][1]])
            for t in range(T):
                root(None, small[:, 64 + 4 + t:65 + 4 + t])
            with pool.Fori(0, LAYERS) as L:
                chain.enter(L)

                def residual(k):
                    for t in range(T):
                        root(L, small[:, 98 + 4 * t:99 + 4 * t])
                    pool.wait_ge(gb_loaded, lap(L, 32 * (k + 1), 96))
                    for t in range(T):
                        pool.wait_ge(hat_ready, lap(L, 2 * (4 + k) + t + 1, 6))
                        link(pool.tensor_tensor(x[:, t, :], xhat[:, t, :], gb[:, 0, :], ALU.mult))
                        sync()
                        pool.tensor_tensor(x[:, t, :], x[:, t, :], gb[:, 1, :], ALU.add).then_inc(x_ready, 1)

                def sdecay(u):
                    if u == 0:
                        pool.wait_ge(dt_done, lap(L, 1, 1))
                        pool.wait_ge(xbc_done, lap(L, 6, 6))
                    if u >= 2:
                        pool.wait_ge(seg_ready, lap(L, u - 1, NH))
                    for n, (m, t) in enumerate(((after, 0), (after, 1), (ones, 1))):
                        ins_ = pool.tensor_tensor(seg_w[:, u % 2, n * P:(n + 1) * P], m,
                                                  dts[:, 4, t * NH + u:t * NH + u + 1].to_broadcast([P, P]), ALU.mult)
                    ins_.then_inc(seg_built, 1)

                residual(0)
                for step in mixed:
                    if step[0] == "sdecay":
                        sdecay(step[1])
                    elif step[0] == "dnorm":
                        root(L, small[:, 184:184 + 2 * DH])
                residual(1)
                residual(2)
                chain.leave()
            pool.wait_ge(x_ready, x_count(LAYERS, 0))
            pool.dma_start(out[0].rearrange("(t p) n -> p t n", p=P), x[:, :, :]).then_inc(out_stored, 16)
            pool.wait_ge(out_stored, 16)

    return nc


INPUTS = ["x", "mem", "positions", "mix_norm_g", "mem_norm_g", "w_in", "moba_q_norm_g", "moba_k_norm_g", "dil_q_norm_g",
          "dil_k_norm_g", "mem_q_norm_g", "mem_k_norm_g", "w_mem_kv", "w_branch_moba", "w_branch_dil", "w_branch_mem", "w_out",
          "ffn_norm_g", "w_ffn_up", "ffn_conv_w", "ffn_conv_b", "w_ffn_down", "ffn1_w_in_2", "ffn1_w_out_2", "ln1_g_2",
          "ln1_b_2", "w_mix_in_2", "gate_bias_2", "diff_lambda_2", "diff_subln_g_2", "ssm_conv_w_2", "ssm_conv_b_2",
          "ssm_dt_bias_2", "ssm_A_log_2", "ssm_D_2", "ssm_norm_g_2", "w_branch_2", "w_mix_out_2", "ln2_g_2", "ln2_b_2",
          "ffn2_w_in_2", "ffn2_w_out_2", "ln3_g_2", "ln3_b_2"]


def kernel(**inputs):
    import concourse.bacc as bacc
    from concourse.bass_utils import run_bass_kernel_spmd

    nc = bacc.Bacc("TRN2", target_bir_lowering=False, num_devices=1)
    arrays, aps = {}, {}
    for name in INPUTS:
        a = np.ascontiguousarray(inputs[name])
        arrays["in_" + name] = a
        aps[name] = nc.dram_tensor("in_" + name, a.shape, mybir.dt.from_np(a.dtype), kind="ExternalInput").ap()
    arrays["const_table"] = constants()
    aps["const"] = nc.dram_tensor("const_table", (P, CONST_ALL), F32, kind="ExternalInput").ap()
    out = nc.dram_tensor("out", (1, TOK, D), F32, kind="ExternalOutput").ap()
    program(nc, aps, out)
    return run_bass_kernel_spmd(nc, [arrays], core_ids=[0]).results[0]["out"]
```
